# Optimizing a Trainium2 kernel written in Bass

```python
import jax, jax.numpy as jnp
from jax import lax
import numpy as np

D_MODEL = 1024
BATCH = 1
SEQ = 1024
DEPTH = 1
DEC_BATCH = 8
DEC_SEQ = 1
PAST_LEN = 8192
PAGE_SIZE = 128

MIX_WIDTH = D_MODEL
MLSTM_WIDTH = MIX_WIDTH // 2
N_MLSTM_HEADS = 4
MLSTM_HEAD_DIM = MLSTM_WIDTH // N_MLSTM_HEADS
POOL_WIDTH = MIX_WIDTH - MLSTM_WIDTH
POOL_WINDOWS = (2, 4, 8, 16)
N_POOL_GROUPS = len(POOL_WINDOWS)
POOL_GROUP_DIM = POOL_WIDTH // N_POOL_GROUPS
POOL_BUF = max(POOL_WINDOWS) - 1
D_FF = -(-8 * D_MODEL // (3 * 256)) * 256
CHUNK = 128
IN_COLS = 4 * MLSTM_WIDTH + 2 * N_MLSTM_HEADS + POOL_WIDTH
EPS = 1e-6

kernel_name = "hymba_mlstm_multiscale_pool_decoder_step"

def rmsnorm(x, g):
    xf = x.astype(jnp.float32)
    r = xf * lax.rsqrt(jnp.mean(xf * xf, axis=-1, keepdims=True) + EPS)
    return (r * g.astype(jnp.float32)).astype(x.dtype)

def head_rmsnorm(h, g):
    Bx, T, H, dh = h.shape
    h = h * lax.rsqrt(jnp.mean(h * h, axis=-1, keepdims=True) + EPS)
    return h.reshape(Bx, T, H * dh) * g.astype(jnp.float32)

def mlstm_chunkwise(q, k, v, i_pre, f_pre, C0, n0, m0, chunk):
    Bx, T, H, dh = q.shape
    nc = T // chunk

    def to_chunks(a):
        a = a.reshape((Bx, nc, chunk) + a.shape[2:])
        return jnp.moveaxis(jnp.moveaxis(a, 3, 2), 1, 0)

    logf = jax.nn.log_sigmoid(f_pre)
    xs = (to_chunks(q), to_chunks(k), to_chunks(v), to_chunks(i_pre), to_chunks(logf))
    causal = jnp.tril(jnp.ones((chunk, chunk), dtype=bool))

    def step(carry, xs_c):
        C, n, m = carry
        qc, kc, vc, ic, lfc = xs_c
        b = jnp.cumsum(lfc, axis=-1)
        inter = b + m[..., None]
        Dm = b[..., :, None] - b[..., None, :] + ic[..., None, :]
        Dm = jnp.where(causal, Dm, -jnp.inf)
        m_t = jnp.maximum(inter, jnp.max(Dm, axis=-1))
        w = jnp.exp(Dm - m_t[..., None])
        g = jnp.exp(inter - m_t)
        s = jnp.einsum('bhtd,bhsd->bhts', qc, kc) * w
        num = jnp.einsum('bhts,bhsd->bhtd', s, vc) + g[..., None] * jnp.einsum('bhvk,bhtk->bhtv', C, qc)
        den = jnp.sum(s, axis=-1) + g * jnp.einsum('bhk,bhtk->bht', n, qc)
        h = num / jnp.maximum(jnp.abs(den), jnp.exp(-m_t))[..., None]
        m_new = m_t[..., -1]
        g_end = jnp.exp(b[..., -1] + m - m_new)
        w_end = w[..., -1, :]
        C_new = g_end[..., None, None] * C + jnp.einsum('bhs,bhsv,bhsk->bhvk', w_end, vc, kc)
        n_new = g_end[..., None] * n + jnp.einsum('bhs,bhsk->bhk', w_end, kc)
        return (C_new, n_new, m_new), h

    (C1, n1, m1), hs = lax.scan(step, (C0, n0, m0), xs)
    hs = jnp.moveaxis(jnp.moveaxis(hs, 0, 1), 2, 3).reshape(Bx, T, H, dh)
    return hs, C1, n1, m1

def multiscale_pool(u_ext, pos0):
    Bx, Te, Wd = u_ext.shape
    T = Te - POOL_BUF
    csum = jnp.concatenate([jnp.zeros((Bx, 1, Wd), jnp.float32), jnp.cumsum(u_ext, axis=1)], axis=1)
    end = POOL_BUF + 1 + jnp.arange(T)
    pos = pos0 + jnp.arange(T)
    outs = []
    for gi, win in enumerate(POOL_WINDOWS):
        cs = csum[..., gi * POOL_GROUP_DIM:(gi + 1) * POOL_GROUP_DIM]
        cnt = jnp.minimum(win, pos + 1).astype(jnp.float32)
        outs.append((cs[:, end] - cs[:, end - win]) / cnt[None, :, None])
    return jnp.concatenate(outs, axis=-1) - u_ext[:, POOL_BUF:]

def trunk_layer(x, pos0, chunk, C0, n0, m0, buf0, g_mix, w_in, b_gate, g_head, w_pool,
                pool_scale, w_out, g_ffn, w_gate, w_up, w_down):
    Bx, T, _ = x.shape
    W, H, dh = MLSTM_WIDTH, N_MLSTM_HEADS, MLSTM_HEAD_DIM
    hn = rmsnorm(x, g_mix)
    proj = jnp.einsum('btd,dc->btc', hn, w_in).astype(jnp.float32)
    q = proj[..., 0:W].reshape(Bx, T, H, dh)
    k = proj[..., W:2 * W].reshape(Bx, T, H, dh) * (dh ** -0.5)
    v = proj[..., 2 * W:3 * W].reshape(Bx, T, H, dh)
    o = jax.nn.sigmoid(proj[..., 3 * W:4 * W])
    gates = proj[..., 4 * W:4 * W + 2 * H] + b_gate.astype(jnp.float32)
    u = proj[..., 4 * W + 2 * H:]
    h_cell, C1, n1, m1 = mlstm_chunkwise(q, k, v, gates[..., :H], gates[..., H:],
                                         C0.astype(jnp.float32), n0.astype(jnp.float32),
                                         m0.astype(jnp.float32), chunk)
    h_m = head_rmsnorm(h_cell, g_head) * o
    u_ext = jnp.concatenate([buf0.astype(jnp.float32), u], axis=1)
    p = multiscale_pool(u_ext, pos0).reshape(Bx, T, N_POOL_GROUPS, POOL_GROUP_DIM)
    p = jnp.einsum('btgc,gcd->btgd', p, w_pool).reshape(Bx, T, POOL_WIDTH) * pool_scale
    mix = jnp.concatenate([h_m, p], axis=-1).astype(x.dtype)
    x = x + jnp.einsum('btc,cd->btd', mix, w_out).astype(x.dtype)
    h2 = rmsnorm(x, g_ffn)
    a = jnp.einsum('btd,df->btf', h2, w_gate)
    bu = jnp.einsum('btd,df->btf', h2, w_up)
    x = x + jnp.einsum('btf,fd->btd', jax.nn.silu(a) * bu, w_down).astype(x.dtype)
    return x, C1, n1, m1, u_ext[:, -POOL_BUF:]

def setup_inputs(seed: int = 0) -> dict:
    key = jax.random.key(seed)
    ks = jax.random.split(key, 20)
    H, dh = N_MLSTM_HEADS, MLSTM_HEAD_DIM
    nrm = jax.random.normal
    f32 = jnp.float32
    b_i = 0.1 * nrm(ks[6], (DEPTH, H), f32)
    b_f = 3.0 + 0.5 * nrm(ks[7], (DEPTH, H), f32)
    return {
        "x_prompt": nrm(ks[0], (BATCH, SEQ, D_MODEL), f32),
        "x_sample": nrm(ks[1], (DEC_BATCH, DEC_SEQ, D_MODEL), f32),
        "state_mlstm_C": 0.05 * nrm(ks[2], (DEPTH, DEC_BATCH, H, dh, dh), f32),
        "state_mlstm_n": 0.5 * nrm(ks[3], (DEPTH, DEC_BATCH, H, dh), f32),
        "state_mlstm_m": nrm(ks[4], (DEPTH, DEC_BATCH, H), f32),
        "state_pool_buf": nrm(ks[5], (DEPTH, DEC_BATCH, POOL_BUF, POOL_WIDTH), f32),
        "g_mix": 1.0 + 0.05 * nrm(ks[8], (DEPTH, D_MODEL), f32),
        "w_in": nrm(ks[9], (DEPTH, D_MODEL, IN_COLS), f32) * D_MODEL ** -0.5,
        "b_gate": jnp.concatenate([b_i, b_f], axis=-1),
        "g_head": 1.0 + 0.05 * nrm(ks[10], (DEPTH, MLSTM_WIDTH), f32),
        "w_pool": nrm(ks[11], (DEPTH, N_POOL_GROUPS, POOL_GROUP_DIM, POOL_GROUP_DIM), f32) * POOL_GROUP_DIM ** -0.5,
        "pool_scale": 1.0 + 0.1 * nrm(ks[12], (DEPTH, POOL_WIDTH), f32),
        "w_out": nrm(ks[13], (DEPTH, MIX_WIDTH, D_MODEL), f32) * MIX_WIDTH ** -0.5,
        "g_ffn": 1.0 + 0.05 * nrm(ks[14], (DEPTH, D_MODEL), f32),
        "w_gate": nrm(ks[15], (DEPTH, D_MODEL, D_FF), f32) * D_MODEL ** -0.5,
        "w_up": nrm(ks[16], (DEPTH, D_MODEL, D_FF), f32) * D_MODEL ** -0.5,
        "w_down": nrm(ks[17], (DEPTH, D_FF, D_MODEL), f32) * D_FF ** -0.5,
        "g_final": 1.0 + 0.05 * nrm(ks[18], (D_MODEL,), f32),
    }

def reference(x_prompt, x_sample, state_mlstm_C, state_mlstm_n, state_mlstm_m, state_pool_buf,
              g_mix, w_in, b_gate, g_head, w_pool, pool_scale, w_out, g_ffn, w_gate, w_up,
              w_down, g_final):
    H, dh = N_MLSTM_HEADS, MLSTM_HEAD_DIM
    xp = x_prompt
    Cp, npl, mp, bp = [], [], [], []
    chunk_p = min(CHUNK, xp.shape[1])
    for l in range(DEPTH):
        C0 = jnp.zeros((xp.shape[0], H, dh, dh), jnp.float32)
        n0 = jnp.zeros((xp.shape[0], H, dh), jnp.float32)
        m0 = jnp.zeros((xp.shape[0], H), jnp.float32)
        buf0 = jnp.zeros((xp.shape[0], POOL_BUF, POOL_WIDTH), jnp.float32)
        xp, C1, n1, m1, b1 = trunk_layer(xp, 0, chunk_p, C0, n0, m0, buf0, g_mix[l], w_in[l],
                                         b_gate[l], g_head[l], w_pool[l], pool_scale[l], w_out[l],
                                         g_ffn[l], w_gate[l], w_up[l], w_down[l])
        Cp.append(C1); npl.append(n1); mp.append(m1); bp.append(b1)
    y_prompt = rmsnorm(xp, g_final)
    xs = x_sample
    Cs, ns, ms, bs = [], [], [], []
    for l in range(DEPTH):
        xs, C1, n1, m1, b1 = trunk_layer(xs, PAST_LEN, xs.shape[1], state_mlstm_C[l], state_mlstm_n[l],
                                         state_mlstm_m[l], state_pool_buf[l], g_mix[l], w_in[l],
                                         b_gate[l], g_head[l], w_pool[l], pool_scale[l], w_out[l],
                                         g_ffn[l], w_gate[l], w_up[l], w_down[l])
        Cs.append(C1); ns.append(n1); ms.append(m1); bs.append(b1)
    y_sample = rmsnorm(xs, g_final)
    sd = state_mlstm_C.dtype
    C_prompt = jnp.stack(Cp, 0).astype(sd)
    n_prompt = jnp.stack(npl, 0).astype(sd)
    m_prompt = jnp.stack(mp, 0).astype(sd)
    pool_buf_prompt = jnp.stack(bp, 0).astype(state_pool_buf.dtype)
    C_sample = jnp.stack(Cs, 0).astype(sd)
    n_sample = jnp.stack(ns, 0).astype(sd)
    m_sample = jnp.stack(ms, 0).astype(sd)
    pool_buf_sample = jnp.stack(bs, 0).astype(state_pool_buf.dtype)
    return (y_prompt, y_sample, C_prompt, n_prompt, m_prompt, pool_buf_prompt,
            C_sample, n_sample, m_sample, pool_buf_sample)


_drawn_inputs = setup_inputs


def setup_inputs(seed=0):
    import zlib

    import numpy as np

    out = dict(_drawn_inputs(seed))
    spreads = {}
    factors = {'g_head': 3.222}
    for name, (base, spread) in spreads.items():
        noise = np.random.default_rng([zlib.crc32(name.encode()), seed]).standard_normal(out[name].shape)
        drawn = base * np.exp(spread * noise) if base else spread * noise
        out[name] = __import__('jax').numpy.asarray(drawn.astype(out[name].dtype))
    for name, factor in factors.items():
        out[name] = (out[name] * factor).astype(out[name].dtype)
    return out
```

```python
from contextlib import ExitStack

import concourse.bass as bass
from concourse import mybir

F32 = mybir.dt.float32
F32R = mybir.dt.float32r
ACT = mybir.ActivationFunctionType
ALU = mybir.AluOpType
AX = mybir.AxisListType


def trunk_kernel(nc, x_prompt, x_sample, state_C, state_n, state_m, state_buf, g_mix, w_in, b_gate, g_head,
                 w_pool, pool_scale, w_out, g_ffn, w_gate, w_up, w_down, g_final,
                 y_prompt, y_sample, C_prompt, n_prompt, m_prompt, buf_prompt,
                 C_sample, n_sample, m_sample, buf_sample):
    P = 128
    T, D = x_prompt.shape[1:]
    S = x_sample.shape[0]
    N = T + S
    KT = D // P
    H = state_n.shape[2]
    W = H * P
    G = w_pool.shape[1]
    BUF = state_buf.shape[2]
    WINDOWS = (2, 4, 8, 16)
    FT = w_gate.shape[2] // P
    NB = 3
    BW = N // NB
    CH = T // P
    R = S * H
    EPS = 1e-6
    NEG = -1e30
    KSCALE = float(P) ** -0.5
    assert N == NB * BW and BW <= 512 and D == 2 * W and G == H == 4 and FT % 2 == 0

    def blk(c):
        return slice(c * BW, (c + 1) * BW)

    def chk(c):
        return slice(c * P, (c + 1) * P)

    at = [nc.sbuf_base + (-nc.sbuf_base) % 32]

    def fixed(name, shape, dt=F32):
        size = 4
        for n in shape[1:]:
            size *= n
        t = nc.alloc_sbuf_tensor_at(name, shape, dt, offset=at[0])
        at[0] += size + (-size) % 32
        return t

    w_hi = fixed("w_hi", [P, 2, KT, P], F32R)
    w_lo = fixed("w_lo", [P, 2, KT, P], F32R)
    w_raw = fixed("w_raw", [P, 2, KT, P])
    hn_hi = fixed("hn_hi", [P, KT, N], F32R)
    hn_lo = fixed("hn_lo", [P, KT, N], F32R)
    ident = fixed("ident", [P, P])
    ones = fixed("ones", [P, P])
    cap = fixed("cap", [P, P])
    gmix_c = fixed("gmix_c", [P, KT])
    gffn_c = fixed("gffn_c", [P, KT])
    ghead_c = fixed("ghead_c", [P, H])
    pscale_c = fixed("pscale_c", [P, G])
    eps_c = fixed("eps_c", [P, 1])
    sel_f = fixed("sel_f", [P, 2 * H])
    sel = fixed("sel", [P, 2 * H], F32R)
    bgate = fixed("bgate", [P, 1])
    inv_count = fixed("inv_count", [P, 16])
    m0 = fixed("m0", [H, S])
    gate_raw = fixed("gate_raw", [P, KT, 2 * H])
    cols = fixed("cols", [P, 2, CH, H])
    m_before = fixed("m_before", [H, CH])
    sample_exp = fixed("sample_exp", [H, S, 3])
    sample_f = fixed("sample_f", [H, S])
    m_s = fixed("m_s", [H, S])
    scol = fixed("scol", [R, 3])
    u_last = fixed("u_last", [P, G, BUF + S])
    buf_sum = fixed("buf_sum", [P, G, S])
    small8 = fixed("small8", [P, S])
    gend = fixed("gend", [P, 2, H])
    per_head = fixed("per_head", [P, 6, H])
    den = per_head[:, 0, :]
    rden = per_head[:, 1, :]
    ssq_h = per_head[:, 2, :]
    ms_h = per_head[:, 3, :]
    rs_h = per_head[:, 4, :]
    half_c = per_head[:, 5, :]
    s_small = fixed("s_small", [R, 8])
    qkv_s = fixed("qkv_s", [P, 3, R])
    fin_ss = fixed("fin_ss", [P, 2])
    fin_sd = fixed("fin_sd", [P, 2])
    fin_rs = fixed("fin_rs", [P, 2])
    X = at[0]

    def placed(name, shape, off, dt=F32):
        return nc.alloc_sbuf_tensor_at(name, shape, dt, offset=X + off)

    ROW = N * 4
    xT = placed("xT", [P, KT, N], 0)
    x_tok = placed("x_tok", [P, 4, D], 8 * ROW)
    hid = placed("hid", [P, 4, 2, N], 8 * ROW, F32R)
    nt0 = placed("nt0", [P, KT, BW], 12 * ROW)
    ssq = placed("ssq", [P, NB, BW], 12 * ROW + KT * BW * 4)
    guw = placed("guw", [P, 2, 2, 2, KT, P], 16 * ROW, F32R)
    at_nt1 = 16 * ROW + 32768
    nt1 = placed("nt1", [P, KT, BW], at_nt1)
    dw_raw = placed("dw_raw", [P, 2, D], at_nt1)
    std = placed("std", [P, BW], at_nt1 + KT * BW * 4)
    rstd = placed("rstd", [P, BW], at_nt1 + (KT + 1) * BW * 4)
    hf = placed("hf", [P, 4, BW], at_nt1 + (KT + 2) * BW * 4)
    nts = (nt0, nt1)
    C_fin = placed("C_fin", [P, H, P], at_nt1 + (KT + 2) * BW * 4)
    n_fin = placed("n_fin", [H, P], at_nt1 + (KT + 2) * BW * 4 + H * P * 4)
    y_tok = placed("y_tok", [P, 2, D], 12 * ROW)
    gfin = placed("gfin", [P, D], at_nt1)
    gi = placed("gi", [H, N], 8 * ROW)
    gf = placed("gf", [H, N], 9 * ROW)
    ab = placed("ab", [H, N], 10 * ROW)
    keep = placed("keep", [H, T], 16 * ROW)
    b_row = placed("b_row", [H, T], 17 * ROW)
    m_row = placed("m_row", [H, T], 18 * ROW)
    r_row = placed("r_row", [H, T], 19 * ROW)
    g_row = placed("g_row", [H, T], 20 * ROW)
    g_hi = placed("g_hi", [H, T], 21 * ROW, F32R)
    buf_rows = placed("buf_rows", [S * BUF, W], 22 * ROW)
    qkvo = placed("qkvo", [P, 4 * H, N], 0)
    PADT = BUF + N
    u = placed("u", [P, G, PADT], 16 * ROW)
    at_m = 16 * ROW + G * PADT * 4
    at_m += (-at_m) % 32
    step = [at_m]

    def temp(name, shape, dt=F32):
        size = 4
        for n in shape[1:]:
            size *= n
        t = placed(name, shape, step[0], dt)
        step[0] += size + (-size) % 32
        return t

    wt = temp("wt", [P, 2, H, P])
    pt = temp("pt", [P, H, P])
    qg = temp("qg", [P, H, P])
    k_tok = temp("k_tok", [P, 2, H, P])
    v_tok = temp("v_tok", [P, 2, H, P + 1])
    wv = temp("wv", [P, H, P + 1])
    C_st = temp("C_st", [P, H, P + 1])
    h_tok = temp("h_tok", [P, H, P])
    junk = temp("junk", [P, H, P])
    C_s = placed("C_s", [P, R, P], 16 * ROW)
    bc_s = placed("bc_s", [P, R // 2, 2 * P + 1], 16 * ROW + R * P * 4)
    tmp_s = placed("tmp_s", [P, R // 2, P], 16 * ROW + R * P * 4 + (R // 2) * (2 * P + 1) * 4)
    step[0] = max(step[0], 16 * ROW + R * P * 4 + (R // 2) * (3 * P + 1) * 4)
    step[0] += (-step[0]) % 32
    win = placed("win", [P, 2, BW + 16], step[0])
    s_rows = temp("s_rows", [R, 3, P])
    s_pack = temp("s_pack", [R, 2 * P + 1])
    n_s = temp("n_s", [R, P])
    n_new = temp("n_new", [R, P])
    u_rows = temp("u_rows", [BUF + S, W])
    h_s = temp("h_s", [R, P])
    inter = temp("inter", [P, R])
    tmp_rows = temp("tmp_rows", [R, P])
    rr = placed("rr", [P, T], step[0], F32R)
    assert X + step[0] + T * 4 <= nc.sbuf_top and at_nt1 + (KT + 6) * BW * 4 + X <= nc.sbuf_top

    x_spill = nc.dram_tensor("x_spill", [P, KT, N], F32)
    gates_d = nc.dram_tensor("gates_d", [R, 3], F32)
    pack_d = nc.dram_tensor("pack_d", [R, 2 * P + 1], F32)

    with ExitStack() as ctx:
        def sem(name):
            return ctx.enter_context(nc.semaphore(name))

        ps = ctx.enter_context(nc.psum_tensor("ps", [P, 8, 512], F32))
        PA = (ps[:, 0, :], ps[:, 1, :])

        x_loaded = [sem(f"x_loaded{i}") for i in range(4)]
        vecs_loaded = sem("vecs_loaded")
        gate_w_loaded = sem("gate_w_loaded")
        consts = sem("consts")
        x_turned = sem("x_turned")
        xt_act = sem("xt_act")
        xt_dve = sem("xt_dve")
        x_spilled = sem("x_spilled")
        x_back = sem("x_back")
        squared = sem("squared")
        sumsq = sem("sumsq")
        norm_total = sem("norm_total")
        norm_std = sem("norm_std")
        norm_rstd = sem("norm_rstd")
        normed = sem("normed")
        hn_hi_done = sem("hn_hi_done")
        hn_lo_pool = sem("hn_lo_pool")
        hn_lo_dve = sem("hn_lo_dve")
        raw_loaded = [sem(f"raw_loaded{i}") for i in range(2)]
        w_zeroed = sem("w_zeroed")
        w_hi_done = sem("w_hi_done")
        w_ready = sem("w_ready")
        unit_done = sem("unit_done")
        unit_evac = sem("unit_evac")
        row_act = sem("row_act")
        row_dve = sem("row_dve")
        row_pool = sem("row_pool")
        cols_turned = sem("cols_turned")
        cols_done = sem("cols_done")
        buf_loaded = sem("buf_loaded")
        buf_turned = sem("buf_turned")
        buf_summed = sem("buf_summed")
        sg_dve = sem("sg_dve")
        sg_act = sem("sg_act")
        gates_sent = sem("gates_sent")
        scol_loaded = sem("scol_loaded")
        n_loaded = sem("n_loaded")
        s_gathered = sem("s_gathered")
        s_turned = sem("s_turned")
        s_rows_done = sem("s_rows_done")
        s_packed = sem("s_packed")
        pack_sent = sem("pack_sent")
        C_loaded = [sem(f"C_loaded{i}") for i in range(2)]
        bc_loaded = [sem(f"bc_loaded{i}") for i in range(2)]
        s_state = sem("s_state")
        C_stored = sem("C_stored")
        inter_turned = sem("inter_turned")
        s_den = sem("s_den")
        s_head = sem("s_head")
        s_pow = sem("s_pow")
        hs_turned = sem("hs_turned")
        s_mixed = sem("s_mixed")
        o_scaled = sem("o_scaled")
        m_init = sem("m_init")
        rg_done = sem("rg_done")
        scores = sem("scores")
        d_done = sem("d_done")
        w_exp = sem("w_exp")
        gend_done = sem("gend_done")
        qg_done = sem("qg_done")
        p_done = sem("p_done")
        kv_turned = sem("kv_turned")
        kv_tok = sem("kv_tok")
        wv_done = sem("wv_done")
        num_done = sem("num_done")
        den_step = sem("den_step")
        h_done = sem("h_done")
        h_squared = sem("h_squared")
        rs_step = sem("rs_step")
        hs_done = sem("hs_done")
        h_turned = sem("h_turned")
        mixed = sem("mixed")
        kv_done = sem("kv_done")
        c_done = sem("c_done")
        C_turned = sem("C_turned")
        C_out = sem("C_out")
        win_step = sem("win_step")
        win_done = sem("win_done")
        u_saved = sem("u_saved")
        p_step = sem("p_step")
        pooled = sem("pooled")
        p_hi = sem("p_hi")
        p_lo = sem("p_lo")
        pmix_hi = sem("pmix_hi")
        pmix_lo = sem("pmix_lo")
        u_rows_turned = sem("u_rows_turned")
        u_rows_done = sem("u_rows_done")
        hmix_hi = sem("hmix_hi")
        hmix_lo = sem("hmix_lo")
        resid = sem("resid")
        resid_sq = sem("resid_sq")
        resid_sum = sem("resid_sum")
        rows_stored = sem("rows_stored")
        C_fin_stored = sem("C_fin_stored")
        gu_loaded = sem("gu_loaded")
        gu_hi = sem("gu_hi")
        gu_ready = sem("gu_ready")
        gu_done = sem("gu_done")
        sig_done = sem("sig_done")
        act_gate = sem("act_gate")
        hid_f = sem("hid_f")
        hid_hi = sem("hid_hi")
        hid_lo = sem("hid_lo")
        dw_loaded = sem("dw_loaded")
        dw_hi = sem("dw_hi")
        dw_ready = sem("dw_ready")
        down_done = sem("down_done")
        x_acc = sem("x_acc")
        gfin_loaded = sem("gfin_loaded")
        y_turned = sem("y_turned")
        y_ss = sem("y_ss")
        y_std = sem("y_std")
        y_rstd = sem("y_rstd")
        y_done = sem("y_done")
        y_stored = [sem(f"y_stored{i}") for i in range(2)]
        stored = sem("stored")

        J_Q, J_U = 1, 1 + 4 * H
        J_POOL = J_U + G
        J_OUT = J_POOL + 1
        UNITS_U = NB * J_U
        UNITS_POOL = NB * J_POOL
        UNITS_OUT = UNITS_POOL + NB * G
        assert J_U % 2 == 1 and J_OUT % 2 == 0 and UNITS_POOL == 63
        N_TOK = T // P + 1
        TILES_OF = (3, 6, 9)
        NSTORES = [0]

        def rows_of(tt):
            return P if tt < T // P else S

        block = ctx.enter_context(nc.Block())

        @block.sync
        def _(sp):
            win_src = w_in[0].rearrange("(k p) n -> p k n", p=P)
            wout_src = w_out[0].rearrange("(k p) n -> p k n", p=P)

            def load_x(tt):
                if tt >= 4:
                    sp.wait_ge(x_turned, 2 * (tt - 3))
                src = x_prompt[0, chk(tt), :] if tt < T // P else x_sample[:, 0, :]
                sp.dma_start(x_tok[0:rows_of(tt), tt % 4, :], src).then_inc(x_loaded[tt % 4], 16)

            def vec(dst, src):
                sp.dma_start(dst, src).then_inc(vecs_loaded, 16)

            def out(dst, src):
                NSTORES[0] += 1
                sp.dma_start(dst, src).then_inc(stored, 16)

            load_x(0)
            load_x(1)
            load_x(2)
            with nc.allow_non_contiguous_dma(reason="small vectors"):
                vec(gmix_c[:], g_mix[0].rearrange("(k p) -> p k", p=P))
                vec(gffn_c[:], g_ffn[0].rearrange("(k p) -> p k", p=P))
                vec(ghead_c[:], g_head[0].rearrange("(k p) -> p k", p=P))
                vec(pscale_c[:], pool_scale[0].rearrange("(k p) -> p k", p=P))
                vec(bgate[0:H, :], b_gate[0, 0:H].rearrange("(h a) -> h a", a=1))
                vec(bgate[32:32 + H, :], b_gate[0, H:2 * H].rearrange("(h a) -> h a", a=1))
                vec(m0[:], state_m[0].rearrange("b h -> h b"))
            load_x(3)
            sp.dma_start(gate_raw[:], win_src[:, :, 4 * W:4 * W + 2 * H]).then_inc(gate_w_loaded, 16)
            sp.dma_start(w_raw[:, 1], win_src[:, :, 0:P]).then_inc(raw_loaded[1], 16)
            load_x(4)
            load_x(5)
            sp.dma_start(w_raw[:, 0], win_src[:, :, P:2 * P]).then_inc(raw_loaded[0], 16)
            for tt in range(6, N_TOK):
                load_x(tt)
            sp.dma_start(buf_rows[:], state_buf[0].rearrange("b j w -> (b j) w")).then_inc(buf_loaded, 16)
            for c in range(NB):
                sp.wait_ge(xt_act, TILES_OF[c])
                sp.wait_ge(xt_dve, TILES_OF[c])
                sp.dma_start(x_spill[:, :, blk(c)], xT[:, :, blk(c)]).then_inc(x_spilled, 16)

            def load_tiles(first, last):
                with sp.Fori(first, last) as i:
                    sp.wait_ge(w_ready, i * 2 + 2)
                    sp.dma_start(w_raw[:, 1], win_src[:, :, bass.ds(i * (2 * P) + 2 * P, P)])\
                      .then_inc(raw_loaded[1], 16)
                    sp.wait_ge(w_ready, i * 2 + 3)
                    sp.dma_start(w_raw[:, 0], win_src[:, :, bass.ds(i * (2 * P) + 3 * P, P)])\
                      .then_inc(raw_loaded[0], 16)

            load_tiles(0, 4)
            sp.wait_ge(sg_act, 1)
            sp.dma_start(gates_d[:].rearrange("(h b) q -> h (b q)", h=H), sample_exp[:].rearrange("h b q -> h (b q)"))\
              .then_inc(gates_sent, 16)
            sp.wait_ge(gates_sent, 16)
            sp.dma_start(scol[:], gates_d[:]).then_inc(scol_loaded, 16)
            sp.wait_ge(cols_done, 1)
            sp.wait_ge(row_act, 8)
            sp.wait_ge(buf_summed, G)
            for h in range(H):
                sp.dma_start(n_s[h * S:(h + 1) * S, :], state_n[0, :, h, :]).then_inc(n_loaded, 16)
            for part in range(2):
                for h in range(2 * part, 2 * part + 2):
                    sp.dma_start(C_s[:, h * S:(h + 1) * S, :], state_C[0, :, h].rearrange("b v k -> v b k"))\
                      .then_inc(C_loaded[part], 16)
            load_tiles(4, 6)
            sp.wait_ge(s_packed, 4)
            sp.dma_start(pack_d[:], s_pack[:]).then_inc(pack_sent, 16)
            sp.wait_ge(pack_sent, 16)
            sp.dma_start(bc_s[:], pack_d[0:R // 2, :].partition_broadcast(P)).then_inc(bc_loaded[0], 16)
            load_tiles(6, 7)
            sp.wait_ge(s_state, 4)
            sp.dma_start(bc_s[:], pack_d[R // 2:R, :].partition_broadcast(P)).then_inc(bc_loaded[1], 16)

            def load_u(j):
                sp.wait_ge(w_ready, j - 1)
                col = 4 * W + 2 * H + (j - J_U) * P
                sp.dma_start(w_raw[:, j % 2], win_src[:, :, col:col + P]).then_inc(raw_loaded[j % 2], 16)

            load_u(J_U)
            for half_ in range(2):
                sp.wait_ge(s_state, 5 * (half_ + 1))
                for h in range(2 * half_, 2 * half_ + 2):
                    sp.dma_start(C_sample[0, :, h].rearrange("b v k -> v b k"), C_s[:, h * S:(h + 1) * S, :])\
                      .then_inc(C_stored, 16)
            load_u(J_U + 1)
            with nc.allow_non_contiguous_dma(reason="a few words"):
                out(m_sample[0].rearrange("b h -> h b"), m_s[:])
                out(m_prompt[0, 0].rearrange("(h a) -> h a", a=1), m_before[:, 0:1])
            for h in range(H):
                sp.dma_start(n_sample[0, :, h, :], n_new[h * S:(h + 1) * S, :]).then_inc(rows_stored, 16)
            out(buf_sample[0, :, 0:BUF - 1, :], state_buf[0, :, 1:BUF, :])
            load_u(J_U + 2)
            load_u(J_U + 3)
            sp.wait_ge(w_ready, J_POOL - 1)
            sp.dma_start(w_raw[:, 1, 0:G, :], w_pool[0].rearrange("g c d -> c g d")).then_inc(raw_loaded[1], 16)
            sp.wait_ge(w_ready, J_POOL)
            sp.dma_start(w_raw[:, 0], wout_src[:, :, 0:P]).then_inc(raw_loaded[0], 16)
            sp.wait_ge(w_ready, J_POOL + 1)
            sp.dma_start(w_raw[:, 1], wout_src[:, :, P:2 * P]).then_inc(raw_loaded[1], 16)
            sp.wait_ge(scores, CH)
            sp.wait_ge(kv_turned, 2 * CH)
            sp.wait_ge(qg_done, CH)
            for c in range(NB):
                sp.dma_start(xT[:, :, blk(c)], x_spill[:, :, blk(c)]).then_inc(x_back, 16)
            sp.wait_ge(u_rows_done, 1)
            sp.dma_start(buf_prompt[0, 0], u_rows[0:BUF, :]).then_inc(rows_stored, 16)
            sp.dma_start(buf_sample[0, :, BUF - 1, :], u_rows[BUF:BUF + S, :]).then_inc(rows_stored, 16)

            with sp.Fori(0, KT // 2 - 1) as i:
                sp.wait_ge(w_ready, i * 2 + J_OUT + 1)
                sp.dma_start(w_raw[:, 0], wout_src[:, :, bass.ds(i * (2 * P) + 2 * P, P)]).then_inc(raw_loaded[0], 16)
                sp.wait_ge(w_ready, i * 2 + J_OUT + 2)
                sp.dma_start(w_raw[:, 1], wout_src[:, :, bass.ds(i * (2 * P) + 3 * P, P)]).then_inc(raw_loaded[1], 16)
            sp.wait_ge(C_out, 2)
            sp.dma_start(C_prompt[0, 0].rearrange("h v k -> v h k"), C_fin[:]).then_inc(C_fin_stored, 16)
            sp.dma_start(n_prompt[0, 0], n_fin[:]).then_inc(C_fin_stored, 16)

            gate_src = w_gate[0].rearrange("(k p) n -> p k n", p=P)
            up_src = w_up[0].rearrange("(k p) n -> p k n", p=P)
            down_src = w_down[0].rearrange("(i a p) n -> i p a n", p=P, a=2)

            def load_gu(col, ready):
                sp.wait_ge(gu_ready, ready)
                sp.dma_start(w_raw[:, 0], gate_src[:, :, col]).then_inc(gu_loaded, 16)
                sp.dma_start(w_raw[:, 1], up_src[:, :, col]).then_inc(gu_loaded, 16)

            sp.wait_ge(w_ready, J_OUT + KT)
            sp.dma_start(w_raw[:, 0], gate_src[:, :, 0:P]).then_inc(gu_loaded, 16)
            sp.dma_start(w_raw[:, 1], up_src[:, :, 0:P]).then_inc(gu_loaded, 16)
            load_gu(slice(P, 2 * P), 1)
            sp.wait_ge(hn_lo_pool, 4 * 2 * NB)
            sp.wait_ge(hn_lo_dve, 4 * 2 * NB)
            sp.dma_start(dw_raw[:], down_src[0]).then_inc(dw_loaded, 16)
            with sp.Fori(0, FT // 2 - 1) as i:
                load_gu(bass.ds(i * (2 * P) + 2 * P, P), i * 2 + 2)
                load_gu(bass.ds(i * (2 * P) + 3 * P, P), i * 2 + 3)
                sp.wait_ge(dw_ready, i + 1)
                sp.dma_start(dw_raw[:], down_src[bass.ds(i + 1, 1)].rearrange("i p a n -> (i p) a n"))\
                  .then_inc(dw_loaded, 16)

            sp.wait_ge(dw_ready, FT // 2)
            sp.dma_start(gfin[:], g_final.partition_broadcast(P)).then_inc(gfin_loaded, 16)
            for tt in range(N_TOK):
                sp.wait_ge(y_done, tt + 1)
                dst = y_prompt[0, chk(tt), :] if tt < T // P else y_sample[:, 0, :]
                sp.dma_start(dst, y_tok[0:rows_of(tt), tt % 2, :]).then_inc(y_stored[tt % 2], 16)
            sp.wait_ge(y_stored[0], 16 * ((N_TOK + 1) // 2))
            sp.wait_ge(y_stored[1], 16 * (N_TOK // 2))
            sp.wait_ge(C_stored, 16 * H)
            sp.wait_ge(x_spilled, 16 * NB)
            sp.wait_ge(rows_stored, 16 * (H + 2))
            sp.wait_ge(C_fin_stored, 32)
            sp.wait_ge(stored, 16 * NSTORES[0])

        @block.gpsimd
        def _(pool):
            pool.memset(ident[:], 0.0).then_inc(consts, 1)
            pool.memset(ones[:], 1.0).then_inc(consts, 1)
            pool.memset(eps_c[:], EPS).then_inc(consts, 1)
            pool.memset(w_hi[:, 0].bitcast(F32), 0.0).then_inc(w_zeroed, 1)
            pool.memset(w_lo[:, 0].bitcast(F32), 0.0).then_inc(w_zeroed, 1)
            pool.wait_ge(consts, 1)
            pool.affine_select(out=ident[:], in_=ident[:], compare_op=ALU.not_equal, fill=1.0, base=0,
                               pattern=[[-1, P]], channel_multiplier=1).then_inc(consts, 1)
            pool.memset(cap[:], 0.0).then_inc(row_pool, 1)
            pool.memset(sel_f[:], 0.0).then_inc(row_pool, 1)
            pool.memset(half_c[:], -0.5).then_inc(row_pool, 1)
            pool.memset(keep[:], 1.0).then_inc(row_pool, 1)
            pool.memset(m_before[:], 0.0).then_inc(row_pool, 1)
            pool.memset(rr[:].bitcast(F32), 0.0).then_inc(row_pool, 1)
            pool.iota(inv_count[:], pattern=[[1, 16]], base=1, channel_multiplier=0,
                      allow_small_or_imprecise_dtypes=True).then_inc(row_pool, 1)
            pool.wait_ge(row_pool, 4)
            pool.affine_select(out=cap[:], in_=cap[:], compare_op=ALU.is_ge, fill=NEG, base=0,
                               pattern=[[1, P]], channel_multiplier=-1).then_inc(row_pool, 1)
            pool.memset(keep[:].rearrange("h (c t) -> h c t", t=P)[:, :, 0:1], 0.0).then_inc(row_pool, 1)
            for q in range(4):
                part = sel_f[:, H * (q // 2):H * (q // 2) + H]
                pool.wait_ge(row_pool, 9 + q)
                pool.affine_select(out=part, in_=part, compare_op=ALU.not_equal, fill=1.0, base=-32 * q,
                                   pattern=[[-1, H]], channel_multiplier=1).then_inc(row_pool, 1)
            pool.wait_ge(row_pool, 13)
            pool.tensor_copy(sel[:], sel_f[:]).then_inc(row_pool, 1)

            def lo_gates():
                pool.wait_ge(w_hi_done, 1)
                pool.tensor_tensor(w_lo[:, 0, :, 0:H], gate_raw[:, :, 0:H], w_hi[:, 0, :, 0:H].bitcast(F32),
                                   ALU.subtract).then_inc(row_pool, 1)
                pool.wait_ge(row_pool, 15)
                pool.tensor_tensor(w_lo[:, 0, :, 32:32 + H], gate_raw[:, :, H:2 * H],
                                   w_hi[:, 0, :, 32:32 + H].bitcast(F32), ALU.subtract).then_inc(w_ready, 1)

            def lo(slot, need, n=KT):
                pool.wait_ge(w_hi_done, need)
                pool.tensor_tensor(w_lo[:, slot, 0:n], w_raw[:, slot, 0:n], w_hi[:, slot, 0:n].bitcast(F32),
                                   ALU.subtract).then_inc(w_ready, 1)

            def norm_lo(k):
                c = k % NB
                for n in range(0, KT, 2):
                    pool.wait_ge(hn_hi_done, KT * k + n + 1)
                    pool.tensor_tensor(hn_lo[:, n, blk(c)], nts[k % 2][:, n, :], hn_hi[:, n, blk(c)].bitcast(F32),
                                       ALU.subtract).then_inc(hn_lo_pool, 1)

            pool.wait_ge(w_zeroed, 2)
            lo_gates()
            norm_lo(0)
            lo(1, 2)
            norm_lo(1)
            norm_lo(2)
            with pool.Fori(0, 2 * H) as i:
                lo(0, i * 2 + 3)
                lo(1, i * 2 + 4)

            pool.wait_ge(s_state, 10)
            pool.wait_ge(C_stored, 16 * H)
            pool.memset(C_st[:], 0.0).then_inc(m_init, 1)
            pool.memset(v_tok[:, :, :, P:P + 1], 1.0).then_inc(m_init, 1)
            pool.memset(u[:, :, 0:BUF], 0.0).then_inc(m_init, 1)
            pool.wait_ge(s_head, 8)
            pool.tensor_scalar(s_small[:, 5:6], s_small[:, 4:5], 1.0 / P, EPS, ALU.mult, ALU.add).then_inc(s_pow, 1)
            pool.wait_ge(s_pow, 1)
            pool.tensor_tensor(s_small[:, 6:7], s_small[:, 5:6], half_c[0:R, 0:1], ALU.pow).then_inc(s_pow, 1)

            def weigh_v(c):
                pool.wait_ge(kv_tok, 2 * c + 2)
                pool.wait_ge(w_exp, c + 1)
                if c:
                    pool.wait_ge(kv_done, c)
                else:
                    pool.wait_ge(m_init, 3)
                wend = wt[:, c % 2, :, P - 1:P].to_broadcast([P, H, P + 1])
                pool.tensor_tensor(wv[:], v_tok[:, c % 2], wend, ALU.mult).then_inc(wv_done, 1)

            def head_rms(c):
                pool.wait_ge(h_squared, c + 1)
                if c:
                    pool.wait_ge(hs_done, c)
                pool.tensor_scalar(ms_h[:], ssq_h[:], 1.0 / P, EPS, ALU.mult, ALU.add).then_inc(rs_step, 1)
                pool.wait_ge(rs_step, 2 * c + 1)
                pool.tensor_tensor(rs_h[:], ms_h[:], half_c[:], ALU.pow).then_inc(rs_step, 1)

            wsteps = [0]

            def windows(g):
                for n, c in enumerate(reversed(range(NB))):
                    pool.wait_ge(unit_evac, UNITS_U + NB * g + NB)
                    if NB * g + n:
                        pool.wait_ge(pooled, NB * g + n)
                    t0, t1 = c * BW, min((c + 1) * BW, T)
                    src, back = u[:, g, :], BUF
                    for d in range(g + 1):
                        k = 1 << d
                        need = WINDOWS[g] - 2 * k
                        n_col = t1 - t0 + need
                        a = back + (t0 if d == 0 else 0) - (need if d == 0 else 0)
                        if d:
                            a = back - need
                            pool.wait_ge(win_step, wsteps[0])
                        dst = win[:, d % 2, 0:n_col]
                        ins = pool.tensor_tensor(dst, src[:, a:a + n_col], src[:, a - k:a - k + n_col], ALU.add)
                        if d < g:
                            ins.then_inc(win_step, 1)
                            wsteps[0] += 1
                        else:
                            ins.then_inc(win_done, 1)
                        src, back = win[:, d % 2, :], need

            pool.wait_ge(s_head, 9)
            AFTER_SLOT = {1: 0, 2: 1, 4: 2, 5: 3}
            LO_AT = {0: J_U + 1, 1: J_U + 2, 3: J_U + 3, 4: J_POOL}
            for c in range(CH):
                def lo_at():
                    lo(LO_AT[c] % 2, LO_AT[c] + 1, G if LO_AT[c] == J_POOL else KT)

                if c in (0, 3):
                    lo_at()
                weigh_v(c)
                head_rms(c)
                if c in (1, 4):
                    lo_at()
                if c in AFTER_SLOT:
                    windows(AFTER_SLOT[c])
                if c == 5:
                    lo(0, J_OUT + 1)
            lo(1, J_OUT + 2)
            with pool.Fori(0, KT // 2 - 1) as i:
                lo(0, i * 2 + J_OUT + 3)
                lo(1, i * 2 + J_OUT + 4)

            def gu_lo(a, need):
                pool.wait_ge(gu_hi, need)
                pool.tensor_tensor(guw[:, a, :, 1], w_raw[:], guw[:, a, :, 0].bitcast(F32), ALU.subtract)\
                    .then_inc(gu_ready, 1)

            def down_lo(need):
                pool.wait_ge(dw_hi, need)
                pool.tensor_tensor(w_lo[:].rearrange("p a k c -> p a (k c)"), dw_raw[:],
                                   w_hi[:].rearrange("p a k c -> p a (k c)").bitcast(F32), ALU.subtract)\
                    .then_inc(dw_ready, 1)

            gu_lo(0, 1)
            norm_lo(3)
            norm_lo(4)
            norm_lo(5)
            gu_lo(1, 2)
            gu_lo(0, 3)
            gu_lo(1, 4)
            with pool.Fori(1, FT // 2 - 1) as i:
                down_lo(i)
                gu_lo(0, i * 2 + 3)
                gu_lo(1, i * 2 + 4)
            down_lo(FT // 2 - 1)
            down_lo(FT // 2)

        @block.scalar
        def _(act):
            def turn_half(tt):
                r = rows_of(tt)
                act.wait_ge(x_turned, 2 * tt + 1)
                b = 2 + 2 * (tt % 2)
                act.activation(xT[:, 0:4, tt * P:tt * P + r],
                               ps[:, b, :].rearrange("p (k t) -> p k t", t=P)[:, :, 0:r], ACT.Copy).then_inc(xt_act, 1)

            def square(c):
                act.wait_ge(xt_act, TILES_OF[c])
                act.wait_ge(xt_dve, TILES_OF[c])
                if c == 2:
                    act.wait_ge(hn_lo_pool, 4)
                    act.wait_ge(hn_lo_dve, 4)
                act.activation(nts[c % 2][:], xT[:, :, blk(c)], ACT.Square).then_inc(squared, 1)

            def norm_root(k):
                act.wait_ge(norm_total, k + 1)
                if k:
                    act.wait_ge(norm_rstd, k)
                else:
                    act.wait_ge(consts, 4)
                act.activation(std[:], ps[:, 7, 0:BW], ACT.Sqrt, bias=eps_c[:], scale=1.0 / D).then_inc(norm_std, 1)

            def norm_hi(k):
                for n in range(KT):
                    act.wait_ge(normed, KT * k + n + 1)
                    act.activation(hn_hi[:, n, blk(k % NB)], nts[k % 2][:, n, :], ACT.Copy).then_inc(hn_hi_done, 1)

            def hi(slot, loaded, free, n=KT):
                act.wait_ge(raw_loaded[slot], loaded)
                if free is not None:
                    act.wait_ge(unit_done, free)
                act.activation(w_hi[:, slot, 0:n], w_raw[:, slot, 0:n], ACT.Copy).then_inc(w_hi_done, 1)

            turn_half(0)
            turn_half(1)
            turn_half(2)
            square(0)
            turn_half(3)
            act.wait_ge(gate_w_loaded, 16)
            act.wait_ge(w_zeroed, 2)
            act.activation(w_hi[:, 0, :, 0:H], gate_raw[:, :, 0:H], ACT.Copy)
            act.activation(w_hi[:, 0, :, 32:32 + H], gate_raw[:, :, H:2 * H], ACT.Copy).then_inc(w_hi_done, 1)
            turn_half(4)
            norm_root(0)
            norm_hi(0)
            hi(1, 16, None)
            turn_half(5)
            square(1)
            turn_half(6)
            turn_half(7)
            norm_root(1)
            norm_hi(1)
            turn_half(8)
            square(2)
            norm_root(2)
            norm_hi(2)

            act.wait_ge(vecs_loaded, 16 * 7)
            for c in range(NB):
                act.wait_ge(unit_done, c + 1)
                act.activation(gi[:, blk(c)], PA[c % 2][0:H, 0:BW], ACT.Identity, bias=bgate[0:H, :])
                act.activation(gf[:, blk(c)], PA[c % 2][32:32 + H, 0:BW], ACT.Identity, bias=bgate[32:32 + H, :])\
                   .then_inc(unit_evac, 1)
            act.wait_ge(unit_evac, NB)
            act.activation(ab[:], gf[:], ACT.Abs).then_inc(row_act, 1)
            act.wait_ge(row_act, 1)
            act.activation(ab[:], ab[:], ACT.Exp, scale=-1.0).then_inc(row_act, 1)
            act.wait_ge(row_act, 2)
            act.activation(ab[:], ab[:], ACT.Ln, bias=ones[0:H, 0:1]).then_inc(row_act, 1)

            def evac(dst, n_units, func=ACT.Copy, scale=1.0):
                act.wait_ge(unit_done, n_units)
                act.activation(dst, ps[:, n_units_bank[0] % 2, 0:BW], func, scale=scale).then_inc(unit_evac, 1)
                n_units_bank[0] += 1

            n_units_bank = [NB]

            def pair(i, tile, func, scale):
                for d in range(2):
                    slot = d
                    hi(slot, i * 16 + (16 if slot == 0 else 32), i * 6 + (NB * d + NB))
                    for c in range(NB):
                        dst = qkvo[:, bass.ds(tile + d, 1), blk(c)].rearrange("p a t -> p (a t)")
                        evac(dst, i * 6 + NB + NB * d + c + 1, func, scale)

            act.wait_ge(x_spilled, 16 * NB)
            for part, (func, scale) in enumerate(((ACT.Copy, 1.0), (ACT.Copy, KSCALE), (ACT.Copy, 1.0),
                                                  (ACT.Sigmoid, 1.0))):
                with act.Fori(2 * part, 2 * part + 2) as i:
                    pair(i, i * 2, func, scale)
                if part == 0:
                    act.wait_ge(row_pool, 14)
                    act.wait_ge(row_dve, 6)
                    act.activation(rr[0:H, :], r_row[:], ACT.Copy).then_inc(row_act, 1)
                    act.wait_ge(row_dve, 8)
                    act.activation(g_row[:], g_row[:], ACT.Exp).then_inc(row_act, 1)
                    act.activation(ab[:, 0:T], m_row[:], ACT.Exp, scale=-1.0).then_inc(row_act, 1)
                    act.wait_ge(row_act, 5)
                    act.activation(g_hi[:], g_row[:], ACT.Copy).then_inc(row_act, 1)
                    act.wait_ge(row_act, 7)
                    act.activation(rr[64:64 + H, :], g_hi[:].bitcast(F32), ACT.Copy).then_inc(row_act, 1)
                    act.wait_ge(sg_dve, 5)
                    act.activation(sample_exp[:].rearrange("h b q -> h (b q)"),
                                   sample_exp[:].rearrange("h b q -> h (b q)"), ACT.Exp).then_inc(sg_act, 1)

            def unit_u(k):
                j, c = J_U + k // NB, k % NB
                if c == 0:
                    nxt = j + 1
                    nth = nxt // 2 if nxt % 2 == 0 else (nxt + 1) // 2
                    hi(nxt % 2, 16 * nth, NB * (nxt - 1), G if nxt == J_POOL else KT)
                dst = u[:, j - J_U, BUF + c * BW:BUF + (c + 1) * BW]
                evac(dst, UNITS_U + k + 1)

            def exp_w(c):
                act.wait_ge(d_done, c + 1)
                act.activation(wt[:, c % 2], wt[:, c % 2], ACT.Exp).then_inc(w_exp, 1)

            def kv_by_token(c):
                act.wait_ge(kv_turned, 2 * c + 1)
                if c >= 2:
                    act.wait_ge(kv_done, c - 1)
                elif c == 0:
                    act.wait_ge(m_init, 3)
                act.activation(k_tok[:, c % 2], ps[:, 2, :].rearrange("p (h t) -> p h t", h=H), ACT.Copy)\
                   .then_inc(kv_tok, 1)
                act.wait_ge(kv_turned, 2 * c + 2)
                act.activation(v_tok[:, c % 2, :, 0:P], ps[:, 3, :].rearrange("p (h t) -> p h t", h=H), ACT.Copy)\
                   .then_inc(kv_tok, 1)

            def square_h(c):
                act.wait_ge(h_done, c + 1)
                if c:
                    act.wait_ge(rs_step, 2 * c)
                for h in range(H):
                    ins = act.activation(junk[:, h, :], h_tok[:, h, :], ACT.Square, accum_out=ssq_h[:, h:h + 1])
                ins.then_inc(h_squared, 1)

            def p_split_hi(g):
                if g == 0:
                    act.wait_ge(unit_done, UNITS_POOL)
                act.wait_ge(pooled, NB * (g + 1))
                act.activation(hn_hi[:, g, :], u[:, g, BUF:BUF + N], ACT.Copy).then_inc(p_hi, 1)

            def pmix(q):
                g, c = q // NB, q % NB
                act.wait_ge(unit_done, UNITS_POOL + q + 1)
                act.activation(hn_hi[:, H + g, blk(c)], ps[:, (UNITS_POOL + q) % 2, 0:BW], ACT.Copy,
                               scale=pscale_c[:, g:g + 1]).then_inc(pmix_hi, 1)

            exp_w(0)
            for c in range(CH):
                if c < 6:
                    kv_by_token(c)
                    unit_u(2 * c)
                    square_h(c)
                    if c + 1 < CH:
                        exp_w(c + 1)
                    unit_u(2 * c + 1)
                    if c == 5:
                        hi(0, 16 * (J_OUT // 2), UNITS_POOL)
                        p_split_hi(0)
                        p_split_hi(1)
                else:
                    kv_by_token(c)
                    for q in range(3):
                        pmix(6 * (c - 6) + q)
                    square_h(c)
                    if c + 1 < CH:
                        exp_w(c + 1)
                    for q in range(3, 6):
                        pmix(6 * (c - 6) + q)
                    if c == 6:
                        p_split_hi(2)
                        p_split_hi(3)
            hi(1, 16 * ((J_OUT + 2) // 2), UNITS_OUT)

            act.wait_ge(s_mixed, 1)
            for c in range(NB):
                act.wait_ge(mixed, min(CH, TILES_OF[c]))
                act.activation(hn_hi[:, 0:H, blk(c)], qkvo[:, 3 * H:4 * H, blk(c)], ACT.Copy).then_inc(hmix_hi, 1)

            def out_squares(m):
                for c in range(NB):
                    act.wait_ge(resid, m * NB + c + 1)
                    act.wait_ge(resid_sum, m * NB + c + 1)
                    act.activation(nt0[:, c, :], xT[:, bass.ds(m, 1), blk(c)].rearrange("p a t -> p (a t)"),
                                   ACT.Square).then_inc(resid_sq, 1)

            act.wait_ge(hmix_lo, NB)
            with act.Fori(0, KT // 2 - 1) as i:
                out_squares(i * 2)
                hi(0, i * 16 + 16 * (J_OUT // 2 + 1), i * 6 + UNITS_OUT + NB)
                out_squares(i * 2 + 1)
                hi(1, i * 16 + 16 * (J_OUT // 2 + 2), i * 6 + UNITS_OUT + 2 * NB)
            out_squares(KT - 2)
            act.wait_ge(gu_loaded, 32)
            act.activation(guw[:, 0, :, 0], w_raw[:], ACT.Copy).then_inc(gu_hi, 1)
            out_squares(KT - 1)
            act.wait_ge(rows_stored, 16 * (H + 2))
            for k in range(NB, 2 * NB):
                norm_root(k)
                norm_hi(k)

            def gu_split(a, tile, used):
                act.wait_ge(gu_loaded, tile * 32 + 32)
                if used is not None:
                    act.wait_ge(gu_done, used)
                act.activation(guw[:, a, :, 0], w_raw[:], ACT.Copy).then_inc(gu_hi, 1)

            def down_split(i, used):
                act.wait_ge(dw_loaded, i * 16 + 16)
                act.wait_ge(*used)
                act.activation(w_hi[:].rearrange("p a k c -> p a (k c)"), dw_raw[:], ACT.Copy).then_inc(dw_hi, 1)

            def hidden(base, e, half):
                act.wait_ge(gu_done, base + (e + 1))
                if not (isinstance(base, int) and base + e < 4):
                    act.wait_ge(hid_lo, base + (e - 3))
                act.activation(hf[:, hslot(half, e), :], ps[:, e % 2, 0:BW], ACT.Sigmoid).then_inc(sig_done, 1)

            def hslot(half, e):
                return (6 * half + e) % 4

            def hidden_hi(base, e, half):
                act.wait_ge(hid_f, base + (e + 1))
                act.activation(hid[:, 2 * half + e // NB, 0, blk(e % NB)], hf[:, hslot(half, e), :], ACT.Copy)\
                   .then_inc(hid_hi, 1)

            def act_gu(base, it, half, nxt0=True, first=False):
                for e in range(6):
                    hidden(base, e, half)
                    if e == 0 and not first:
                        down_split(it + (-1), (gu_done, 1) if isinstance(it, int) and it == 1
                                   else (down_done, it * 24 + (-24)))
                    if e == NB and nxt0:
                        gu_split(0, it * 2 + 2, it * 6 + NB)
                    if e:
                        hidden_hi(base, e - 1, half)
                hidden_hi(base, 5, half)
                if nxt0:
                    gu_split(1, it * 2 + 3, it * 6 + 6)

            gu_split(1, 1, None)
            act.wait_ge(C_fin_stored, 32)
            act_gu(0, 0, 0, first=True)
            act_gu(6, 1, 1)
            with act.Fori(0, FT // 4 - 1) as i:
                act_gu(i * 12 + 12, i * 2 + 2, 0)
                act_gu(i * 12 + 18, i * 2 + 3, 1)
            last = FT // 2 - 1
            act_gu(6 * last, last, 0, nxt0=False)
            down_split(last, (down_done, 24 * last))

            for tt in range(N_TOK):
                r = rows_of(tt)
                b = 2 * (tt % 2)
                act.wait_ge(y_turned, tt + 1)
                if tt >= 2:
                    act.wait_ge(y_done, tt - 1)
                    act.wait_ge(y_stored[tt % 2], 16 * (tt // 2))
                act.activation(y_tok[0:r, tt % 2, :].rearrange("p (a t) -> p a t", a=2), ps[0:r, b:b + 2, :], ACT.Square,
                               accum_out=fin_ss[0:r, tt % 2:tt % 2 + 1]).then_inc(y_ss, 1)
                act.wait_ge(y_ss, tt + 1)
                act.activation(fin_sd[0:r, tt % 2:tt % 2 + 1], fin_ss[0:r, tt % 2:tt % 2 + 1], ACT.Sqrt,
                               bias=eps_c[0:r, :], scale=1.0 / D).then_inc(y_std, 1)

        FINAL_TURN = {10: 0, 13: 1, 18: 2, 20: 3, 22: 4}
        FINAL_AFTER = {13: 0, 16: 1, 20: 2, 22: 3, 23: 4}

        @block.vector
        def _(dve):
            def turn_half(tt):
                r = rows_of(tt)
                dve.wait_ge(x_turned, 2 * tt + 2)
                b = 3 + 2 * (tt % 2)
                dve.tensor_copy(xT[:, 4:8, tt * P:tt * P + r],
                                ps[:, b, :].rearrange("p (k t) -> p k t", t=P)[:, :, 0:r]).then_inc(xt_dve, 1)

            def block_sum(c):
                dve.wait_ge(squared, c + 1)
                dve.tensor_reduce(ssq[:, c, :], nts[c % 2][:].rearrange("p k t -> p t k"), AX.X, ALU.add)\
                   .then_inc(sumsq, 1)

            def norm(k, g):
                c = k % NB
                dve.wait_ge(norm_std, k + 1)
                if k:
                    dve.wait_ge(normed, KT * k)
                dve.reciprocal(rstd[:], std[:]).then_inc(norm_rstd, 1)
                dve.wait_ge(norm_rstd, k + 1)
                if k >= 2:
                    dve.wait_ge(hn_lo_pool, 4 * (k - 1))
                    dve.wait_ge(hn_lo_dve, 4 * (k - 1))
                for n in range(KT):
                    dve.scalar_tensor_tensor(out=nts[k % 2][:, n, :], in0=xT[:, n, blk(c)], scalar=g[:, n:n + 1],
                                             in1=rstd[:], op0=ALU.mult, op1=ALU.mult).then_inc(normed, 1)
                    if n >= 3 and n % 2:
                        lo_odd(k, n - 2)
                lo_odd(k, KT - 1)

            def lo_odd(k, n):
                dve.wait_ge(hn_hi_done, KT * k + n + 1)
                dve.tensor_tensor(hn_lo[:, n, blk(k % NB)], nts[k % 2][:, n, :], hn_hi[:, n, blk(k % NB)].bitcast(F32),
                                  ALU.subtract).then_inc(hn_lo_dve, 1)

            turn_half(0)
            turn_half(1)
            turn_half(2)
            block_sum(0)
            turn_half(3)
            turn_half(4)
            dve.wait_ge(vecs_loaded, 16 * 7)
            norm(0, gmix_c)
            turn_half(5)
            block_sum(1)
            turn_half(6)
            turn_half(7)
            norm(1, gmix_c)
            turn_half(8)
            block_sum(2)
            norm(2, gmix_c)

            dve.wait_ge(unit_evac, NB)
            dve.wait_ge(row_act, 1)
            dve.tensor_scalar(gf[:], gf[:], 0.0, None, ALU.min).then_inc(row_dve, 1)
            dve.wait_ge(row_act, 3)
            dve.wait_ge(row_dve, 1)
            dve.tensor_tensor(gf[:], gf[:], ab[:], ALU.subtract).then_inc(row_dve, 1)
            dve.wait_ge(row_dve, 2)
            dve.wait_ge(row_pool, 14)
            dve.tensor_tensor_scan(b_row[:], keep[:], gf[:, 0:T], 0.0, ALU.mult, ALU.add).then_inc(row_dve, 1)
            dve.tensor_tensor_scan(m_row[:], gf[:, 0:T], gi[:, 0:T], 0.0, ALU.add, ALU.max).then_inc(row_dve, 1)
            dve.tensor_tensor(sample_f[:], gf[:, T:N], m0[:], ALU.add).then_inc(sg_dve, 1)
            dve.wait_ge(sg_dve, 1)
            dve.tensor_tensor(m_s[:], sample_f[:], gi[:, T:N], ALU.max).then_inc(sg_dve, 1)
            dve.wait_ge(sg_dve, 2)
            dve.tensor_tensor(sample_exp[:, :, 0], gi[:, T:N], m_s[:], ALU.subtract).then_inc(sg_dve, 1)
            dve.tensor_tensor(sample_exp[:, :, 1], sample_f[:], m_s[:], ALU.subtract).then_inc(sg_dve, 1)
            dve.tensor_scalar(sample_exp[:, :, 2], m_s[:], -1.0, None, ALU.mult).then_inc(sg_dve, 1)
            dve.wait_ge(row_dve, 4)
            dve.tensor_tensor(gi[:, 0:T], gi[:, 0:T], b_row[:], ALU.subtract).then_inc(row_dve, 1)
            dve.tensor_tensor(r_row[:], b_row[:], m_row[:], ALU.subtract).then_inc(row_dve, 1)
            dve.tensor_copy(m_before[:, 1:CH], m_row[:, P - 1:T - 1:P]).then_inc(row_dve, 1)
            dve.wait_ge(row_dve, 7)
            dve.tensor_tensor(g_row[:].rearrange("h (c t) -> h c t", t=P), r_row[:].rearrange("h (c t) -> h c t", t=P),
                              m_before[:].rearrange("h (c a) -> h c a", a=1).to_broadcast([H, CH, P]), ALU.add)\
               .then_inc(row_dve, 1)
            dve.wait_ge(row_act, 4)
            dve.tensor_tensor(rr[32:32 + H, :], r_row[:], rr[0:H, :].bitcast(F32), ALU.subtract).then_inc(row_dve, 1)
            dve.wait_ge(row_act, 7)
            dve.tensor_tensor(rr[96:96 + H, :], g_row[:], g_hi[:].bitcast(F32), ALU.subtract).then_inc(row_dve, 1)
            dve.wait_ge(row_dve, 8)
            dve.tensor_copy(m_before[:, 0:1], m_row[:, T - 1:T]).then_inc(row_dve, 1)
            dve.reciprocal(inv_count[:], inv_count[:]).then_inc(row_dve, 1)
            dve.wait_ge(cols_turned, 1)
            dve.tensor_copy(cols[:].rearrange("p a c h -> p (a c h)"), ps[:, 2, 0:2 * CH * H]).then_inc(cols_done, 1)
            dve.wait_ge(buf_turned, 1)
            for g in range(G):
                view = ps[:, 3, g * P:g * P + S * BUF].rearrange("p (b j) -> p b j", j=BUF)
                dve.tensor_reduce(buf_sum[:, g, :], view[:, :, BUF - (WINDOWS[g] - 1):BUF], AX.X, ALU.add)\
                   .then_inc(buf_summed, 1)

            dve.wait_ge(unit_evac, NB * (1 + 3 * H))
            dve.tensor_copy(qkv_s[:].rearrange("p a (h b) -> p (a h) b", h=H), qkvo[:, 0:3 * H, T:N]).then_inc(s_gathered, 1)
            dve.wait_ge(s_turned, 3)
            dve.tensor_copy(s_rows[:].rearrange("r a d -> r (a d)"), ps[0:R, 2, 0:3 * P]).then_inc(s_rows_done, 1)
            dve.wait_ge(s_rows_done, 1)
            dve.wait_ge(scol_loaded, 16)
            dve.tensor_scalar(s_pack[:, 0:P], s_rows[:, 0, :], scol[:, 1:2], None, ALU.mult).then_inc(s_packed, 1)
            dve.tensor_scalar(s_pack[:, P:2 * P], s_rows[:, 1, :], scol[:, 0:1], None, ALU.mult).then_inc(s_packed, 1)
            dve.tensor_copy(s_pack[:, 2 * P:2 * P + 1], scol[:, 1:2]).then_inc(s_packed, 1)
            dve.wait_ge(n_loaded, 16 * H)
            dve.wait_ge(s_packed, 3)
            dve.scalar_tensor_tensor(out=n_new[:], in0=n_s[:], scalar=scol[:, 1:2], in1=s_pack[:, P:2 * P],
                                     op0=ALU.mult, op1=ALU.add).then_inc(s_packed, 1)
            dve.tensor_tensor_reduce(tmp_rows[:], s_rows[:, 0, :], s_pack[:, P:2 * P], 1.0, 0.0, ALU.mult, ALU.add,
                                     s_small[:, 0:1]).then_inc(s_head, 1)
            dve.wait_ge(s_head, 1)
            dve.tensor_tensor_reduce(tmp_rows[:], n_s[:], s_pack[:, 0:P], 1.0, 0.0, ALU.mult, ALU.add,
                                     s_small[:, 1:2]).then_inc(s_head, 1)
            dve.wait_ge(s_head, 2)
            dve.tensor_tensor(s_small[:, 2:3], s_small[:, 0:1], s_small[:, 1:2], ALU.add).then_inc(s_head, 1)
            dve.wait_ge(s_head, 3)
            dve.scalar_tensor_tensor(out=s_small[:, 3:4], in0=s_small[:, 2:3], scalar=-1.0, in1=scol[:, 2:3],
                                     op0=ALU.mult, op1=ALU.max).then_inc(s_den, 1)
            dve.wait_ge(s_den, 1)
            dve.tensor_tensor(s_small[:, 3:4], s_small[:, 2:3], s_small[:, 3:4], ALU.max).then_inc(s_head, 1)
            dve.wait_ge(s_head, 4)
            dve.reciprocal(s_small[:, 7:8], s_small[:, 3:4]).then_inc(s_head, 1)
            for half_ in range(2):
                rs = slice(half_ * (R // 2), (half_ + 1) * (R // 2))
                hs = slice(2 * half_, 2 * half_ + 2)
                dve.wait_ge(C_loaded[half_], 32)
                dve.wait_ge(bc_loaded[half_], 16)
                n0 = 5 * half_
                if half_:
                    dve.wait_ge(s_state, n0)
                dve.tensor_tensor(tmp_s[:], C_s[:, rs, :], bc_s[:, :, 0:P], ALU.mult).then_inc(s_state, 1)
                dve.wait_ge(s_state, n0 + 1)
                dve.tensor_reduce(inter[:, rs], tmp_s[:], AX.X, ALU.add).then_inc(s_state, 1)
                dve.wait_ge(s_state, n0 + 2)
                vcol = qkvo[:, 2 * H + 2 * half_:2 * H + 2 * half_ + 2, T:N].rearrange("p h (b a) -> p h b a", a=1)\
                    .to_broadcast([P, 2, S, P])
                dve.tensor_tensor(tmp_s[:].rearrange("p (h b) k -> p h b k", h=2),
                                  bc_s[:, :, P:2 * P].rearrange("p (h b) k -> p h b k", h=2), vcol, ALU.mult)\
                   .then_inc(s_state, 1)
                dve.tensor_tensor(C_s[:, rs, :], C_s[:, rs, :], bc_s[:, :, 2 * P:2 * P + 1].to_broadcast([P, R // 2, P]),
                                  ALU.mult).then_inc(s_state, 1)
                dve.wait_ge(s_state, n0 + 4)
                dve.tensor_tensor(C_s[:, rs, :], C_s[:, rs, :], tmp_s[:], ALU.add).then_inc(s_state, 1)
            dve.wait_ge(inter_turned, 1)
            dve.wait_ge(s_head, 5)
            dve.scalar_tensor_tensor(out=h_s[:], in0=s_rows[:, 2, :], scalar=s_small[:, 0:1], in1=ps[0:R, 5, 0:P],
                                     op0=ALU.mult, op1=ALU.add).then_inc(s_head, 1)
            dve.wait_ge(s_head, 6)
            dve.tensor_scalar(h_s[:], h_s[:], s_small[:, 7:8], None, ALU.mult).then_inc(s_head, 1)
            dve.wait_ge(s_head, 7)
            dve.tensor_tensor_reduce(tmp_rows[:], h_s[:], h_s[:], 1.0, 0.0, ALU.mult, ALU.add,
                                     s_small[:, 4:5]).then_inc(s_head, 1)
            dve.wait_ge(s_pow, 2)
            dve.tensor_scalar(h_s[:], h_s[:], s_small[:, 6:7], None, ALU.mult).then_inc(s_head, 1)
            for h in range(H):
                dve.wait_ge(unit_evac, NB * (1 + 3 * H + h + 1))
                dve.tensor_scalar(qkvo[:, 3 * H + h, :], qkvo[:, 3 * H + h, :], ghead_c[:, h:h + 1], None, ALU.mult)\
                   .then_inc(o_scaled, 1)

            def exponents(c):
                dve.wait_ge(rg_done, c + 1)
                if c >= 2:
                    dve.wait_ge(p_done, c - 1)
                    dve.wait_ge(wv_done, c - 1)
                for h in range(H):
                    ins = dve.scalar_tensor_tensor(out=wt[:, c % 2, h, :], in0=ps[:, 2, h * P:(h + 1) * P],
                                                   scalar=cols[:, 0, c, h:h + 1], in1=cap[:], op0=ALU.add, op1=ALU.min)
                ins.then_inc(d_done, 1)

            def scaled_q(c):
                gv = ps[:, 3, :].rearrange("p (h t) -> p h t", h=H)
                if c >= 2:
                    dve.wait_ge(c_done, c - 1)
                dve.tensor_copy(gend[:, c % 2, :], gv[:, :, P - 1]).then_inc(gend_done, 1)
                if c:
                    dve.wait_ge(num_done, c)
                dve.tensor_tensor(qg[:], qkvo[:, 0:H, chk(c)], gv, ALU.mult).then_inc(qg_done, 1)

            def weights(c):
                dve.wait_ge(scores, c + 1)
                dve.wait_ge(w_exp, c + 1)
                if c:
                    dve.wait_ge(num_done, c)
                dve.tensor_tensor(pt[:], ps[:, 4, :].rearrange("p (h t) -> p h t", h=H), wt[:, c % 2], ALU.mult)\
                   .then_inc(p_done, 1)

            nv = ps[:, 6:8, 0:2 * (P + 1)].rearrange("p a (h v) -> p a h v", v=P + 1)

            def head(c):
                dve.wait_ge(num_done, c + 1)
                den2 = den[:].rearrange("p (a h) -> p a h", a=2)
                dve.scalar_tensor_tensor(out=den2, in0=nv[:, :, :, P], scalar=-1.0,
                                         in1=cols[:, 1, c, :].rearrange("p (a h) -> p a h", a=2), op0=ALU.mult,
                                         op1=ALU.max).then_inc(den_step, 1)
                dve.wait_ge(den_step, 3 * c + 1)
                dve.tensor_tensor(den2, nv[:, :, :, P], den2, ALU.max).then_inc(den_step, 1)
                dve.wait_ge(den_step, 3 * c + 2)
                if c:
                    dve.wait_ge(h_turned, c)
                dve.reciprocal(rden[:], den[:]).then_inc(den_step, 1)
                dve.wait_ge(den_step, 3 * c + 3)
                dve.tensor_tensor(h_tok[:].rearrange("p (a h) v -> p a h v", a=2), nv[:, :, :, 0:P],
                                  rden[:].rearrange("p (a h b) -> p a h b", a=2, b=1).to_broadcast([P, 2, 2, P]),
                                  ALU.mult).then_inc(h_done, 1)

            def scaled_h(c):
                dve.wait_ge(rs_step, 2 * c + 2)
                dve.tensor_tensor(h_tok[:], h_tok[:], rs_h[:].rearrange("p (h a) -> p h a", a=1).to_broadcast([P, H, P]),
                                  ALU.mult).then_inc(hs_done, 1)

            def mix(c):
                dve.wait_ge(h_turned, c + 1)
                if c == 0:
                    dve.wait_ge(o_scaled, H)
                dve.tensor_tensor(qkvo[:, 3 * H:4 * H, chk(c)], ps[:, 5, :].rearrange("p (h t) -> p h t", h=H),
                                  qkvo[:, 3 * H:4 * H, chk(c)], ALU.mult).then_inc(mixed, 1)

            def state(c):
                dve.wait_ge(kv_done, c + 1)
                dve.wait_ge(gend_done, c + 1)
                if c:
                    dve.wait_ge(c_done, c)
                for h in range(H):
                    ins = dve.scalar_tensor_tensor(out=C_st[:, h, :], in0=C_st[:, h, :], scalar=gend[:, c % 2, h:h + 1],
                                                   in1=nv[:, h // 2, h % 2, :], op0=ALU.mult, op1=ALU.add)
                ins.then_inc(c_done, 1)

            psteps = [0]

            def p_wait():
                if psteps[0]:
                    dve.wait_ge(p_step, psteps[0])

            def p_inc(ins):
                psteps[0] += 1
                ins.then_inc(p_step, 1)

            def pool_group(g):
                k = WINDOWS[g]
                dve.wait_ge(unit_evac, UNITS_U + NB * g + NB)
                dve.tensor_copy(u_last[:, g, :], u[:, g, BUF + T - BUF:BUF + N]).then_inc(u_saved, 1)
                dve.wait_ge(u_saved, g + 1)
                us = u[:, g, BUF + T:BUF + N]
                dve.wait_ge(buf_summed, G)
                p_wait()
                p_inc(dve.tensor_tensor(small8[:], buf_sum[:, g, :], us, ALU.add))
                p_wait()
                p_inc(dve.scalar_tensor_tensor(out=us, in0=small8[:], scalar=1.0 / k, in1=us, op0=ALU.mult,
                                               op1=ALU.subtract))
                for n, c in enumerate(reversed(range(NB))):
                    t0, t1 = c * BW, min((c + 1) * BW, T)
                    dve.wait_ge(win_done, NB * g + n + 1)
                    s = win[:, g % 2, 0:t1 - t0]
                    head_n = k - 1 if c == 0 else 0
                    if head_n:
                        uh = u[:, g, BUF:BUF + head_n]
                        p_inc(dve.tensor_tensor(s[:, 0:head_n], s[:, 0:head_n], inv_count[:, 0:head_n], ALU.mult))
                        p_wait()
                        p_inc(dve.tensor_tensor(uh, s[:, 0:head_n], uh, ALU.subtract))
                    uu = u[:, g, BUF + t0 + head_n:BUF + t1]
                    dve.scalar_tensor_tensor(out=uu, in0=s[:, head_n:], scalar=1.0 / k, in1=uu, op0=ALU.mult,
                                             op1=ALU.subtract).then_inc(pooled, 1)

            def p_split_lo(g):
                dve.wait_ge(p_hi, g + 1)
                p_wait()
                dve.tensor_tensor(hn_lo[:, g, :], u[:, g, BUF:BUF + N], hn_hi[:, g, :].bitcast(F32), ALU.subtract)\
                   .then_inc(p_lo, 1)

            def pmix(q):
                g, c = q // NB, q % NB
                dve.wait_ge(pmix_hi, q + 1)
                dve.scalar_tensor_tensor(out=hn_lo[:, H + g, blk(c)], in0=ps[:, (UNITS_POOL + q) % 2, 0:BW],
                                         scalar=pscale_c[:, g:g + 1], in1=hn_hi[:, H + g, blk(c)].bitcast(F32),
                                         op0=ALU.mult, op1=ALU.subtract).then_inc(pmix_lo, 1)

            dve.wait_ge(m_init, 3)
            exponents(0)
            scaled_q(0)
            weights(0)
            AFTER_SLOT = {1: 0, 2: 1, 4: 2}
            for c in range(CH):
                if c:
                    mix(c - 1)
                if c >= 6:
                    for q in range(3):
                        pmix(6 * (c - 6) + q)
                head(c)
                if c + 1 < CH:
                    exponents(c + 1)
                    scaled_q(c + 1)
                state(c)
                if c + 1 < CH:
                    weights(c + 1)
                scaled_h(c)
                if c in AFTER_SLOT:
                    pool_group(AFTER_SLOT[c])
                if c == 5:
                    p_split_lo(0)
                    p_split_lo(1)
                if c >= 6:
                    for q in range(3, 6):
                        pmix(6 * (c - 6) + q)
                if c == 6:
                    p_split_lo(2)
                    p_split_lo(3)
                if c == 5:
                    pool_group(3)
                if c == CH - 1:
                    dve.wait_ge(u_rows_turned, 1)
                    dve.tensor_copy(u_rows[:], ps[0:BUF + S, 5, :]).then_inc(u_rows_done, 1)
                if c == 3:
                    dve.wait_ge(hs_turned, 1)
                    dve.tensor_tensor(qkvo[:, 3 * H:4 * H, T:N], ps[:, 5, 0:R].rearrange("p (h b) -> p h b", h=H),
                                      qkvo[:, 3 * H:4 * H, T:N], ALU.mult).then_inc(s_mixed, 1)
            mix(CH - 1)

            for c in range(NB):
                dve.wait_ge(hmix_hi, c + 1)
                dve.tensor_tensor(hn_lo[:, 0:H, blk(c)], qkvo[:, 3 * H:4 * H, blk(c)], hn_hi[:, 0:H, blk(c)].bitcast(F32),
                                  ALU.subtract).then_inc(hmix_lo, 1)
            dve.wait_ge(C_turned, 1)
            dve.wait_ge(rows_stored, 16 * (H + 2))
            dve.tensor_copy(C_fin[:].rearrange("p h k -> p (h k)"), ps[:, 2, :]).then_inc(C_out, 1)
            dve.tensor_copy(n_fin[:], ps[0:H, 3, 0:P]).then_inc(C_out, 1)

            dve.wait_ge(hmix_lo, NB)
            for c in range(NB):
                dve.memset(ssq[:, c, :], 0.0).then_inc(resid_sum, 1)
            dve.wait_ge(x_back, 16 * NB)

            def residual(m, start):
                for c in range(NB):
                    dve.wait_ge(unit_done, m * NB + UNITS_OUT + c + 1)
                    xs = xT[:, bass.ds(m, 1), blk(c)].rearrange("p a t -> p (a t)")
                    dve.tensor_tensor(xs, ps[:, (start + c) % 2, 0:BW], xs, ALU.add).then_inc(resid, 1)

            def square_sum(m):
                for c in range(NB):
                    dve.wait_ge(resid_sq, m * NB + c + 1)
                    dve.wait_ge(resid_sum, m * NB + c + 1)
                    dve.tensor_tensor(ssq[:, c, :], ssq[:, c, :], nt0[:, c, :], ALU.add).then_inc(resid_sum, 1)

            with dve.Fori(0, KT // 2) as i:
                residual(i * 2, UNITS_OUT)
                square_sum(i * 2)
                residual(i * 2 + 1, UNITS_OUT + NB)
                square_sum(i * 2 + 1)
            for k in range(NB, 2 * NB):
                norm(k, gffn_c)

            def hidden(base, half):
                for e in range(6):
                    s = hf[:, (6 * half + e) % 4, :]
                    dve.wait_ge(sig_done, base + (e + 1))
                    dve.tensor_tensor(s, ps[:, e % 2, 0:BW], s, ALU.mult).then_inc(act_gate, 1)
                    dve.wait_ge(act_gate, base + (e + 1))
                    dve.tensor_tensor(s, ps[:, 2 + e % 2, 0:BW], s, ALU.mult).then_inc(hid_f, 1)
                    if e:
                        hidden_lo(base, e - 1, half)
                hidden_lo(base, 5, half)

            def hidden_lo(base, e, half):
                dve.wait_ge(hid_hi, base + (e + 1))
                t, c = 2 * half + e // NB, e % NB
                dve.tensor_tensor(hid[:, t, 1, blk(c)], hf[:, (6 * half + e) % 4, :], hid[:, t, 0, blk(c)].bitcast(F32),
                                  ALU.subtract).then_inc(hid_lo, 1)

            def down(base):
                for c in range(NB):
                    for n in range(KT):
                        q = c * KT + n
                        dve.wait_ge(down_done, base + (q + 1))
                        dve.tensor_tensor(xT[:, n, blk(c)], ps[:, 4 + q % 3, 0:BW], xT[:, n, blk(c)], ALU.add)\
                           .then_inc(x_acc, 1)

            hidden(0, 0)
            with dve.Fori(0, FT // 4) as i:
                hidden(i * 12 + 6, 1)
                down(i * 48)
                hidden(i * 12 + 12, 0)
                down(i * 48 + 24)
            last = 24 * (FT // 2 - 1)

            def final(tt):
                r = rows_of(tt)
                b = 2 * (tt % 2)
                dve.wait_ge(y_std, tt + 1)
                dve.reciprocal(fin_rs[0:r, tt % 2:tt % 2 + 1], fin_sd[0:r, tt % 2:tt % 2 + 1]).then_inc(y_rstd, 1)
                dve.wait_ge(y_rstd, tt + 1)
                dve.wait_ge(gfin_loaded, 16)
                dve.scalar_tensor_tensor(out=y_tok[0:r, tt % 2, :].rearrange("p (a t) -> p a t", a=2),
                                         in0=ps[0:r, b:b + 2, :], scalar=fin_rs[0:r, tt % 2:tt % 2 + 1],
                                         in1=gfin[0:r, :].rearrange("p (a t) -> p a t", a=2), op0=ALU.mult, op1=ALU.mult)\
                   .then_inc(y_done, 1)

            for c in range(NB):
                for n in range(KT):
                    q = c * KT + n
                    dve.wait_ge(down_done, last + q + 1)
                    dve.tensor_tensor(xT[:, n, blk(c)], ps[:, 4 + q % 3, 0:BW], xT[:, n, blk(c)], ALU.add)\
                       .then_inc(x_acc, 1)
                    if q in FINAL_AFTER:
                        final(FINAL_AFTER[q])
            for tt in range(len(FINAL_AFTER), N_TOK):
                final(tt)

        @block.tensor
        def _(pe):
            def turn(tt):
                r = rows_of(tt)
                pe.wait_ge(x_loaded[tt % 4], 16 * (tt // 4 + 1))
                for half, freed in ((0, xt_act), (1, xt_dve)):
                    if tt >= 2:
                        pe.wait_ge(freed, tt - 1)
                    for n in range(4):
                        k = 4 * half + n
                        ins = pe.transpose(ps[:, 2 + 2 * (tt % 2) + half, n * P:n * P + r],
                                           x_tok[0:r, tt % 4, k * P:(k + 1) * P], ident[0:r, 0:r])
                    ins.then_inc(x_turned, 1)

            def norm_sum(k):
                if k < NB:
                    pe.wait_ge(sumsq, k + 1)
                else:
                    pe.wait_ge(resid_sum, NB * KT + (k - NB) + 1)
                if k:
                    pe.wait_ge(norm_std, k)
                pe.matmul(ps[:, 7, 0:BW], ones[:], ssq[:, k % NB, :], start=True, stop=True).then_inc(norm_total, 1)

            def product(out, lhs_hi, lhs_lo, rhs_hi, rhs_lo, ks):
                for i, k in enumerate(ks):
                    pe.matmul(out, lhs_hi(k), rhs_hi(k), start=(i == 0), stop=False)
                    pe.matmul(out, lhs_hi(k), rhs_lo(k), start=False, stop=False)
                    ins = pe.matmul(out, lhs_lo(k), rhs_hi(k), start=False, stop=(i == len(ks) - 1))
                return ins

            def unit(slot, bank, c, ks=range(KT)):
                return product(ps[:, bank, 0:BW], lambda k: w_hi[:, slot, k, :], lambda k: w_lo[:, slot, k, :],
                               lambda k: hn_hi[:, k, blk(c)], lambda k: hn_lo[:, k, blk(c)], ks)

            pe.wait_ge(consts, 4)
            for tt in range(5):
                turn(tt)
            norm_sum(0)
            for tt in range(5, 8):
                turn(tt)
            norm_sum(1)
            turn(8)
            norm_sum(2)

            pe.wait_ge(w_ready, 1)
            for c in range(NB):
                pe.wait_ge(hn_lo_pool, 4 * (c + 1))
                pe.wait_ge(hn_lo_dve, 4 * (c + 1))
                if c >= 2:
                    pe.wait_ge(unit_evac, c - 1)
                unit(0, c % 2, c).then_inc(unit_done, 1)

            def pair(i):
                for d in range(2):
                    pe.wait_ge(w_ready, i * 2 + 2 + d)
                    for c in range(NB):
                        n = NB + NB * d + c
                        pe.wait_ge(unit_evac, i * 6 + (n - 1))
                        unit((1 + d) % 2, n % 2, c).then_inc(unit_done, 1)

            with pe.Fori(0, 4) as i:
                pair(i)
            pe.wait_ge(row_dve, 5)
            pe.wait_ge(row_act, 6)
            for n, row in enumerate((gi, ab)):
                for c in range(CH):
                    ins = pe.transpose(ps[:, 2, (n * CH + c) * H:(n * CH + c + 1) * H], row[:, chk(c)], ident[0:H, 0:H])
            ins.then_inc(cols_turned, 1)
            pe.wait_ge(buf_loaded, 16)
            for g in range(G):
                ins = pe.transpose(ps[:, 3, g * P:g * P + S * BUF], buf_rows[:, chk(g)], ident[0:S * BUF, 0:S * BUF])
            ins.then_inc(buf_turned, 1)
            with pe.Fori(4, 6) as i:
                pair(i)
            pe.wait_ge(s_gathered, 1)
            pe.wait_ge(cols_done, 1)
            for n in range(3):
                ins = pe.transpose(ps[0:R, 2, n * P:(n + 1) * P], qkv_s[:, n, :], ident[:])\
                    .then_inc(s_turned, 1)
            with pe.Fori(6, 8) as i:
                pair(i)

            def rows_everywhere(c):
                if c:
                    pe.wait_ge(kv_tok, 2 * c)
                for q, bank in ((0, 2), (1, 3)):
                    for h in range(H):
                        n = H * q + h
                        ins = pe.matmul(ps[:, bank, chk(h)], sel[:, n:n + 1].to_broadcast([P, P]), rr[:, chk(c)],
                                        start=True, stop=True)
                ins.then_inc(rg_done, 1)

            def score(c):
                if c:
                    pe.wait_ge(p_done, c)
                for h in range(H):
                    ins = pe.matmul(ps[:, 4, chk(h)], qkvo[:, H + h, chk(c)], qkvo[:, h, chk(c)], start=True, stop=True)
                ins.then_inc(scores, 1)

            def kv_turn(c):
                for n, bank, freed in ((1, 2, d_done), (2, 3, qg_done)):
                    pe.wait_ge(freed, c + 1)
                    for h in range(H):
                        ins = pe.transpose(ps[:, bank, chk(h)], qkvo[:, n * H + h, chk(c)], ident[:])
                    ins.then_inc(kv_turned, 1)

            nv = ps[:, 6:8, 0:2 * (P + 1)].rearrange("p a (h v) -> p a h v", v=P + 1)

            def numerator(c):
                pe.wait_ge(p_done, c + 1)
                pe.wait_ge(qg_done, c + 1)
                pe.wait_ge(kv_tok, 2 * c + 2)
                if c:
                    pe.wait_ge(c_done, c)
                for h in range(H):
                    pe.matmul(nv[:, h // 2, h % 2, :], pt[:, h, :], v_tok[:, c % 2, h, :], start=True, stop=False)
                    ins = pe.matmul(nv[:, h // 2, h % 2, :], qg[:, h, :], C_st[:, h, :], start=False, stop=True)
                ins.then_inc(num_done, 1)

            def outer(c):
                pe.wait_ge(h_done, c + 1)
                pe.wait_ge(wv_done, c + 1)
                for h in range(H):
                    ins = pe.matmul(nv[:, h // 2, h % 2, :], k_tok[:, c % 2, h, :], wv[:, h, :], start=True, stop=True)
                ins.then_inc(kv_done, 1)

            def h_turn(c):
                pe.wait_ge(hs_done, c + 1)
                if c:
                    pe.wait_ge(mixed, c)
                else:
                    pe.wait_ge(s_head, 6)
                if c == 3:
                    pe.wait_ge(s_mixed, 1)
                if c == CH - 1:
                    pe.wait_ge(u_rows_done, 1)
                for h in range(H):
                    ins = pe.transpose(ps[:, 5, chk(h)], h_tok[:, h, :], ident[:])
                ins.then_inc(h_turned, 1)

            def unit_u(k):
                j, c = J_U + k // NB, k % NB
                pe.wait_ge(w_ready, j + 1)
                pe.wait_ge(unit_evac, UNITS_U + k - 1)
                unit(j % 2, (UNITS_U + k) % 2, c).then_inc(unit_done, 1)

            def unit_pool(q):
                g, c = q // NB, q % NB
                pe.wait_ge(w_ready, J_POOL + 1)
                if q < 2:
                    pe.wait_ge(unit_evac, UNITS_POOL - 1 + q)
                else:
                    pe.wait_ge(pmix_lo, q - 1)
                pe.wait_ge(p_lo, g + 1)
                bank = ps[:, (UNITS_POOL + q) % 2, 0:BW]
                pe.matmul(bank, w_hi[:, 1, g, :], hn_hi[:, g, blk(c)], start=True, stop=False)
                pe.matmul(bank, w_hi[:, 1, g, :], hn_lo[:, g, blk(c)], start=False, stop=False)
                pe.matmul(bank, w_lo[:, 1, g, :], hn_hi[:, g, blk(c)], start=False, stop=True).then_inc(unit_done, 1)

            pe.wait_ge(row_dve, 10)
            pe.wait_ge(row_act, 8)
            pe.wait_ge(s_rows_done, 1)
            pe.wait_ge(buf_summed, G)
            rows_everywhere(0)
            score(0)
            pe.wait_ge(s_state, 10)
            pe.transpose(ps[0:R, 5, 0:P], inter[:], ident[:]).then_inc(inter_turned, 1)
            for c in range(CH):
                kv_turn(c)
                if c < 6:
                    unit_u(2 * c)
                else:
                    for q in range(3):
                        unit_pool(6 * (c - 6) + q)
                numerator(c)
                if c + 1 < CH:
                    rows_everywhere(c + 1)
                    score(c + 1)
                if c < 6:
                    unit_u(2 * c + 1)
                else:
                    unit_pool(6 * (c - 6) + 3)
                    unit_pool(6 * (c - 6) + 4)
                outer(c)
                if c >= 6:
                    unit_pool(6 * (c - 6) + 5)
                if c == 3:
                    pe.wait_ge(mixed, c)
                    pe.wait_ge(s_head, 9)
                    pe.transpose(ps[:, 5, 0:R], h_s[:], ident[0:R, 0:R]).then_inc(hs_turned, 1)
                if c == CH - 1:
                    pe.wait_ge(mixed, c)
                    pe.wait_ge(u_saved, G)
                    for g in range(G):
                        ins = pe.transpose(ps[0:BUF + S, 5, chk(g)], u_last[:, g, :], ident[:])
                    ins.then_inc(u_rows_turned, 1)
                h_turn(c)
            pe.wait_ge(c_done, CH)
            pe.wait_ge(kv_tok, 2 * CH)
            for h in range(H):
                pe.transpose(ps[:, 2, chk(h)], C_st[:, h, 0:P], ident[:])
            pe.transpose(ps[0:H, 3, 0:P], C_st[:, :, P], ident[:]).then_inc(C_turned, 1)

            def out_tile(m, slot, start, first):
                pe.wait_ge(w_ready, m + J_OUT + 1)
                for c in range(NB):
                    if first and c < 2:
                        pe.wait_ge(pmix_lo, NB * G - 1 + c)
                    else:
                        pe.wait_ge(resid, m * NB + (c - 1))
                    if first:
                        pe.wait_ge(hmix_lo, c + 1)
                    unit(slot, (start + c) % 2, c).then_inc(unit_done, 1)

            out_tile(0, 0, UNITS_OUT, True)
            out_tile(1, 1, UNITS_OUT + NB, False)
            with pe.Fori(1, KT // 2) as i:
                out_tile(i * 2, 0, UNITS_OUT, False)
                out_tile(i * 2 + 1, 1, UNITS_OUT + NB, False)
            norm_sum(NB)
            norm_sum(NB + 1)
            norm_sum(NB + 2)

            def gate_up(base, tile, first=False):
                for a in range(2):
                    pe.wait_ge(gu_ready, tile * 2 + (a + 1))
                    for c in range(NB):
                        e = NB * a + c
                        if first and a == 0:
                            pe.wait_ge(hn_lo_pool, 4 * (NB + c + 1))
                            pe.wait_ge(hn_lo_dve, 4 * (NB + c + 1))
                        if not (first and e < 2):
                            pe.wait_ge(hid_f, base + (e - 1))
                        for g in range(2):
                            ins = product(ps[:, 2 * g + e % 2, 0:BW], lambda k: guw[:, a, g, 0, k, :],
                                          lambda k: guw[:, a, g, 1, k, :], lambda k: hn_hi[:, k, blk(c)],
                                          lambda k: hn_lo[:, k, blk(c)], range(KT))
                        ins.then_inc(gu_done, 1)

            dw = [w[:].rearrange("p a k c -> p a (k c)") for w in (w_hi, w_lo)]

            def down(it, base, units, half, first=False, finals=None):
                pe.wait_ge(dw_ready, it + 1)
                for c in range(NB):
                    pe.wait_ge(hid_lo, units + (NB + c + 1))
                    for n in range(KT):
                        q = c * KT + n
                        if not (first and q < 3):
                            pe.wait_ge(x_acc, base + (q - 2))
                        product(ps[:, 4 + q % 3, 0:BW], lambda k: dw[0][:, k, chk(n)], lambda k: dw[1][:, k, chk(n)],
                                lambda k: hid[:, 2 * half + k, 0, blk(c)], lambda k: hid[:, 2 * half + k, 1, blk(c)],
                                range(2)).then_inc(down_done, 1)
                        if finals and q in finals:
                            y_turn(finals[q], base)

            def y_turn(tt, base):
                r = rows_of(tt)
                need = next(c for c in range(NB) if TILES_OF[c] > tt and (tt * P + r) <= (c + 1) * BW)
                pe.wait_ge(x_acc, base + KT * (need + 1))
                if tt >= 2:
                    pe.wait_ge(y_done, tt - 1)
                for k in range(KT):
                    ins = pe.transpose(ps[0:r, 2 * (tt % 2) + k // 4, (k % 4) * P:(k % 4 + 1) * P],
                                       xT[:, k, tt * P:tt * P + r], ident[:])
                ins.then_inc(y_turned, 1)

            gate_up(0, 0, first=True)
            gate_up(6, 1)
            down(0, 0, 0, 0, first=True)
            gate_up(12, 2)
            down(1, 24, 6, 1)
            with pe.Fori(1, FT // 4) as i:
                gate_up(i * 12 + 6, i * 2 + 1)
                down(i * 2, i * 48, i * 12, 0)
                gate_up(i * 12 + 12, i * 2 + 2)
                down(i * 2 + 1, i * 48 + 24, i * 12 + 6, 1)
            last = FT // 2 - 1
            down(last, 24 * last, 6 * last, 0, finals=FINAL_TURN)
            for tt in range(len(FINAL_TURN), N_TOK):
                y_turn(tt, 24 * last)


_INS = ['x_prompt', 'x_sample', 'state_mlstm_C', 'state_mlstm_n', 'state_mlstm_m', 'state_pool_buf', 'g_mix', 'w_in',
        'b_gate', 'g_head', 'w_pool', 'pool_scale', 'w_out', 'g_ffn', 'w_gate', 'w_up', 'w_down', 'g_final']
_OUTS = [(1, 1024, 1024), (8, 1, 1024), (1, 1, 4, 128, 128), (1, 1, 4, 128), (1, 1, 4), (1, 1, 15, 512),
         (1, 8, 4, 128, 128), (1, 8, 4, 128), (1, 8, 4), (1, 8, 15, 512)]


def kernel(**inputs):
    import numpy as _np
    import concourse.bacc as _bacc
    from concourse import mybir as _mybir
    from concourse.bass_utils import run_bass_kernel_spmd as _run

    nc = _bacc.Bacc("TRN2", target_bir_lowering=False, num_devices=1)
    arrays, args = {}, []
    for name in _INS:
        a = _np.ascontiguousarray(inputs[name])
        arrays[f"in_{name}"] = a
        args.append(nc.dram_tensor(f"in_{name}", a.shape, _mybir.dt.from_np(a.dtype), kind="ExternalInput").ap())
    for i, shape in enumerate(_OUTS):
        args.append(nc.dram_tensor(f"out_{i}", shape, _mybir.dt.float32, kind="ExternalOutput").ap())
    trunk_kernel(nc, *args)
    r = _run(nc, [arrays], core_ids=[0])
    return tuple(r.results[0][f"out_{i}"] for i in range(len(_OUTS)))
```

```python
from contextlib import ExitStack

import concourse.bass as bass
from concourse import mybir

F32 = mybir.dt.float32
F32R = mybir.dt.float32r
ACT = mybir.ActivationFunctionType
ALU = mybir.AluOpType
AX = mybir.AxisListType


def trunk_kernel(nc, x_prompt, x_sample, state_C, state_n, state_m, state_buf, g_mix, w_in, b_gate, g_head,
                 w_pool, pool_scale, w_out, g_ffn, w_gate, w_up, w_down, g_final,
                 y_prompt, y_sample, C_prompt, n_prompt, m_prompt, buf_prompt,
                 C_sample, n_sample, m_sample, buf_sample):
    P = 128
    T, D = x_prompt.shape[1:]
    S = x_sample.shape[0]
    N = T + S
    KT = D // P
    H = state_n.shape[2]
    W = H * P
    G = w_pool.shape[1]
    BUF = state_buf.shape[2]
    WINDOWS = (2, 4, 8, 16)
    FT = w_gate.shape[2] // P
    NB = 3
    BW = N // NB
    CH = T // P
    R = S * H
    EPS = 1e-6
    NEG = -1e30
    KSCALE = float(P) ** -0.5
    assert N == NB * BW and BW <= 512 and D == 2 * W and G == H == 4 and FT % 2 == 0

    def blk(c):
        return slice(c * BW, (c + 1) * BW)

    def chk(c):
        return slice(c * P, (c + 1) * P)

    at = [nc.sbuf_base + (-nc.sbuf_base) % 32]

    def fixed(name, shape, dt=F32):
        size = 4
        for n in shape[1:]:
            size *= n
        t = nc.alloc_sbuf_tensor_at(name, shape, dt, offset=at[0])
        at[0] += size + (-size) % 32
        return t

    w_hi = fixed("w_hi", [P, 2, KT, P], F32R)
    w_lo = fixed("w_lo", [P, 2, KT, P], F32R)
    w_raw = fixed("w_raw", [P, 2, KT, P])
    hn_hi = fixed("hn_hi", [P, KT, N], F32R)
    hn_lo = fixed("hn_lo", [P, KT, N], F32R)
    ident = fixed("ident", [P, P])
    ones = fixed("ones", [P, P])
    cap = fixed("cap", [P, P])
    gmix_c = fixed("gmix_c", [P, KT])
    gffn_c = fixed("gffn_c", [P, KT])
    ghead_c = fixed("ghead_c", [P, H])
    pscale_c = fixed("pscale_c", [P, G])
    eps_c = fixed("eps_c", [P, 1])
    sel = fixed("sel", [P, 2 * H], F32R)
    bgate = fixed("bgate", [P, 1])
    inv_count = fixed("inv_count", [P, 16])
    m0 = fixed("m0", [H, S])
    gate_raw = fixed("gate_raw", [P, KT, 2 * H])
    cols = fixed("cols", [P, 2, CH, H])
    m_before = fixed("m_before", [H, CH])
    sample_exp = fixed("sample_exp", [H, S, 3])
    sample_f = fixed("sample_f", [H, S])
    m_s = fixed("m_s", [H, S])
    scol = fixed("scol", [R, 3])
    u_last = fixed("u_last", [P, G, BUF + S])
    buf_sum = fixed("buf_sum", [P, G, S])
    small8 = fixed("small8", [P, S])
    gend = fixed("gend", [P, 2, H])
    per_head = fixed("per_head", [P, 6, H])
    den = per_head[:, 0, :]
    rden = per_head[:, 1, :]
    ssq_h = per_head[:, 2, :]
    ms_h = per_head[:, 3, :]
    rs_h = per_head[:, 4, :]
    half_c = per_head[:, 5, :]
    s_small = fixed("s_small", [R, 8])
    qkv_s = fixed("qkv_s", [P, 3, R])
    N_TOK = T // P + 1
    by_tok = fixed("by_tok", [P, 3, N_TOK])
    X = at[0]

    def placed(name, shape, off, dt=F32):
        return nc.alloc_sbuf_tensor_at(name, shape, dt, offset=X + off)

    ROW = N * 4
    xT = placed("xT", [P, KT, N], 0)
    x_tok = placed("x_tok", [P, 4, D], 8 * ROW)
    nt0 = placed("nt0", [P, KT, BW], 14 * ROW)
    hid = placed("hid", [P, 4, 2, N], 8 * ROW, F32R)
    out_sq = placed("out_sq", [P, NB, BW], 12 * ROW)
    ssq = placed("ssq", [P, NB, BW], 12 * ROW + KT * BW * 4)
    guw = placed("guw", [P, 2, 2, 2, KT, P], 16 * ROW, F32R)
    at_nt1 = 16 * ROW + 32768
    nt1 = placed("nt1", [P, KT, BW], at_nt1)
    dw_raw = placed("dw_raw", [P, 2, D], at_nt1)
    rstd_x = placed("rstd_x", [P, N], at_nt1 + KT * BW * 4)
    sq_junk = placed("sq_junk", [P, D], at_nt1 + KT * BW * 4 + N * 4)
    rstd = placed("rstd", [P, NB, BW], at_nt1 + 2 * D * 4)
    std = placed("std", [P, BW], at_nt1 + 2 * D * 4 + NB * BW * 4)
    hf = placed("hf", [P, 4, BW], at_nt1 + (KT + 2) * BW * 4)
    nts = (nt0, nt1)
    C_fin = placed("C_fin", [P, H, P], at_nt1 + (KT + 2) * BW * 4)
    n_fin = placed("n_fin", [H, P], at_nt1 + (KT + 2) * BW * 4 + H * P * 4)
    y_tok = placed("y_tok", [P, 2, D], 12 * ROW)
    gfin = placed("gfin", [P, D], at_nt1)
    gi = placed("gi", [H, N], 12 * ROW)
    gf = placed("gf", [H, N], 13 * ROW)
    ab = placed("ab", [H, N], 8 * ROW)
    sel_f = placed("sel_f", [P, 2 * H], 12 * ROW - 64)
    keep = placed("keep", [H, T], 17 * ROW)
    b_row = placed("b_row", [H, T], 18 * ROW)
    m_row = placed("m_row", [H, T], 19 * ROW)
    r_row = placed("r_row", [H, T], 20 * ROW)
    g_row = placed("g_row", [H, T], 21 * ROW)
    g_hi = placed("g_hi", [H, T], 22 * ROW, F32R)
    buf_rows = placed("buf_rows", [S * BUF, W], 23 * ROW)
    qkvo = placed("qkvo", [P, 4 * H, N], 0)
    PADT = BUF + N
    u = placed("u", [P, G, PADT], 16 * ROW)
    at_m = 16 * ROW + G * PADT * 4
    at_m += (-at_m) % 32
    step = [at_m]

    def temp(name, shape, dt=F32):
        size = 4
        for n in shape[1:]:
            size *= n
        t = placed(name, shape, step[0], dt)
        step[0] += size + (-size) % 32
        return t

    wt = temp("wt", [P, 2, H, P])
    pt = temp("pt", [P, H, P])
    qg = temp("qg", [P, H, P])
    k_tok = temp("k_tok", [P, 2, H, P])
    v_tok = temp("v_tok", [P, 2, H, P + 1])
    wv = temp("wv", [P, H, P + 1])
    C_st = temp("C_st", [P, H, P + 1])
    h_tok = temp("h_tok", [P, H, P])
    junk = temp("junk", [P, H, P])
    C_s = placed("C_s", [P, R, P], 16 * ROW)
    bc_s = placed("bc_s", [P, R // 2, 2 * P + 1], 16 * ROW + R * P * 4)
    tmp_s = placed("tmp_s", [P, R // 2, P], 16 * ROW + R * P * 4 + (R // 2) * (2 * P + 1) * 4)
    step[0] = max(step[0], 16 * ROW + R * P * 4 + (R // 2) * (3 * P + 1) * 4)
    step[0] += (-step[0]) % 32
    win = placed("win", [P, 2, BW + 16], step[0])
    s_rows = temp("s_rows", [R, 3, P])
    s_pack = temp("s_pack", [R, 2 * P + 1])
    n_s = temp("n_s", [R, P])
    n_new = temp("n_new", [R, P])
    u_rows = temp("u_rows", [BUF + S, W])
    h_s = temp("h_s", [R, P])
    inter = temp("inter", [P, R])
    tmp_rows = temp("tmp_rows", [R, P])
    rr = placed("rr", [P, T], step[0], F32R)
    assert X + step[0] + T * 4 <= nc.sbuf_top and at_nt1 + (KT + 6) * BW * 4 + X <= nc.sbuf_top
    assert KT * BW * 4 + N * 4 + D * 4 <= (KT + 6) * BW * 4

    x_spill = nc.dram_tensor("x_spill", [P, KT, N], F32)
    gates_d = nc.dram_tensor("gates_d", [R, 3], F32)
    pack_d = nc.dram_tensor("pack_d", [R, 2 * P + 1], F32)

    with ExitStack() as ctx:
        def sem(name):
            return ctx.enter_context(nc.semaphore(name))

        ps = ctx.enter_context(nc.psum_tensor("ps", [P, 8, 512], F32))
        PA = (ps[:, 0, :], ps[:, 1, :])

        x_loaded = [sem(f"x_loaded{i}") for i in range(4)]
        vecs_loaded = sem("vecs_loaded")
        gate_w_loaded = sem("gate_w_loaded")
        consts = sem("consts")
        x_turned = sem("x_turned")
        xt_act = sem("xt_act")
        xt_dve = sem("xt_dve")
        x_spilled = [sem(f"x_spilled{i}") for i in range(NB)]
        x_back = sem("x_back")
        x_squared = sem("x_squared")
        x_std = sem("x_std")
        x_rstd = sem("x_rstd")
        rstd_spread = sem("rstd_spread")
        rstd_copied = sem("rstd_copied")
        norm_total = sem("norm_total")
        norm_std = sem("norm_std")
        norm_rstd = sem("norm_rstd")
        normed = sem("normed")
        hn_hi_done = sem("hn_hi_done")
        hn_lo_pool = sem("hn_lo_pool")
        hn_lo_dve = sem("hn_lo_dve")
        raw_loaded = [sem(f"raw_loaded{i}") for i in range(2)]
        w_zeroed = sem("w_zeroed")
        w_hi_done = sem("w_hi_done")
        w_ready = sem("w_ready")
        unit_done = sem("unit_done")
        unit_evac = sem("unit_evac")
        row_act = sem("row_act")
        row_dve = sem("row_dve")
        row_pool = sem("row_pool")
        cols_turned = sem("cols_turned")
        cols_done = sem("cols_done")
        buf_loaded = sem("buf_loaded")
        buf_turned = sem("buf_turned")
        buf_summed = sem("buf_summed")
        sg_dve = sem("sg_dve")
        sg_act = sem("sg_act")
        gates_sent = sem("gates_sent")
        scol_loaded = sem("scol_loaded")
        n_loaded = sem("n_loaded")
        s_gathered = sem("s_gathered")
        s_turned = sem("s_turned")
        s_rows_done = sem("s_rows_done")
        s_packed = sem("s_packed")
        pack_sent = sem("pack_sent")
        C_loaded = [sem(f"C_loaded{i}") for i in range(2)]
        bc_loaded = [sem(f"bc_loaded{i}") for i in range(2)]
        s_state = sem("s_state")
        s_scaled = sem("s_scaled")
        C_stored = sem("C_stored")
        inter_turned = sem("inter_turned")
        s_den = sem("s_den")
        s_head = sem("s_head")
        s_pow = sem("s_pow")
        hs_turned = sem("hs_turned")
        s_mixed = sem("s_mixed")
        o_scaled = sem("o_scaled")
        m_init = sem("m_init")
        rg_done = sem("rg_done")
        scores = sem("scores")
        d_done = sem("d_done")
        w_exp = sem("w_exp")
        gend_done = sem("gend_done")
        qg_done = sem("qg_done")
        p_done = sem("p_done")
        kv_turned = sem("kv_turned")
        kv_tok = sem("kv_tok")
        wv_done = sem("wv_done")
        num_done = sem("num_done")
        den_step = sem("den_step")
        h_done = sem("h_done")
        h_squared = sem("h_squared")
        rs_step = sem("rs_step")
        hs_done = sem("hs_done")
        h_turned = sem("h_turned")
        mixed = sem("mixed")
        kv_done = sem("kv_done")
        c_done = sem("c_done")
        C_turned = sem("C_turned")
        C_out = sem("C_out")
        win_step = sem("win_step")
        win_done = sem("win_done")
        u_saved = sem("u_saved")
        p_step = sem("p_step")
        pooled = sem("pooled")
        p_hi = sem("p_hi")
        p_lo = sem("p_lo")
        pmix_hi = sem("pmix_hi")
        pmix_lo = sem("pmix_lo")
        u_rows_turned = sem("u_rows_turned")
        u_rows_done = sem("u_rows_done")
        hmix_hi = sem("hmix_hi")
        hmix_lo = sem("hmix_lo")
        resid = sem("resid")
        resid_sq = sem("resid_sq")
        resid_sum = sem("resid_sum")
        rows_stored = sem("rows_stored")
        C_fin_stored = sem("C_fin_stored")
        gu_loaded = sem("gu_loaded")
        gu_hi = sem("gu_hi")
        gu_ready = sem("gu_ready")
        gu_done = sem("gu_done")
        sig_done = sem("sig_done")
        gate_scaled = sem("gate_scaled")
        act_gate = sem("act_gate")
        act_up = sem("act_up")
        hid_f = sem("hid_f")
        hid_hi = sem("hid_hi")
        hid_lo = sem("hid_lo")
        dw_loaded = sem("dw_loaded")
        dw_hi = sem("dw_hi")
        dw_ready = sem("dw_ready")
        down_done = sem("down_done")
        x_acc = sem("x_acc")
        gfin_loaded = sem("gfin_loaded")
        y_turned = sem("y_turned")
        y_ss = sem("y_ss")
        y_std = sem("y_std")
        y_rstd = sem("y_rstd")
        y_done = sem("y_done")
        y_stored = [sem(f"y_stored{i}") for i in range(2)]
        stored = sem("stored")

        J_Q, J_U = 1, 1 + 4 * H
        J_POOL = J_U + G
        J_OUT = J_POOL + 1
        UNITS_U = NB * J_U
        UNITS_POOL = NB * J_POOL
        UNITS_OUT = UNITS_POOL + NB * G
        assert J_U % 2 == 1 and J_OUT % 2 == 0 and UNITS_POOL == 63
        GROUP_OF = tuple(reversed(range(G)))
        POOL_AT = {(1, 0): [(0, 2)], (1, 1): [(0, 1)], (2, 0): [(0, 0)],
                   (3, 0): [(1, 2)], (3, 1): [(1, 1)], (4, 0): [(1, 0)],
                   (4, 1): [(2, 2)], (5, 0): [(2, 1), (2, 0), (3, 2), (3, 1), (3, 0)]}
        TILES_OF = (3, 6, 9)
        NSTORES = [0]

        def rows_of(tt):
            return P if tt < T // P else S

        block = ctx.enter_context(nc.Block())

        dw_last = guw[:, 0].rearrange("p g s k c -> p (g s k c)").rearrange("p (s a n) -> p s a n", s=2, a=2)

        def gate_bank(e):
            return (e + 1) % 2

        @block.sync
        def _(sp):
            win_src = w_in[0].rearrange("(k p) n -> p k n", p=P)
            wout_src = w_out[0].rearrange("(k p) n -> p k n", p=P)

            def load_x(tt):
                if tt >= 4:
                    sp.wait_ge(x_turned, 2 * (tt - 3))
                    sp.wait_ge(x_squared, tt - 3)
                src = x_prompt[0, chk(tt), :] if tt < T // P else x_sample[:, 0, :]
                sp.dma_start(x_tok[0:rows_of(tt), tt % 4, :], src).then_inc(x_loaded[tt % 4], 16)

            def vec(dst, src):
                sp.dma_start(dst, src).then_inc(vecs_loaded, 16)

            def out(dst, src):
                NSTORES[0] += 1
                sp.dma_start(dst, src).then_inc(stored, 16)

            load_x(0)
            load_x(1)
            load_x(2)
            with nc.allow_non_contiguous_dma(reason="small vectors"):
                vec(gmix_c[:], g_mix[0].rearrange("(k p) -> p k", p=P))
                vec(gffn_c[:], g_ffn[0].rearrange("(k p) -> p k", p=P))
                vec(ghead_c[:], g_head[0].rearrange("(k p) -> p k", p=P))
                vec(pscale_c[:], pool_scale[0].rearrange("(k p) -> p k", p=P))
                vec(bgate[0:H, :], b_gate[0, 0:H].rearrange("(h a) -> h a", a=1))
                vec(bgate[32:32 + H, :], b_gate[0, H:2 * H].rearrange("(h a) -> h a", a=1))
                vec(m0[:], state_m[0].rearrange("b h -> h b"))
            load_x(3)
            sp.dma_start(gate_raw[:], win_src[:, :, 4 * W:4 * W + 2 * H]).then_inc(gate_w_loaded, 16)
            sp.dma_start(w_raw[:, 1], win_src[:, :, 0:P]).then_inc(raw_loaded[1], 16)
            load_x(4)
            load_x(5)
            sp.dma_start(w_raw[:, 0], win_src[:, :, P:2 * P]).then_inc(raw_loaded[0], 16)
            for tt in range(6, N_TOK):
                load_x(tt)
            sp.dma_start(buf_rows[:], state_buf[0].rearrange("b j w -> (b j) w")).then_inc(buf_loaded, 16)
            for c in range(NB):
                sp.wait_ge(xt_act, TILES_OF[c])
                sp.wait_ge(xt_dve, TILES_OF[c])
                sp.dma_start(x_spill[:, :, blk(c)], xT[:, :, blk(c)]).then_inc(x_spilled[c], 16)

            def load_tiles(first, last):
                with sp.Fori(first, last) as i:
                    sp.wait_ge(w_ready, i * 2 + 2)
                    sp.dma_start(w_raw[:, 1], win_src[:, :, bass.ds(i * (2 * P) + 2 * P, P)])\
                      .then_inc(raw_loaded[1], 16)
                    sp.wait_ge(w_ready, i * 2 + 3)
                    sp.dma_start(w_raw[:, 0], win_src[:, :, bass.ds(i * (2 * P) + 3 * P, P)])\
                      .then_inc(raw_loaded[0], 16)

            load_tiles(0, 4)
            sp.wait_ge(sg_act, 1)
            sp.dma_start(gates_d[:].rearrange("(h b) q -> h (b q)", h=H), sample_exp[:].rearrange("h b q -> h (b q)"))\
              .then_inc(gates_sent, 16)
            sp.wait_ge(gates_sent, 16)
            sp.dma_start(scol[:], gates_d[:]).then_inc(scol_loaded, 16)
            sp.wait_ge(cols_done, 1)
            sp.wait_ge(row_act, 8)
            sp.wait_ge(buf_summed, G)
            for h in range(H):
                sp.dma_start(n_s[h * S:(h + 1) * S, :], state_n[0, :, h, :]).then_inc(n_loaded, 16)
            for part in range(2):
                for h in range(2 * part, 2 * part + 2):
                    sp.dma_start(C_s[:, h * S:(h + 1) * S, :], state_C[0, :, h].rearrange("b v k -> v b k"))\
                      .then_inc(C_loaded[part], 16)
            load_tiles(4, 6)
            sp.wait_ge(s_packed, 4)
            sp.dma_start(pack_d[:], s_pack[:]).then_inc(pack_sent, 16)
            sp.wait_ge(pack_sent, 16)
            sp.dma_start(bc_s[:], pack_d[0:R // 2, :].partition_broadcast(P)).then_inc(bc_loaded[0], 16)
            load_tiles(6, 7)
            sp.wait_ge(s_state, 3)
            sp.wait_ge(s_scaled, 1)
            sp.dma_start(bc_s[:], pack_d[R // 2:R, :].partition_broadcast(P)).then_inc(bc_loaded[1], 16)

            def load_u(j):
                sp.wait_ge(w_ready, j - 1)
                col = 4 * W + 2 * H + GROUP_OF[j - J_U] * P
                sp.dma_start(w_raw[:, j % 2], win_src[:, :, col:col + P]).then_inc(raw_loaded[j % 2], 16)

            load_u(J_U)
            for half_ in range(2):
                sp.wait_ge(s_state, 4 * (half_ + 1))
                for h in range(2 * half_, 2 * half_ + 2):
                    sp.dma_start(C_sample[0, :, h].rearrange("b v k -> v b k"), C_s[:, h * S:(h + 1) * S, :])\
                      .then_inc(C_stored, 16)
            load_u(J_U + 1)
            with nc.allow_non_contiguous_dma(reason="a few words"):
                out(m_sample[0].rearrange("b h -> h b"), m_s[:])
                out(m_prompt[0, 0].rearrange("(h a) -> h a", a=1), m_before[:, 0:1])
            for h in range(H):
                sp.dma_start(n_sample[0, :, h, :], n_new[h * S:(h + 1) * S, :]).then_inc(rows_stored, 16)
            out(buf_sample[0, :, 0:BUF - 1, :], state_buf[0, :, 1:BUF, :])
            load_u(J_U + 2)
            load_u(J_U + 3)
            sp.wait_ge(w_ready, J_POOL - 1)
            sp.dma_start(w_raw[:, 1, 0:G, :], w_pool[0].rearrange("g c d -> c g d")).then_inc(raw_loaded[1], 16)
            sp.wait_ge(w_ready, J_POOL)
            sp.dma_start(w_raw[:, 0], wout_src[:, :, 0:P]).then_inc(raw_loaded[0], 16)
            sp.wait_ge(w_ready, J_POOL + 1)
            sp.dma_start(w_raw[:, 1], wout_src[:, :, P:2 * P]).then_inc(raw_loaded[1], 16)
            sp.wait_ge(scores, CH)
            sp.wait_ge(kv_turned, 2 * CH)
            sp.wait_ge(qg_done, CH)
            for c in range(NB):
                sp.dma_start(xT[:, :, blk(c)], x_spill[:, :, blk(c)]).then_inc(x_back, 16)
            sp.wait_ge(u_rows_done, 1)
            sp.dma_start(buf_prompt[0, 0], u_rows[0:BUF, :]).then_inc(rows_stored, 16)
            sp.dma_start(buf_sample[0, :, BUF - 1, :], u_rows[BUF:BUF + S, :]).then_inc(rows_stored, 16)

            with sp.Fori(0, KT // 2 - 1) as i:
                sp.wait_ge(w_ready, i * 2 + J_OUT + 1)
                sp.dma_start(w_raw[:, 0], wout_src[:, :, bass.ds(i * (2 * P) + 2 * P, P)]).then_inc(raw_loaded[0], 16)
                sp.wait_ge(w_ready, i * 2 + J_OUT + 2)
                sp.dma_start(w_raw[:, 1], wout_src[:, :, bass.ds(i * (2 * P) + 3 * P, P)]).then_inc(raw_loaded[1], 16)
            sp.wait_ge(C_out, 2)
            sp.dma_start(C_prompt[0, 0].rearrange("h v k -> v h k"), C_fin[:]).then_inc(C_fin_stored, 16)
            sp.dma_start(n_prompt[0, 0], n_fin[:]).then_inc(C_fin_stored, 16)

            gate_src = w_gate[0].rearrange("(k p) n -> p k n", p=P)
            up_src = w_up[0].rearrange("(k p) n -> p k n", p=P)
            down_src = w_down[0].rearrange("(i a p) n -> i p a n", p=P, a=2)

            def load_gu(col, ready):
                sp.wait_ge(gu_ready, ready)
                sp.dma_start(w_raw[:, 0], gate_src[:, :, col]).then_inc(gu_loaded, 16)
                sp.dma_start(w_raw[:, 1], up_src[:, :, col]).then_inc(gu_loaded, 16)

            sp.wait_ge(w_ready, J_OUT + KT)
            sp.dma_start(w_raw[:, 0], gate_src[:, :, 0:P]).then_inc(gu_loaded, 16)
            sp.dma_start(w_raw[:, 1], up_src[:, :, 0:P]).then_inc(gu_loaded, 16)
            load_gu(slice(P, 2 * P), 1)
            sp.dma_start(dw_raw[:], down_src[0]).then_inc(dw_loaded, 16)
            with sp.Fori(0, FT // 2 - 1) as i:
                load_gu(bass.ds(i * (2 * P) + 2 * P, P), i * 2 + 2)
                load_gu(bass.ds(i * (2 * P) + 3 * P, P), i * 2 + 3)
                sp.wait_ge(dw_ready, i + 1)
                sp.dma_start(dw_raw[:], down_src[bass.ds(i + 1, 1)].rearrange("i p a n -> (i p) a n"))\
                  .then_inc(dw_loaded, 16)

            sp.wait_ge(dw_ready, FT // 2)
            sp.dma_start(gfin[:], g_final.partition_broadcast(P)).then_inc(gfin_loaded, 16)
            for tt in range(N_TOK):
                sp.wait_ge(y_done, tt + 1)
                dst = y_prompt[0, chk(tt), :] if tt < T // P else y_sample[:, 0, :]
                sp.dma_start(dst, y_tok[0:rows_of(tt), tt % 2, :]).then_inc(y_stored[tt % 2], 16)
            sp.wait_ge(y_stored[0], 16 * ((N_TOK + 1) // 2))
            sp.wait_ge(y_stored[1], 16 * (N_TOK // 2))
            sp.wait_ge(C_stored, 16 * H)
            for c in range(NB):
                sp.wait_ge(x_spilled[c], 16)
            sp.wait_ge(rows_stored, 16 * (H + 2))
            sp.wait_ge(C_fin_stored, 32)
            sp.wait_ge(stored, 16 * NSTORES[0])

        @block.gpsimd
        def _(pool):
            pool.memset(ident[:], 0.0).then_inc(consts, 1)
            pool.memset(ones[:], 1.0).then_inc(consts, 1)
            pool.memset(eps_c[:], EPS).then_inc(consts, 1)
            pool.memset(w_hi[:, 0].bitcast(F32), 0.0).then_inc(w_zeroed, 1)
            pool.memset(w_lo[:, 0].bitcast(F32), 0.0).then_inc(w_zeroed, 1)
            pool.wait_ge(consts, 1)
            pool.affine_select(out=ident[:], in_=ident[:], compare_op=ALU.not_equal, fill=1.0, base=0,
                               pattern=[[-1, P]], channel_multiplier=1).then_inc(consts, 1)
            pool.memset(cap[:], 0.0).then_inc(row_pool, 1)
            pool.memset(sel_f[:], 0.0).then_inc(row_pool, 1)
            pool.memset(half_c[:], -0.5).then_inc(row_pool, 1)
            pool.memset(keep[:], 1.0).then_inc(row_pool, 1)
            pool.memset(m_before[:], 0.0).then_inc(row_pool, 1)
            pool.iota(inv_count[:], pattern=[[1, 16]], base=1, channel_multiplier=0,
                      allow_small_or_imprecise_dtypes=True).then_inc(row_pool, 1)
            pool.wait_ge(row_pool, 4)
            pool.affine_select(out=cap[:], in_=cap[:], compare_op=ALU.is_ge, fill=NEG, base=0,
                               pattern=[[1, P]], channel_multiplier=-1).then_inc(row_pool, 1)
            pool.memset(keep[:].rearrange("h (c t) -> h c t", t=P)[:, :, 0:1], 0.0).then_inc(row_pool, 1)
            for q in range(4):
                part = sel_f[:, H * (q // 2):H * (q // 2) + H]
                pool.wait_ge(row_pool, 8 + q)
                pool.affine_select(out=part, in_=part, compare_op=ALU.not_equal, fill=1.0, base=-32 * q,
                                   pattern=[[-1, H]], channel_multiplier=1).then_inc(row_pool, 1)
            pool.wait_ge(row_pool, 12)
            pool.tensor_copy(sel[:], sel_f[:]).then_inc(row_pool, 1)

            def lo_gates():
                pool.wait_ge(w_hi_done, 1)
                pool.tensor_tensor(w_lo[:, 0, :, 0:H], gate_raw[:, :, 0:H], w_hi[:, 0, :, 0:H].bitcast(F32),
                                   ALU.subtract).then_inc(row_pool, 1)
                pool.wait_ge(row_pool, 14)
                pool.tensor_tensor(w_lo[:, 0, :, 32:32 + H], gate_raw[:, :, H:2 * H],
                                   w_hi[:, 0, :, 32:32 + H].bitcast(F32), ALU.subtract).then_inc(w_ready, 1)

            def lo(slot, need, n=KT):
                pool.wait_ge(w_hi_done, need)
                pool.tensor_tensor(w_lo[:, slot, 0:n], w_raw[:, slot, 0:n], w_hi[:, slot, 0:n].bitcast(F32),
                                   ALU.subtract).then_inc(w_ready, 1)

            def norm_lo(k):
                c = k % NB
                for n in range(0, KT, 2):
                    pool.wait_ge(hn_hi_done, KT * k + n + 1)
                    pool.tensor_tensor(hn_lo[:, n, blk(c)], nts[k % 2][:, n, :], hn_hi[:, n, blk(c)].bitcast(F32),
                                       ALU.subtract).then_inc(hn_lo_pool, 1)

            pool.wait_ge(w_zeroed, 2)
            lo_gates()
            norm_lo(0)
            lo(1, 2)
            norm_lo(1)
            norm_lo(2)
            pool.wait_ge(x_squared, N_TOK)
            pool.wait_ge(normed, NB * KT)
            pool.memset(rr[:].bitcast(F32), 0.0).then_inc(row_pool, 1)
            with pool.Fori(0, 2 * H - 1) as i:
                lo(0, i * 2 + 3)
                lo(1, i * 2 + 4)

            def decay_state(half_):
                rs = slice(half_ * (R // 2), (half_ + 1) * (R // 2))
                pool.wait_ge(bc_loaded[half_], 16)
                pool.wait_ge(s_state, 4 * half_ + 1)
                pool.tensor_tensor(C_s[:, rs, :], C_s[:, rs, :],
                                   bc_s[:, :, 2 * P:2 * P + 1].to_broadcast([P, R // 2, P]), ALU.mult)\
                    .then_inc(s_scaled, 1)

            decay_state(0)
            lo(0, 4 * H + 1)
            decay_state(1)
            lo(1, 4 * H + 2)

            pool.wait_ge(s_state, 8)
            pool.wait_ge(C_stored, 16 * H)
            pool.memset(C_st[:], 0.0).then_inc(m_init, 1)
            pool.memset(v_tok[:, :, :, P:P + 1], 1.0).then_inc(m_init, 1)
            pool.memset(u[:, :, 0:BUF], 0.0).then_inc(m_init, 1)
            pool.wait_ge(s_head, 8)
            pool.tensor_scalar(s_small[:, 5:6], s_small[:, 4:5], 1.0 / P, EPS, ALU.mult, ALU.add).then_inc(s_pow, 1)
            pool.wait_ge(s_pow, 1)
            pool.tensor_tensor(s_small[:, 6:7], s_small[:, 5:6], half_c[0:R, 0:1], ALU.pow).then_inc(s_pow, 1)

            def weigh_v(c):
                pool.wait_ge(kv_tok, 2 * c + 2)
                pool.wait_ge(w_exp, c + 1)
                if c:
                    pool.wait_ge(kv_done, c)
                else:
                    pool.wait_ge(m_init, 3)
                wend = wt[:, c % 2, :, P - 1:P].to_broadcast([P, H, P + 1])
                pool.tensor_tensor(wv[:], v_tok[:, c % 2], wend, ALU.mult).then_inc(wv_done, 1)

            def head_rms(c):
                pool.wait_ge(h_squared, c + 1)
                if c:
                    pool.wait_ge(hs_done, c)
                pool.tensor_scalar(ms_h[:], ssq_h[:], 1.0 / P, EPS, ALU.mult, ALU.add).then_inc(rs_step, 1)
                pool.wait_ge(rs_step, 2 * c + 1)
                pool.tensor_tensor(rs_h[:], ms_h[:], half_c[:], ALU.pow).then_inc(rs_step, 1)

            wsteps = [0]

            def windows(n, c):
                g, q = GROUP_OF[n], NB * n + (NB - 1 - c)
                pool.wait_ge(unit_evac, UNITS_U + NB * n + NB)
                if q:
                    pool.wait_ge(pooled, q)
                t0, t1 = c * BW, min((c + 1) * BW, T)
                src, at_t0 = u[:, g, :], BUF + t0
                for d in range(g + 1):
                    k = 1 << d
                    need = WINDOWS[g] - 2 * k
                    n_col = t1 - t0 + need
                    a = at_t0 - need
                    if d:
                        pool.wait_ge(win_step, wsteps[0])
                    ins = pool.tensor_tensor(win[:, d % 2, 0:n_col], src[:, a:a + n_col], src[:, a - k:a - k + n_col],
                                             ALU.add)
                    if d < g:
                        ins.then_inc(win_step, 1)
                        wsteps[0] += 1
                    else:
                        ins.then_inc(win_done, 1)
                    src, at_t0 = win[:, d % 2, :], need

            def windows_at(c, place):
                for n, b in POOL_AT.get((c, place), ()):
                    windows(n, b)

            pool.wait_ge(s_head, 9)
            LO_AT = {0: J_U + 1, 1: J_U + 2, 3: J_U + 3, 4: J_POOL}
            for c in range(CH):
                def lo_at():
                    lo(LO_AT[c] % 2, LO_AT[c] + 1, G if LO_AT[c] == J_POOL else KT)

                if c in (0, 3):
                    lo_at()
                weigh_v(c)
                windows_at(c - 1, 1)
                head_rms(c)
                if c in (1, 4):
                    lo_at()
                windows_at(c, 0)
                if c == 5:
                    lo(0, J_OUT + 1)
            lo(1, J_OUT + 2)
            with pool.Fori(0, KT // 2 - 1) as i:
                lo(0, i * 2 + J_OUT + 3)
                lo(1, i * 2 + J_OUT + 4)

            def gu_lo(a, need):
                pool.wait_ge(gu_hi, need)
                pool.tensor_tensor(guw[:, a, :, 1], w_raw[:], guw[:, a, :, 0].bitcast(F32), ALU.subtract)\
                    .then_inc(gu_ready, 1)

            def down_lo(need):
                pool.wait_ge(dw_hi, need)
                pool.tensor_tensor(w_lo[:].rearrange("p a k c -> p a (k c)"), dw_raw[:],
                                   w_hi[:].rearrange("p a k c -> p a (k c)").bitcast(F32), ALU.subtract)\
                    .then_inc(dw_ready, 1)

            gu_lo(0, 1)
            gu_lo(1, 2)
            gu_lo(0, 3)
            gu_lo(1, 4)
            with pool.Fori(1, FT // 2 - 1) as i:
                down_lo(i)
                gu_lo(0, i * 2 + 3)
                gu_lo(1, i * 2 + 4)
            down_lo(FT // 2 - 1)
            pool.wait_ge(dw_hi, FT // 2)
            pool.tensor_tensor(dw_last[:, 1], dw_raw[:], dw_last[:, 0].bitcast(F32), ALU.subtract).then_inc(dw_ready, 1)

        @block.scalar
        def _(act):
            def turn_half(tt):
                r = rows_of(tt)
                act.wait_ge(x_turned, 2 * tt + 1)
                b = 2 + 2 * (tt % 2)
                act.activation(xT[:, 0:4, tt * P:tt * P + r],
                               ps[:, b, :].rearrange("p (k t) -> p k t", t=P)[:, :, 0:r], ACT.Copy).then_inc(xt_act, 1)

            def square(tt):
                r = rows_of(tt)
                act.wait_ge(x_loaded[tt % 4], 16 * (tt // 4 + 1))
                if tt:
                    act.wait_ge(x_squared, tt)
                act.activation(sq_junk[0:r, :], x_tok[0:r, tt % 4, :], ACT.Square, accum_out=by_tok[0:r, 0, tt:tt + 1])\
                   .then_inc(x_squared, 1)
                act.wait_ge(x_squared, tt + 1)
                if tt == 0:
                    act.wait_ge(consts, 4)
                act.activation(by_tok[0:r, 1, tt:tt + 1], by_tok[0:r, 0, tt:tt + 1], ACT.Sqrt, bias=eps_c[0:r, :],
                               scale=1.0 / D).then_inc(x_std, 1)

            def norm_root(c):
                act.wait_ge(norm_total, c + 1)
                if c:
                    act.wait_ge(norm_rstd, c)
                act.activation(std[:], ps[:, 7, 0:BW], ACT.Sqrt, bias=eps_c[:], scale=1.0 / D).then_inc(norm_std, 1)

            def scaled_hi(c):
                act.wait_ge(unit_done, UNITS_OUT + NB * (KT - 1) + c + 1)
                for n in range(KT):
                    act.wait_ge(resid, n * NB + c + 1)
                    act.activation(hn_hi[:, n, blk(c)], xT[:, n, blk(c)], ACT.Copy, scale=gffn_c[:, n:n + 1])\
                       .then_inc(hn_hi_done, 1)

            def norm_hi(k):
                for n in range(KT):
                    act.wait_ge(normed, KT * k + n + 1)
                    act.activation(hn_hi[:, n, blk(k % NB)], nts[k % 2][:, n, :], ACT.Copy).then_inc(hn_hi_done, 1)

            def hi(slot, loaded, free, n=KT):
                act.wait_ge(raw_loaded[slot], loaded)
                if free is not None:
                    act.wait_ge(unit_done, free)
                act.activation(w_hi[:, slot, 0:n], w_raw[:, slot, 0:n], ACT.Copy).then_inc(w_hi_done, 1)

            def evac(dst, n_units, func=ACT.Copy, scale=1.0):
                act.wait_ge(unit_done, n_units)
                act.activation(dst, ps[:, n_units_bank[0] % 2, 0:BW], func, scale=scale).then_inc(unit_evac, 1)
                n_units_bank[0] += 1

            n_units_bank = [0]

            def evac_gates(c):
                act.wait_ge(unit_done, 2 * c + 1)
                act.activation(gi[:, blk(c)], PA[0][0:H, 0:BW], ACT.Identity, bias=bgate[0:H, :])
                act.activation(gf[:, blk(c)], PA[0][32:32 + H, 0:BW], ACT.Identity, bias=bgate[32:32 + H, :])\
                   .then_inc(unit_evac, 1)
                n_units_bank[0] += 1

            def evac_q0(c):
                act.wait_ge(x_spilled[c], 16)
                evac(qkvo[:, 0, blk(c)], 2 * c + 2)

            turn_half(0)
            square(0)
            turn_half(1)
            square(1)
            turn_half(2)
            square(2)
            act.wait_ge(gate_w_loaded, 16)
            act.wait_ge(w_zeroed, 2)
            act.activation(w_hi[:, 0, :, 0:H], gate_raw[:, :, 0:H], ACT.Copy)
            act.activation(w_hi[:, 0, :, 32:32 + H], gate_raw[:, :, H:2 * H], ACT.Copy).then_inc(w_hi_done, 1)
            turn_half(3)
            norm_hi(0)
            hi(1, 16, None)
            square(3)
            turn_half(4)
            square(4)
            turn_half(5)
            square(5)
            norm_hi(1)
            act.wait_ge(vecs_loaded, 16 * 7)
            evac_gates(0)
            turn_half(6)
            square(6)
            turn_half(7)
            square(7)
            evac_q0(0)
            turn_half(8)
            square(8)
            norm_hi(2)
            evac_gates(1)
            evac_q0(1)
            evac_gates(2)

            act.wait_ge(unit_evac, 2 * NB - 1)
            act.activation(ab[:], gf[:], ACT.Abs).then_inc(row_act, 1)
            act.wait_ge(row_act, 1)
            act.activation(ab[:], ab[:], ACT.Exp, scale=-1.0).then_inc(row_act, 1)
            act.wait_ge(row_act, 2)
            act.activation(ab[:], ab[:], ACT.Ln, bias=ones[0:H, 0:1]).then_inc(row_act, 1)

            evac_q0(2)

            def pair(i, tile, func, scale):
                for d in range(2):
                    slot = d
                    hi(slot, i * 16 + (16 if slot == 0 else 32), i * 6 + (NB * d + NB))
                    for c in range(NB):
                        dst = qkvo[:, bass.ds(tile + d, 1), blk(c)].rearrange("p a t -> p (a t)")
                        evac(dst, i * 6 + NB + NB * d + c + 1, func, scale)

            hi(0, 16, 2 * NB - 1)
            hi(1, 32, 2 * NB)
            for c in range(NB):
                evac(qkvo[:, 1, blk(c)], 2 * NB + c + 1)
            for part, (func, scale) in enumerate(((ACT.Copy, 1.0), (ACT.Copy, KSCALE), (ACT.Copy, 1.0),
                                                  (ACT.Sigmoid, 1.0))):
                with act.Fori(max(2 * part, 1), 2 * part + 2) as i:
                    pair(i, i * 2, func, scale)
                if part == 0:
                    act.wait_ge(row_pool, 15)
                    act.wait_ge(row_dve, 6)
                    act.activation(rr[0:H, :], r_row[:], ACT.Copy).then_inc(row_act, 1)
                    act.wait_ge(row_dve, 8)
                    act.activation(g_row[:], g_row[:], ACT.Exp).then_inc(row_act, 1)
                    act.activation(ab[:, 0:T], m_row[:], ACT.Exp, scale=-1.0).then_inc(row_act, 1)
                    act.wait_ge(row_act, 5)
                    act.activation(g_hi[:], g_row[:], ACT.Copy).then_inc(row_act, 1)
                    act.wait_ge(row_act, 7)
                    act.activation(rr[64:64 + H, :], g_hi[:].bitcast(F32), ACT.Copy).then_inc(row_act, 1)
                    act.wait_ge(sg_dve, 5)
                    act.activation(sample_exp[:].rearrange("h b q -> h (b q)"),
                                   sample_exp[:].rearrange("h b q -> h (b q)"), ACT.Exp).then_inc(sg_act, 1)

            def unit_u(k):
                j, c = J_U + k // NB, k % NB
                if c == 0:
                    nxt = j + 1
                    nth = nxt // 2 if nxt % 2 == 0 else (nxt + 1) // 2
                    hi(nxt % 2, 16 * nth, NB * (nxt - 1), G if nxt == J_POOL else KT)
                dst = u[:, GROUP_OF[j - J_U], BUF + c * BW:BUF + (c + 1) * BW]
                evac(dst, UNITS_U + k + 1)

            def exp_w(c):
                act.wait_ge(d_done, c + 1)
                act.activation(wt[:, c % 2], wt[:, c % 2], ACT.Exp).then_inc(w_exp, 1)

            def kv_by_token(c):
                act.wait_ge(kv_turned, 2 * c + 1)
                if c >= 2:
                    act.wait_ge(kv_done, c - 1)
                elif c == 0:
                    act.wait_ge(m_init, 3)
                act.activation(k_tok[:, c % 2], ps[:, 2, :].rearrange("p (h t) -> p h t", h=H), ACT.Copy)\
                   .then_inc(kv_tok, 1)
                act.wait_ge(kv_turned, 2 * c + 2)
                act.activation(v_tok[:, c % 2, :, 0:P], ps[:, 3, :].rearrange("p (h t) -> p h t", h=H), ACT.Copy)\
                   .then_inc(kv_tok, 1)

            def square_h(c):
                act.wait_ge(h_done, c + 1)
                if c:
                    act.wait_ge(rs_step, 2 * c)
                for h in range(H):
                    ins = act.activation(junk[:, h, :], h_tok[:, h, :], ACT.Square, accum_out=ssq_h[:, h:h + 1])
                ins.then_inc(h_squared, 1)

            def p_split_hi(n):
                g = GROUP_OF[n]
                if n == 0:
                    act.wait_ge(unit_done, UNITS_POOL)
                act.wait_ge(pooled, NB * (n + 1))
                act.activation(hn_hi[:, g, :], u[:, g, BUF:BUF + N], ACT.Copy).then_inc(p_hi, 1)

            def pmix(q):
                g, c = GROUP_OF[q // NB], q % NB
                act.wait_ge(unit_done, UNITS_POOL + q + 1)
                act.activation(hn_hi[:, H + g, blk(c)], ps[:, (UNITS_POOL + q) % 2, 0:BW], ACT.Copy,
                               scale=pscale_c[:, g:g + 1]).then_inc(pmix_hi, 1)

            exp_w(0)
            for c in range(CH):
                kv_by_token(c)
                if c < 6:
                    unit_u(2 * c)
                elif c == 6:
                    p_split_hi(0)
                    p_split_hi(1)
                    p_split_hi(2)
                else:
                    for q in (6, 7, 8):
                        pmix(q)
                square_h(c)
                if c + 1 < CH:
                    exp_w(c + 1)
                if c < 6:
                    unit_u(2 * c + 1)
                    if c == 5:
                        hi(0, 16 * (J_OUT // 2), UNITS_POOL)
                elif c == 6:
                    p_split_hi(3)
                    for q in range(6):
                        pmix(q)
                else:
                    for q in (9, 10, 11):
                        pmix(q)
            hi(1, 16 * ((J_OUT + 2) // 2), UNITS_OUT)

            act.wait_ge(s_mixed, 1)
            for c in range(NB):
                act.wait_ge(mixed, min(CH, TILES_OF[c]))
                act.activation(hn_hi[:, 0:H, blk(c)], qkvo[:, 3 * H:4 * H, blk(c)], ACT.Copy).then_inc(hmix_hi, 1)

            def out_square(m, c):
                act.wait_ge(resid, m * NB + c + 1)
                act.wait_ge(resid_sum, m * NB + c + 1)
                act.activation(out_sq[:, c, :], xT[:, bass.ds(m, 1), blk(c)].rearrange("p a t -> p (a t)"),
                               ACT.Square).then_inc(resid_sq, 1)

            def out_squares(m):
                for c in range(NB):
                    out_square(m, c)

            act.wait_ge(hmix_lo, NB)
            with act.Fori(0, KT // 2 - 1) as i:
                out_squares(i * 2)
                hi(0, i * 16 + 16 * (J_OUT // 2 + 1), i * 6 + UNITS_OUT + NB)
                out_squares(i * 2 + 1)
                hi(1, i * 16 + 16 * (J_OUT // 2 + 2), i * 6 + UNITS_OUT + 2 * NB)
            out_squares(KT - 2)
            act.wait_ge(gu_loaded, 32)
            act.activation(guw[:, 0, :, 0], w_raw[:], ACT.Copy).then_inc(gu_hi, 1)
            for c in range(NB):
                scaled_hi(c)
                out_square(KT - 1, c)
            act.wait_ge(rows_stored, 16 * (H + 2))
            for c in range(NB):
                norm_root(c)

            def gu_split(a, tile, used):
                act.wait_ge(gu_loaded, tile * 32 + 32)
                if used is not None:
                    act.wait_ge(gu_done, used)
                act.activation(guw[:, a, :, 0], w_raw[:], ACT.Copy).then_inc(gu_hi, 1)

            def down_split(i, used):
                act.wait_ge(dw_loaded, i * 16 + 16)
                act.wait_ge(*used)
                act.activation(w_hi[:].rearrange("p a k c -> p a (k c)"), dw_raw[:], ACT.Copy).then_inc(dw_hi, 1)

            def hidden(base, e, half):
                act.wait_ge(gate_scaled, base + (e + 1))
                act.activation(ps[:, gate_bank(e), 0:BW], hf[:, hslot(half, e), :], ACT.Sigmoid).then_inc(sig_done, 1)

            def hslot(half, e):
                return (6 * half + e) % 4

            def hidden_hi(base, e, half):
                act.wait_ge(hid_f, base + (e + 1))
                act.activation(hid[:, 2 * half + e // NB, 0, blk(e % NB)], hf[:, hslot(half, e), :], ACT.Copy)\
                   .then_inc(hid_hi, 1)

            def down_split_last(used):
                act.wait_ge(dw_loaded, 16 * (FT // 2))
                act.wait_ge(gu_done, used)
                act.activation(dw_last[:, 0], dw_raw[:], ACT.Copy).then_inc(dw_hi, 1)

            def act_gu(base, it, half, nxt0=True, first=False):
                for e in range(6):
                    hidden(base, e, half)
                    if e == 0 and not first:
                        down_split(it + (-1), (gu_done, 1) if isinstance(it, int) and it == 1
                                   else (down_done, it * 24 + (-24)))
                    if e == NB and nxt0:
                        gu_split(0, it * 2 + 2, it * 6 + NB)
                    if e == NB and not nxt0:
                        down_split_last(base + NB)
                    if e:
                        hidden_hi(base, e - 1, half)
                hidden_hi(base, 5, half)
                if nxt0:
                    gu_split(1, it * 2 + 3, it * 6 + 6)

            gu_split(1, 1, None)
            act_gu(0, 0, 0, first=True)
            act_gu(6, 1, 1)
            with act.Fori(0, FT // 4 - 1) as i:
                act_gu(i * 12 + 12, i * 2 + 2, 0)
                act_gu(i * 12 + 18, i * 2 + 3, 1)
            last = FT // 2 - 1
            act_gu(6 * last, last, 0, nxt0=False)

            for tt in range(N_TOK):
                r = rows_of(tt)
                b = 2 * (tt % 2)
                act.wait_ge(y_turned, tt + 1)
                if tt >= 2:
                    act.wait_ge(y_done, tt - 1)
                    act.wait_ge(y_stored[tt % 2], 16 * (tt // 2))
                act.activation(y_tok[0:r, tt % 2, :].rearrange("p (a t) -> p a t", a=2), ps[0:r, b:b + 2, :], ACT.Square,
                               accum_out=by_tok[0:r, 0, tt:tt + 1]).then_inc(y_ss, 1)
                act.wait_ge(y_ss, tt + 1)
                act.activation(by_tok[0:r, 1, tt:tt + 1], by_tok[0:r, 0, tt:tt + 1], ACT.Sqrt,
                               bias=eps_c[0:r, :], scale=1.0 / D).then_inc(y_std, 1)

        LAST_PARTS = ((0, 3 * P), (3 * P, 5 * P), (5 * P, 7 * P), (7 * P, N))
        FINAL_TURN = {9: 0, 11: 1, 13: 2, 17: 3, 20: 4, 25: 5, 28: 6}
        FINAL_AFTER = {11: 0, 13: 1, 16: 2, 20: 3, 23: 4, 28: 5, 31: 6}

        @block.vector
        def _(dve):
            def turn_half(tt):
                r = rows_of(tt)
                dve.wait_ge(x_turned, 2 * tt + 2)
                b = 3 + 2 * (tt % 2)
                dve.tensor_copy(xT[:, 4:8, tt * P:tt * P + r],
                                ps[:, b, :].rearrange("p (k t) -> p k t", t=P)[:, :, 0:r]).then_inc(xt_dve, 1)

            def root_to_rstd(tt):
                r = rows_of(tt)
                dve.wait_ge(x_std, tt + 1)
                dve.reciprocal(by_tok[0:r, 2, tt:tt + 1], by_tok[0:r, 1, tt:tt + 1]).then_inc(x_rstd, 1)

            def take_rstd(tt):
                r = rows_of(tt)
                dve.wait_ge(rstd_spread, tt + 1)
                dve.tensor_copy(rstd_x[:, tt * P:tt * P + r], ps[:, 6 + tt % 2, 0:r])\
                   .then_inc(rstd_copied, 1)

            def norm(k, g):
                c = k % NB
                dve.wait_ge(rstd_copied, TILES_OF[c])
                dve.wait_ge(xt_act, TILES_OF[c])
                dve.wait_ge(xt_dve, TILES_OF[c])
                if k >= 2:
                    dve.wait_ge(hn_lo_pool, 4 * (k - 1))
                    dve.wait_ge(hn_lo_dve, 4 * (k - 1))
                for n in range(KT):
                    dve.scalar_tensor_tensor(out=nts[k % 2][:, n, :], in0=xT[:, n, blk(c)], scalar=g[:, n:n + 1],
                                             in1=rstd_x[:, blk(c)], op0=ALU.mult, op1=ALU.mult).then_inc(normed, 1)
                    if n >= 3 and n % 2:
                        lo_odd(k, n - 2)
                lo_odd(k, KT - 1)

            def lo_odd(k, n):
                dve.wait_ge(hn_hi_done, KT * k + n + 1)
                dve.tensor_tensor(hn_lo[:, n, blk(k % NB)], nts[k % 2][:, n, :], hn_hi[:, n, blk(k % NB)].bitcast(F32),
                                  ALU.subtract).then_inc(hn_lo_dve, 1)

            turn_half(0)
            root_to_rstd(0)
            turn_half(1)
            root_to_rstd(1)
            take_rstd(0)
            turn_half(2)
            root_to_rstd(2)
            take_rstd(1)
            take_rstd(2)
            turn_half(3)
            dve.wait_ge(vecs_loaded, 16 * 7)
            norm(0, gmix_c)
            turn_half(4)
            root_to_rstd(3)
            root_to_rstd(4)
            take_rstd(3)
            take_rstd(4)
            turn_half(5)
            root_to_rstd(5)
            take_rstd(5)
            norm(1, gmix_c)
            turn_half(6)
            root_to_rstd(6)
            turn_half(7)
            root_to_rstd(7)
            take_rstd(6)
            take_rstd(7)
            turn_half(8)
            root_to_rstd(8)
            take_rstd(8)
            norm(2, gmix_c)

            dve.wait_ge(unit_evac, 2 * NB - 1)
            dve.wait_ge(row_act, 1)
            dve.tensor_scalar(gf[:], gf[:], 0.0, None, ALU.min).then_inc(row_dve, 1)
            dve.wait_ge(row_act, 3)
            dve.wait_ge(row_dve, 1)
            dve.tensor_tensor(gf[:], gf[:], ab[:], ALU.subtract).then_inc(row_dve, 1)
            dve.wait_ge(row_dve, 2)
            dve.wait_ge(row_pool, 15)
            dve.tensor_tensor_scan(b_row[:], keep[:], gf[:, 0:T], 0.0, ALU.mult, ALU.add).then_inc(row_dve, 1)
            dve.tensor_tensor_scan(m_row[:], gf[:, 0:T], gi[:, 0:T], 0.0, ALU.add, ALU.max).then_inc(row_dve, 1)
            dve.tensor_tensor(sample_f[:], gf[:, T:N], m0[:], ALU.add).then_inc(sg_dve, 1)
            dve.wait_ge(sg_dve, 1)
            dve.tensor_tensor(m_s[:], sample_f[:], gi[:, T:N], ALU.max).then_inc(sg_dve, 1)
            dve.wait_ge(sg_dve, 2)
            dve.tensor_tensor(sample_exp[:, :, 0], gi[:, T:N], m_s[:], ALU.subtract).then_inc(sg_dve, 1)
            dve.tensor_tensor(sample_exp[:, :, 1], sample_f[:], m_s[:], ALU.subtract).then_inc(sg_dve, 1)
            dve.tensor_scalar(sample_exp[:, :, 2], m_s[:], -1.0, None, ALU.mult).then_inc(sg_dve, 1)
            dve.wait_ge(row_dve, 4)
            dve.tensor_tensor(gi[:, 0:T], gi[:, 0:T], b_row[:], ALU.subtract).then_inc(row_dve, 1)
            dve.tensor_tensor(r_row[:], b_row[:], m_row[:], ALU.subtract).then_inc(row_dve, 1)
            dve.tensor_copy(m_before[:, 1:CH], m_row[:, P - 1:T - 1:P]).then_inc(row_dve, 1)
            dve.wait_ge(row_dve, 7)
            dve.tensor_tensor(g_row[:].rearrange("h (c t) -> h c t", t=P), r_row[:].rearrange("h (c t) -> h c t", t=P),
                              m_before[:].rearrange("h (c a) -> h c a", a=1).to_broadcast([H, CH, P]), ALU.add)\
               .then_inc(row_dve, 1)
            dve.wait_ge(row_act, 4)
            dve.tensor_tensor(rr[32:32 + H, :], r_row[:], rr[0:H, :].bitcast(F32), ALU.subtract).then_inc(row_dve, 1)
            dve.wait_ge(row_act, 7)
            dve.tensor_tensor(rr[96:96 + H, :], g_row[:], g_hi[:].bitcast(F32), ALU.subtract).then_inc(row_dve, 1)
            dve.wait_ge(row_dve, 8)
            dve.tensor_copy(m_before[:, 0:1], m_row[:, T - 1:T]).then_inc(row_dve, 1)
            dve.reciprocal(inv_count[:], inv_count[:]).then_inc(row_dve, 1)
            dve.wait_ge(cols_turned, 1)
            dve.tensor_copy(cols[:].rearrange("p a c h -> p (a c h)"), ps[:, 2, 0:2 * CH * H]).then_inc(cols_done, 1)
            dve.wait_ge(buf_turned, 1)
            for g in range(G):
                view = ps[:, 3, g * P:g * P + S * BUF].rearrange("p (b j) -> p b j", j=BUF)
                dve.tensor_reduce(buf_sum[:, g, :], view[:, :, BUF - (WINDOWS[g] - 1):BUF], AX.X, ALU.add)\
                   .then_inc(buf_summed, 1)

            dve.wait_ge(unit_evac, NB * (1 + 3 * H))
            dve.tensor_copy(qkv_s[:].rearrange("p a (h b) -> p (a h) b", h=H), qkvo[:, 0:3 * H, T:N]).then_inc(s_gathered, 1)
            dve.wait_ge(s_turned, 3)
            dve.tensor_copy(s_rows[:].rearrange("r a d -> r (a d)"), ps[0:R, 2, 0:3 * P]).then_inc(s_rows_done, 1)
            dve.wait_ge(s_rows_done, 1)
            dve.wait_ge(scol_loaded, 16)
            dve.tensor_scalar(s_pack[:, 0:P], s_rows[:, 0, :], scol[:, 1:2], None, ALU.mult).then_inc(s_packed, 1)
            dve.tensor_scalar(s_pack[:, P:2 * P], s_rows[:, 1, :], scol[:, 0:1], None, ALU.mult).then_inc(s_packed, 1)
            dve.tensor_copy(s_pack[:, 2 * P:2 * P + 1], scol[:, 1:2]).then_inc(s_packed, 1)
            dve.wait_ge(n_loaded, 16 * H)
            dve.wait_ge(s_packed, 3)
            dve.scalar_tensor_tensor(out=n_new[:], in0=n_s[:], scalar=scol[:, 1:2], in1=s_pack[:, P:2 * P],
                                     op0=ALU.mult, op1=ALU.add).then_inc(s_packed, 1)
            dve.tensor_tensor_reduce(tmp_rows[:], s_rows[:, 0, :], s_pack[:, P:2 * P], 1.0, 0.0, ALU.mult, ALU.add,
                                     s_small[:, 0:1]).then_inc(s_head, 1)
            dve.wait_ge(s_head, 1)
            dve.tensor_tensor_reduce(tmp_rows[:], n_s[:], s_pack[:, 0:P], 1.0, 0.0, ALU.mult, ALU.add,
                                     s_small[:, 1:2]).then_inc(s_head, 1)
            dve.wait_ge(s_head, 2)
            dve.tensor_tensor(s_small[:, 2:3], s_small[:, 0:1], s_small[:, 1:2], ALU.add).then_inc(s_head, 1)
            dve.wait_ge(s_head, 3)
            dve.scalar_tensor_tensor(out=s_small[:, 3:4], in0=s_small[:, 2:3], scalar=-1.0, in1=scol[:, 2:3],
                                     op0=ALU.mult, op1=ALU.max).then_inc(s_den, 1)
            dve.wait_ge(s_den, 1)
            dve.tensor_tensor(s_small[:, 3:4], s_small[:, 2:3], s_small[:, 3:4], ALU.max).then_inc(s_head, 1)
            dve.wait_ge(s_head, 4)
            dve.reciprocal(s_small[:, 7:8], s_small[:, 3:4]).then_inc(s_head, 1)
            for half_ in range(2):
                rs = slice(half_ * (R // 2), (half_ + 1) * (R // 2))
                dve.wait_ge(C_loaded[half_], 32)
                dve.wait_ge(bc_loaded[half_], 16)
                n0 = 4 * half_
                if half_:
                    dve.wait_ge(s_state, n0)
                dve.tensor_tensor(tmp_s[:], C_s[:, rs, :], bc_s[:, :, 0:P], ALU.mult).then_inc(s_state, 1)
                dve.wait_ge(s_state, n0 + 1)
                dve.tensor_reduce(inter[:, rs], tmp_s[:], AX.X, ALU.add).then_inc(s_state, 1)
                dve.wait_ge(s_state, n0 + 2)
                vcol = qkvo[:, 2 * H + 2 * half_:2 * H + 2 * half_ + 2, T:N].rearrange("p h (b a) -> p h b a", a=1)\
                    .to_broadcast([P, 2, S, P])
                dve.tensor_tensor(tmp_s[:].rearrange("p (h b) k -> p h b k", h=2),
                                  bc_s[:, :, P:2 * P].rearrange("p (h b) k -> p h b k", h=2), vcol, ALU.mult)\
                   .then_inc(s_state, 1)
                dve.wait_ge(s_scaled, half_ + 1)
                dve.wait_ge(s_state, n0 + 3)
                dve.tensor_tensor(C_s[:, rs, :], C_s[:, rs, :], tmp_s[:], ALU.add).then_inc(s_state, 1)

            def decode_heads():
                dve.wait_ge(inter_turned, 1)
                dve.wait_ge(s_head, 5)
                dve.scalar_tensor_tensor(out=h_s[:], in0=s_rows[:, 2, :], scalar=s_small[:, 0:1], in1=ps[0:R, 5, 0:P],
                                         op0=ALU.mult, op1=ALU.add).then_inc(s_head, 1)
                dve.wait_ge(s_head, 6)
                dve.tensor_scalar(h_s[:], h_s[:], s_small[:, 7:8], None, ALU.mult).then_inc(s_head, 1)
                dve.wait_ge(s_head, 7)
                dve.tensor_tensor_reduce(tmp_rows[:], h_s[:], h_s[:], 1.0, 0.0, ALU.mult, ALU.add,
                                         s_small[:, 4:5]).then_inc(s_head, 1)
                dve.wait_ge(s_pow, 2)
                dve.tensor_scalar(h_s[:], h_s[:], s_small[:, 6:7], None, ALU.mult).then_inc(s_head, 1)

            def scale_o():
                for h in range(H):
                    dve.wait_ge(unit_evac, NB * (1 + 3 * H + h + 1))
                    dve.tensor_scalar(qkvo[:, 3 * H + h, :], qkvo[:, 3 * H + h, :], ghead_c[:, h:h + 1], None, ALU.mult)\
                       .then_inc(o_scaled, 1)

            def exponents(c):
                dve.wait_ge(rg_done, c + 1)
                if c >= 2:
                    dve.wait_ge(p_done, c - 1)
                    dve.wait_ge(wv_done, c - 1)
                for h in range(H):
                    ins = dve.scalar_tensor_tensor(out=wt[:, c % 2, h, :], in0=ps[:, 2, h * P:(h + 1) * P],
                                                   scalar=cols[:, 0, c, h:h + 1], in1=cap[:], op0=ALU.add, op1=ALU.min)
                ins.then_inc(d_done, 1)

            def scaled_q(c):
                gv = ps[:, 3, :].rearrange("p (h t) -> p h t", h=H)
                if c >= 2:
                    dve.wait_ge(c_done, c - 1)
                dve.tensor_copy(gend[:, c % 2, :], gv[:, :, P - 1]).then_inc(gend_done, 1)
                if c:
                    dve.wait_ge(num_done, c)
                dve.tensor_tensor(qg[:], qkvo[:, 0:H, chk(c)], gv, ALU.mult).then_inc(qg_done, 1)

            def weights(c):
                dve.wait_ge(scores, c + 1)
                dve.wait_ge(w_exp, c + 1)
                if c:
                    dve.wait_ge(num_done, c)
                dve.tensor_tensor(pt[:], ps[:, 4, :].rearrange("p (h t) -> p h t", h=H), wt[:, c % 2], ALU.mult)\
                   .then_inc(p_done, 1)

            nv = ps[:, 6:8, 0:2 * (P + 1)].rearrange("p a (h v) -> p a h v", v=P + 1)

            def head(c):
                dve.wait_ge(num_done, c + 1)
                den2 = den[:].rearrange("p (a h) -> p a h", a=2)
                dve.scalar_tensor_tensor(out=den2, in0=nv[:, :, :, P], scalar=-1.0,
                                         in1=cols[:, 1, c, :].rearrange("p (a h) -> p a h", a=2), op0=ALU.mult,
                                         op1=ALU.max).then_inc(den_step, 1)
                dve.wait_ge(den_step, 3 * c + 1)
                dve.tensor_tensor(den2, nv[:, :, :, P], den2, ALU.max).then_inc(den_step, 1)
                dve.wait_ge(den_step, 3 * c + 2)
                if c:
                    dve.wait_ge(h_turned, c)
                dve.reciprocal(rden[:], den[:]).then_inc(den_step, 1)
                dve.wait_ge(den_step, 3 * c + 3)
                dve.tensor_tensor(h_tok[:].rearrange("p (a h) v -> p a h v", a=2), nv[:, :, :, 0:P],
                                  rden[:].rearrange("p (a h b) -> p a h b", a=2, b=1).to_broadcast([P, 2, 2, P]),
                                  ALU.mult).then_inc(h_done, 1)

            def scaled_h(c):
                dve.wait_ge(rs_step, 2 * c + 2)
                dve.tensor_tensor(h_tok[:], h_tok[:], rs_h[:].rearrange("p (h a) -> p h a", a=1).to_broadcast([P, H, P]),
                                  ALU.mult).then_inc(hs_done, 1)

            def mix(c):
                dve.wait_ge(h_turned, c + 1)
                if c == 0:
                    dve.wait_ge(o_scaled, H)
                dve.tensor_tensor(qkvo[:, 3 * H:4 * H, chk(c)], ps[:, 5, :].rearrange("p (h t) -> p h t", h=H),
                                  qkvo[:, 3 * H:4 * H, chk(c)], ALU.mult).then_inc(mixed, 1)

            def state(c):
                dve.wait_ge(kv_done, c + 1)
                dve.wait_ge(gend_done, c + 1)
                if c:
                    dve.wait_ge(c_done, c)
                for h in range(H):
                    ins = dve.scalar_tensor_tensor(out=C_st[:, h, :], in0=C_st[:, h, :], scalar=gend[:, c % 2, h:h + 1],
                                                   in1=nv[:, h // 2, h % 2, :], op0=ALU.mult, op1=ALU.add)
                ins.then_inc(c_done, 1)

            psteps = [0]

            def p_wait():
                if psteps[0]:
                    dve.wait_ge(p_step, psteps[0])

            def p_inc(ins):
                psteps[0] += 1
                ins.then_inc(p_step, 1)

            def pool_block(n, c):
                g, q = GROUP_OF[n], NB * n + (NB - 1 - c)
                k = WINDOWS[g]
                if c == NB - 1:
                    dve.wait_ge(unit_evac, UNITS_U + NB * n + NB)
                    dve.tensor_copy(u_last[:, g, :], u[:, g, BUF + T - BUF:BUF + N]).then_inc(u_saved, 1)
                    dve.wait_ge(u_saved, n + 1)
                    us = u[:, g, BUF + T:BUF + N]
                    dve.wait_ge(buf_summed, G)
                    p_wait()
                    p_inc(dve.tensor_tensor(small8[:], buf_sum[:, g, :], us, ALU.add))
                    p_wait()
                    p_inc(dve.scalar_tensor_tensor(out=us, in0=small8[:], scalar=1.0 / k, in1=us, op0=ALU.mult,
                                                   op1=ALU.subtract))
                t0, t1 = c * BW, min((c + 1) * BW, T)
                dve.wait_ge(win_done, q + 1)
                s = win[:, g % 2, 0:t1 - t0]
                head_n = k - 1 if c == 0 else 0
                if head_n:
                    uh = u[:, g, BUF:BUF + head_n]
                    p_inc(dve.tensor_tensor(s[:, 0:head_n], s[:, 0:head_n], inv_count[:, 0:head_n], ALU.mult))
                    p_wait()
                    p_inc(dve.tensor_tensor(uh, s[:, 0:head_n], uh, ALU.subtract))
                uu = u[:, g, BUF + t0 + head_n:BUF + t1]
                dve.scalar_tensor_tensor(out=uu, in0=s[:, head_n:], scalar=1.0 / k, in1=uu, op0=ALU.mult,
                                         op1=ALU.subtract).then_inc(pooled, 1)

            def pool_at(c, place):
                for n, b in POOL_AT.get((c, place), ()):
                    pool_block(n, b)

            def p_split_lo(n):
                g = GROUP_OF[n]
                dve.wait_ge(p_hi, n + 1)
                p_wait()
                dve.tensor_tensor(hn_lo[:, g, :], u[:, g, BUF:BUF + N], hn_hi[:, g, :].bitcast(F32), ALU.subtract)\
                   .then_inc(p_lo, 1)

            def pmix(q):
                g, c = GROUP_OF[q // NB], q % NB
                dve.wait_ge(pmix_hi, q + 1)
                dve.scalar_tensor_tensor(out=hn_lo[:, H + g, blk(c)], in0=ps[:, (UNITS_POOL + q) % 2, 0:BW],
                                         scalar=pscale_c[:, g:g + 1], in1=hn_hi[:, H + g, blk(c)].bitcast(F32),
                                         op0=ALU.mult, op1=ALU.subtract).then_inc(pmix_lo, 1)

            dve.wait_ge(m_init, 3)
            exponents(0)
            scaled_q(0)
            weights(0)
            decode_heads()
            scale_o()
            for c in range(CH):
                if c == 7:
                    pmix(6)
                if c:
                    mix(c - 1)
                if c == 7:
                    pmix(7)
                pool_at(c - 1, 0)
                if c == 6:
                    p_split_lo(0)
                head(c)
                if c + 1 < CH:
                    exponents(c + 1)
                    scaled_q(c + 1)
                state(c)
                if c + 1 < CH:
                    weights(c + 1)
                pool_at(c - 1, 1)
                if c == 6:
                    p_split_lo(1)
                    pmix(0)
                    pmix(1)
                if c == 7:
                    pmix(8)
                scaled_h(c)
                if c == 6:
                    p_split_lo(2)
                    pmix(2)
                    pmix(3)
                    p_split_lo(3)
                    pmix(4)
                    pmix(5)
                if c == 7:
                    for q in (9, 10, 11):
                        pmix(q)
                    dve.wait_ge(u_rows_turned, 1)
                    dve.tensor_copy(u_rows[:], ps[0:BUF + S, 5, :]).then_inc(u_rows_done, 1)
                if c == 3:
                    dve.wait_ge(hs_turned, 1)
                    dve.tensor_tensor(qkvo[:, 3 * H:4 * H, T:N], ps[:, 5, 0:R].rearrange("p (h b) -> p h b", h=H),
                                      qkvo[:, 3 * H:4 * H, T:N], ALU.mult).then_inc(s_mixed, 1)
            mix(CH - 1)

            for c in range(NB):
                dve.wait_ge(hmix_hi, c + 1)
                dve.tensor_tensor(hn_lo[:, 0:H, blk(c)], qkvo[:, 3 * H:4 * H, blk(c)], hn_hi[:, 0:H, blk(c)].bitcast(F32),
                                  ALU.subtract).then_inc(hmix_lo, 1)
            dve.wait_ge(C_turned, 1)
            dve.wait_ge(rows_stored, 16 * (H + 2))
            dve.tensor_copy(C_fin[:].rearrange("p h k -> p (h k)"), ps[:, 2, :]).then_inc(C_out, 1)
            dve.tensor_copy(n_fin[:], ps[0:H, 3, 0:P]).then_inc(C_out, 1)

            dve.wait_ge(hmix_lo, NB)
            for c in range(NB):
                dve.memset(ssq[:, c, :], 0.0).then_inc(resid_sum, 1)
            dve.wait_ge(x_back, 16 * NB)

            def residual(m, start, c):
                dve.wait_ge(unit_done, m * NB + UNITS_OUT + c + 1)
                xs = xT[:, bass.ds(m, 1), blk(c)].rearrange("p a t -> p (a t)")
                dve.tensor_tensor(xs, ps[:, (start + c) % 2, 0:BW], xs, ALU.add).then_inc(resid, 1)

            def square_sum(m, c):
                dve.wait_ge(resid_sq, m * NB + c + 1)
                dve.wait_ge(resid_sum, m * NB + c + 1)
                dve.tensor_tensor(ssq[:, c, :], ssq[:, c, :], out_sq[:, c, :], ALU.add).then_inc(resid_sum, 1)

            def out_tile(m, start):
                for c in range(NB):
                    residual(m, start, c)
                for c in range(NB):
                    square_sum(m, c)

            def scaled_lo(c):
                for n in range(KT):
                    dve.wait_ge(hn_hi_done, KT * (NB + c) + n + 1)
                    dve.scalar_tensor_tensor(out=hn_lo[:, n, blk(c)], in0=xT[:, n, blk(c)], scalar=gffn_c[:, n:n + 1],
                                             in1=hn_hi[:, n, blk(c)].bitcast(F32), op0=ALU.mult, op1=ALU.subtract)\
                       .then_inc(hn_lo_dve, 1)

            def norm_inverse(c):
                dve.wait_ge(norm_std, c + 1)
                dve.reciprocal(rstd[:, c, :], std[:]).then_inc(norm_rstd, 1)

            with dve.Fori(0, KT // 2 - 1) as i:
                out_tile(i * 2, UNITS_OUT)
                out_tile(i * 2 + 1, UNITS_OUT + NB)
            out_tile(KT - 2, UNITS_OUT)
            residual(KT - 1, UNITS_OUT + NB, 0)
            scaled_lo(0)
            residual(KT - 1, UNITS_OUT + NB, 1)
            scaled_lo(1)
            residual(KT - 1, UNITS_OUT + NB, 2)
            square_sum(KT - 1, 0)
            scaled_lo(2)
            square_sum(KT - 1, 1)
            square_sum(KT - 1, 2)
            for c in range(NB):
                norm_inverse(c)

            def hidden(base, half):
                for e in range(6):
                    s, r = hf[:, (6 * half + e) % 4, :], rstd[:, e % NB, :]
                    dve.wait_ge(gu_done, base + (e + 1))
                    if isinstance(base, int) and base + e < NB:
                        dve.wait_ge(norm_rstd, e + 1)
                    dve.tensor_tensor(s, ps[:, gate_bank(e), 0:BW], r, ALU.mult).then_inc(gate_scaled, 1)
                    if e:
                        hidden_lo(base, e - 1, half)
                    dve.wait_ge(sig_done, base + (e + 1))
                    dve.tensor_tensor(s, ps[:, gate_bank(e), 0:BW], s, ALU.mult).then_inc(act_gate, 1)
                    dve.wait_ge(act_gate, base + (e + 1))
                    dve.tensor_tensor(s, ps[:, 2 + gate_bank(e), 0:BW], s, ALU.mult).then_inc(act_up, 1)
                    dve.wait_ge(act_up, base + (e + 1))
                    dve.tensor_tensor(s, s, r, ALU.mult).then_inc(hid_f, 1)
                hidden_lo(base, 5, half)

            def hidden_lo(base, e, half):
                dve.wait_ge(hid_hi, base + (e + 1))
                t, c = 2 * half + e // NB, e % NB
                dve.tensor_tensor(hid[:, t, 1, blk(c)], hf[:, (6 * half + e) % 4, :], hid[:, t, 0, blk(c)].bitcast(F32),
                                  ALU.subtract).then_inc(hid_lo, 1)

            def down(base):
                for c in range(NB):
                    for n in range(KT):
                        q = c * KT + n
                        dve.wait_ge(down_done, base + (q + 1))
                        dve.tensor_tensor(xT[:, n, blk(c)], ps[:, 4 + q % 4, 0:BW], xT[:, n, blk(c)], ALU.add)\
                           .then_inc(x_acc, 1)

            dve.wait_ge(C_fin_stored, 32)
            hidden(0, 0)
            with dve.Fori(0, FT // 4) as i:
                hidden(i * 12 + 6, 1)
                down(i * 48)
                hidden(i * 12 + 12, 0)
                down(i * 48 + 24)
            last = 24 * (FT // 2 - 1)

            def final(tt):
                r = rows_of(tt)
                b = 2 * (tt % 2)
                dve.wait_ge(y_std, tt + 1)
                dve.reciprocal(by_tok[0:r, 2, tt:tt + 1], by_tok[0:r, 1, tt:tt + 1]).then_inc(y_rstd, 1)
                dve.wait_ge(y_rstd, tt + 1)
                dve.wait_ge(gfin_loaded, 16)
                dve.scalar_tensor_tensor(out=y_tok[0:r, tt % 2, :].rearrange("p (a t) -> p a t", a=2),
                                         in0=ps[0:r, b:b + 2, :], scalar=by_tok[0:r, 2, tt:tt + 1],
                                         in1=gfin[0:r, :].rearrange("p (a t) -> p a t", a=2), op0=ALU.mult, op1=ALU.mult)\
                   .then_inc(y_done, 1)

            for c, (t0, t1) in enumerate(LAST_PARTS):
                for n in range(KT):
                    q = c * KT + n
                    dve.wait_ge(down_done, last + q + 1)
                    dve.tensor_tensor(xT[:, n, t0:t1], ps[:, 4 + q % 4, 0:t1 - t0], xT[:, n, t0:t1], ALU.add)\
                       .then_inc(x_acc, 1)
                    if q in FINAL_AFTER:
                        final(FINAL_AFTER[q])
            for tt in range(len(FINAL_AFTER), N_TOK):
                final(tt)

        @block.tensor
        def _(pe):
            def turn(tt):
                r = rows_of(tt)
                pe.wait_ge(x_loaded[tt % 4], 16 * (tt // 4 + 1))
                for half, freed in ((0, xt_act), (1, xt_dve)):
                    if tt >= 2:
                        pe.wait_ge(freed, tt - 1)
                    for n in range(4):
                        k = 4 * half + n
                        ins = pe.transpose(ps[:, 2 + 2 * (tt % 2) + half, n * P:n * P + r],
                                           x_tok[0:r, tt % 4, k * P:(k + 1) * P], ident[0:r, 0:r])
                    ins.then_inc(x_turned, 1)

            def spread_rstd(tt):
                r = rows_of(tt)
                pe.wait_ge(x_rstd, tt + 1)
                if tt >= 2:
                    pe.wait_ge(rstd_copied, tt - 1)
                pe.matmul(ps[:, 6 + tt % 2, 0:r], by_tok[0:r, 2, tt:tt + 1].to_broadcast([r, P]),
                          ident[0:r, 0:r], start=True, stop=True).then_inc(rstd_spread, 1)

            def norm_sum(c):
                pe.wait_ge(resid_sum, NB * KT + c + 1)
                if c:
                    pe.wait_ge(norm_std, c)
                pe.matmul(ps[:, 7, 0:BW], ones[:], ssq[:, c, :], start=True, stop=True).then_inc(norm_total, 1)

            def product(out, lhs_hi, lhs_lo, rhs_hi, rhs_lo, ks):
                for i, k in enumerate(ks):
                    pe.matmul(out, lhs_hi(k), rhs_hi(k), start=(i == 0), stop=False)
                    pe.matmul(out, lhs_hi(k), rhs_lo(k), start=False, stop=False)
                    ins = pe.matmul(out, lhs_lo(k), rhs_hi(k), start=False, stop=(i == len(ks) - 1))
                return ins

            def unit(slot, bank, c, ks=range(KT)):
                return product(ps[:, bank, 0:BW], lambda k: w_hi[:, slot, k, :], lambda k: w_lo[:, slot, k, :],
                               lambda k: hn_hi[:, k, blk(c)], lambda k: hn_lo[:, k, blk(c)], ks)

            def first_units(c, tile):
                pe.wait_ge(w_ready, tile + 1)
                pe.wait_ge(hn_lo_pool, 4 * (c + 1))
                pe.wait_ge(hn_lo_dve, 4 * (c + 1))
                if c:
                    pe.wait_ge(unit_evac, 2 * c + tile - 1)
                unit(tile, tile, c).then_inc(unit_done, 1)

            pe.wait_ge(consts, 4)
            turn(0)
            turn(1)
            spread_rstd(0)
            turn(2)
            spread_rstd(1)
            spread_rstd(2)
            turn(3)
            turn(4)
            first_units(0, 0)
            spread_rstd(3)
            spread_rstd(4)
            turn(5)
            spread_rstd(5)
            first_units(0, 1)
            turn(6)
            turn(7)
            spread_rstd(6)
            spread_rstd(7)
            first_units(1, 0)
            turn(8)
            spread_rstd(8)
            first_units(1, 1)
            first_units(2, 0)
            first_units(2, 1)
            pe.wait_ge(w_ready, 3)
            for c in range(NB):
                pe.wait_ge(unit_evac, 2 * NB + c - 1)
                unit(0, c % 2, c).then_inc(unit_done, 1)

            def pair(i):
                for d in range(2):
                    pe.wait_ge(w_ready, i * 2 + 2 + d)
                    for c in range(NB):
                        n = NB + NB * d + c
                        pe.wait_ge(unit_evac, i * 6 + (n - 1))
                        unit((1 + d) % 2, n % 2, c).then_inc(unit_done, 1)

            with pe.Fori(1, 4) as i:
                pair(i)
            pe.wait_ge(row_dve, 5)
            pe.wait_ge(row_act, 6)
            for n, row in enumerate((gi, ab)):
                for c in range(CH):
                    ins = pe.transpose(ps[:, 2, (n * CH + c) * H:(n * CH + c + 1) * H], row[:, chk(c)], ident[0:H, 0:H])
            ins.then_inc(cols_turned, 1)
            pe.wait_ge(buf_loaded, 16)
            for g in range(G):
                ins = pe.transpose(ps[:, 3, g * P:g * P + S * BUF], buf_rows[:, chk(g)], ident[0:S * BUF, 0:S * BUF])
            ins.then_inc(buf_turned, 1)
            with pe.Fori(4, 6) as i:
                pair(i)
            pe.wait_ge(s_gathered, 1)
            pe.wait_ge(cols_done, 1)
            for n in range(3):
                ins = pe.transpose(ps[0:R, 2, n * P:(n + 1) * P], qkv_s[:, n, :], ident[:])\
                    .then_inc(s_turned, 1)
            with pe.Fori(6, 8) as i:
                pair(i)

            def rows_everywhere(c):
                if c:
                    pe.wait_ge(kv_tok, 2 * c)
                for q, bank in ((0, 2), (1, 3)):
                    for h in range(H):
                        n = H * q + h
                        ins = pe.matmul(ps[:, bank, chk(h)], sel[:, n:n + 1].to_broadcast([P, P]), rr[:, chk(c)],
                                        start=True, stop=True)
                ins.then_inc(rg_done, 1)

            def score(c):
                if c:
                    pe.wait_ge(p_done, c)
                for h in range(H):
                    ins = pe.matmul(ps[:, 4, chk(h)], qkvo[:, H + h, chk(c)], qkvo[:, h, chk(c)], start=True, stop=True)
                ins.then_inc(scores, 1)

            def kv_turn(c):
                for n, bank, freed in ((1, 2, d_done), (2, 3, qg_done)):
                    pe.wait_ge(freed, c + 1)
                    for h in range(H):
                        ins = pe.transpose(ps[:, bank, chk(h)], qkvo[:, n * H + h, chk(c)], ident[:])
                    ins.then_inc(kv_turned, 1)

            nv = ps[:, 6:8, 0:2 * (P + 1)].rearrange("p a (h v) -> p a h v", v=P + 1)

            def numerator(c):
                pe.wait_ge(p_done, c + 1)
                pe.wait_ge(qg_done, c + 1)
                pe.wait_ge(kv_tok, 2 * c + 2)
                if c:
                    pe.wait_ge(c_done, c)
                for h in range(H):
                    pe.matmul(nv[:, h // 2, h % 2, :], pt[:, h, :], v_tok[:, c % 2, h, :], start=True, stop=False)
                    ins = pe.matmul(nv[:, h // 2, h % 2, :], qg[:, h, :], C_st[:, h, :], start=False, stop=True)
                ins.then_inc(num_done, 1)

            def outer(c):
                pe.wait_ge(h_done, c + 1)
                pe.wait_ge(wv_done, c + 1)
                for h in range(H):
                    ins = pe.matmul(nv[:, h // 2, h % 2, :], k_tok[:, c % 2, h, :], wv[:, h, :], start=True, stop=True)
                ins.then_inc(kv_done, 1)

            def h_turn(c):
                pe.wait_ge(hs_done, c + 1)
                if c:
                    pe.wait_ge(mixed, c)
                else:
                    pe.wait_ge(s_head, 6)
                if c == 3:
                    pe.wait_ge(s_mixed, 1)
                if c == CH - 1:
                    pe.wait_ge(u_rows_done, 1)
                for h in range(H):
                    ins = pe.transpose(ps[:, 5, chk(h)], h_tok[:, h, :], ident[:])
                ins.then_inc(h_turned, 1)

            def unit_u(k):
                j, c = J_U + k // NB, k % NB
                pe.wait_ge(w_ready, j + 1)
                pe.wait_ge(unit_evac, UNITS_U + k - 1)
                unit(j % 2, (UNITS_U + k) % 2, c).then_inc(unit_done, 1)

            def unit_pool(q):
                g, c = GROUP_OF[q // NB], q % NB
                pe.wait_ge(w_ready, J_POOL + 1)
                if q < 2:
                    pe.wait_ge(unit_evac, UNITS_POOL - 1 + q)
                else:
                    pe.wait_ge(pmix_lo, q - 1)
                pe.wait_ge(p_lo, q // NB + 1)
                bank = ps[:, (UNITS_POOL + q) % 2, 0:BW]
                pe.matmul(bank, w_hi[:, 1, g, :], hn_hi[:, g, blk(c)], start=True, stop=False)
                pe.matmul(bank, w_hi[:, 1, g, :], hn_lo[:, g, blk(c)], start=False, stop=False)
                pe.matmul(bank, w_lo[:, 1, g, :], hn_hi[:, g, blk(c)], start=False, stop=True).then_inc(unit_done, 1)

            pe.wait_ge(row_dve, 10)
            pe.wait_ge(row_act, 8)
            pe.wait_ge(s_rows_done, 1)
            pe.wait_ge(buf_summed, G)
            rows_everywhere(0)
            score(0)
            pe.wait_ge(s_state, 6)
            pe.transpose(ps[0:R, 5, 0:P], inter[:], ident[:]).then_inc(inter_turned, 1)
            for c in range(CH):
                if c == 0:
                    unit_u(0)
                    unit_u(1)
                kv_turn(c)
                if 0 < c < 6:
                    unit_u(2 * c)
                if c == 7:
                    for q in (6, 7, 8):
                        unit_pool(q)
                if c:
                    h_turn(c - 1)
                numerator(c)
                if c + 1 < CH:
                    rows_everywhere(c + 1)
                    score(c + 1)
                if 0 < c < 6:
                    unit_u(2 * c + 1)
                if c == 6:
                    unit_pool(0)
                    unit_pool(1)
                if c == 7:
                    unit_pool(9)
                outer(c)
                if c == 6:
                    for q in (2, 3, 4, 5):
                        unit_pool(q)
                if c == 7:
                    unit_pool(10)
                    unit_pool(11)
                if c == 3:
                    pe.wait_ge(mixed, c)
                    pe.wait_ge(s_head, 9)
                    pe.transpose(ps[:, 5, 0:R], h_s[:], ident[0:R, 0:R]).then_inc(hs_turned, 1)
                if c == CH - 1:
                    pe.wait_ge(mixed, c)
                    pe.wait_ge(u_saved, G)
                    for g in range(G):
                        ins = pe.transpose(ps[0:BUF + S, 5, chk(g)], u_last[:, g, :], ident[:])
                    ins.then_inc(u_rows_turned, 1)
            h_turn(CH - 1)
            pe.wait_ge(c_done, CH)
            pe.wait_ge(kv_tok, 2 * CH)
            for h in range(H):
                pe.transpose(ps[:, 2, chk(h)], C_st[:, h, 0:P], ident[:])
            pe.transpose(ps[0:H, 3, 0:P], C_st[:, :, P], ident[:]).then_inc(C_turned, 1)

            def out_tile(m, slot, start, first):
                pe.wait_ge(w_ready, m + J_OUT + 1)
                for c in range(NB):
                    if first and c < 2:
                        pe.wait_ge(pmix_lo, NB * G - 1 + c)
                    else:
                        pe.wait_ge(resid, m * NB + (c - 1))
                    if first:
                        pe.wait_ge(hmix_lo, c + 1)
                    unit(slot, (start + c) % 2, c).then_inc(unit_done, 1)

            out_tile(0, 0, UNITS_OUT, True)
            out_tile(1, 1, UNITS_OUT + NB, False)
            with pe.Fori(1, KT // 2) as i:
                out_tile(i * 2, 0, UNITS_OUT, False)
                out_tile(i * 2 + 1, 1, UNITS_OUT + NB, False)

            def gate_up(base, tile, first=False):
                for a in range(2):
                    pe.wait_ge(gu_ready, tile * 2 + (a + 1))
                    for c in range(NB):
                        e = NB * a + c
                        if first and a == 0:
                            pe.wait_ge(hn_lo_dve, 4 * NB + KT * (c + 1))
                        if first and e < 2:
                            pe.wait_ge(resid, NB * (KT - 1) + 2 + e)
                        else:
                            pe.wait_ge(act_up, base + (e - 1))
                        for g in range(2):
                            if first and 1 <= 2 * e + g <= NB:
                                norm_sum(2 * e + g - 1)
                            ins = product(ps[:, 2 * g + gate_bank(e), 0:BW], lambda k: guw[:, a, g, 0, k, :],
                                          lambda k: guw[:, a, g, 1, k, :], lambda k: hn_hi[:, k, blk(c)],
                                          lambda k: hn_lo[:, k, blk(c)], range(KT))
                        ins.then_inc(gu_done, 1)

            dw = [w[:].rearrange("p a k c -> p a (k c)") for w in (w_hi, w_lo)]

            def down(it, base, units, half, first=False):
                pe.wait_ge(dw_ready, it + 1)
                for c in range(NB):
                    pe.wait_ge(hid_lo, units + (NB + c + 1))
                    for n in range(KT):
                        q = c * KT + n
                        if not (first and q < 4):
                            pe.wait_ge(x_acc, base + (q - 3))
                        product(ps[:, 4 + q % 4, 0:BW], lambda k: dw[0][:, k, chk(n)], lambda k: dw[1][:, k, chk(n)],
                                lambda k: hid[:, 2 * half + k, 0, blk(c)], lambda k: hid[:, 2 * half + k, 1, blk(c)],
                                range(2)).then_inc(down_done, 1)

            def down_last(it):
                base = 24 * it
                pe.wait_ge(dw_ready, it + 1)
                pe.wait_ge(hid_lo, 6 * (it + 1))
                for c, (t0, t1) in enumerate(LAST_PARTS):
                    for n in range(KT):
                        q = c * KT + n
                        pe.wait_ge(x_acc, base + (q - 3))
                        product(ps[:, 4 + q % 4, 0:t1 - t0], lambda k: dw_last[:, 0, k, chk(n)],
                                lambda k: dw_last[:, 1, k, chk(n)], lambda k: hid[:, k, 0, t0:t1],
                                lambda k: hid[:, k, 1, t0:t1], range(2)).then_inc(down_done, 1)
                        if q in FINAL_TURN:
                            y_turn(FINAL_TURN[q], base)

            def y_turn(tt, base):
                r = rows_of(tt)
                need = next(c for c, part in enumerate(LAST_PARTS) if tt * P < part[1])
                pe.wait_ge(x_acc, base + KT * (need + 1))
                if tt >= 2:
                    pe.wait_ge(y_done, tt - 1)
                for k in range(KT):
                    ins = pe.transpose(ps[0:r, 2 * (tt % 2) + k // 4, (k % 4) * P:(k % 4 + 1) * P],
                                       xT[:, k, tt * P:tt * P + r], ident[:])
                ins.then_inc(y_turned, 1)

            gate_up(0, 0, first=True)
            gate_up(6, 1)
            down(0, 0, 0, 0, first=True)
            gate_up(12, 2)
            down(1, 24, 6, 1)
            with pe.Fori(1, FT // 4) as i:
                gate_up(i * 12 + 6, i * 2 + 1)
                down(i * 2, i * 48, i * 12, 0)
                gate_up(i * 12 + 12, i * 2 + 2)
                down(i * 2 + 1, i * 48 + 24, i * 12 + 6, 1)
            last = FT // 2 - 1
            down_last(last)
            for tt in range(len(FINAL_TURN), N_TOK):
                y_turn(tt, 24 * last)


_INS = ['x_prompt', 'x_sample', 'state_mlstm_C', 'state_mlstm_n', 'state_mlstm_m', 'state_pool_buf', 'g_mix', 'w_in',
        'b_gate', 'g_head', 'w_pool', 'pool_scale', 'w_out', 'g_ffn', 'w_gate', 'w_up', 'w_down', 'g_final']
_OUTS = [(1, 1024, 1024), (8, 1, 1024), (1, 1, 4, 128, 128), (1, 1, 4, 128), (1, 1, 4), (1, 1, 15, 512),
         (1, 8, 4, 128, 128), (1, 8, 4, 128), (1, 8, 4), (1, 8, 15, 512)]


def kernel(**inputs):
    import numpy as _np
    import concourse.bacc as _bacc
    from concourse import mybir as _mybir
    from concourse.bass_utils import run_bass_kernel_spmd as _run

    nc = _bacc.Bacc("TRN2", target_bir_lowering=False, num_devices=1)
    arrays, args = {}, []
    for name in _INS:
        a = _np.ascontiguousarray(inputs[name])
        arrays[f"in_{name}"] = a
        args.append(nc.dram_tensor(f"in_{name}", a.shape, _mybir.dt.from_np(a.dtype), kind="ExternalInput").ap())
    for i, shape in enumerate(_OUTS):
        args.append(nc.dram_tensor(f"out_{i}", shape, _mybir.dt.float32, kind="ExternalOutput").ap())
    trunk_kernel(nc, *args)
    r = _run(nc, [arrays], core_ids=[0])
    return tuple(r.results[0][f"out_{i}"] for i in range(len(_OUTS)))
```

```python
from contextlib import ExitStack

import concourse.bass as bass
from concourse import mybir

F32 = mybir.dt.float32
F32R = mybir.dt.float32r
ACT = mybir.ActivationFunctionType
ALU = mybir.AluOpType
AX = mybir.AxisListType


def trunk_kernel(nc, x_prompt, x_sample, state_C, state_n, state_m, state_buf, g_mix, w_in, b_gate, g_head,
                 w_pool, pool_scale, w_out, g_ffn, w_gate, w_up, w_down, g_final,
                 y_prompt, y_sample, C_prompt, n_prompt, m_prompt, buf_prompt,
                 C_sample, n_sample, m_sample, buf_sample):
    P = 128
    T, D = x_prompt.shape[1:]
    S = x_sample.shape[0]
    N = T + S
    KT = D // P
    H = state_n.shape[2]
    W = H * P
    G = w_pool.shape[1]
    BUF = state_buf.shape[2]
    WINDOWS = (2, 4, 8, 16)
    FT = w_gate.shape[2] // P
    NB = 3
    BW = N // NB
    CH = T // P
    R = S * H
    EPS = 1e-6
    NEG = -1e30
    KSCALE = float(P) ** -0.5
    assert N == NB * BW and BW <= 512 and D == 2 * W and G == H == 4 and FT % 2 == 0

    def blk(c):
        return slice(c * BW, (c + 1) * BW)

    def chk(c):
        return slice(c * P, (c + 1) * P)

    at = [nc.sbuf_base + (-nc.sbuf_base) % 32]

    def fixed(name, shape, dt=F32):
        size = 4
        for n in shape[1:]:
            size *= n
        t = nc.alloc_sbuf_tensor_at(name, shape, dt, offset=at[0])
        at[0] += size + (-size) % 32
        return t

    w_hi = fixed("w_hi", [P, 2, KT, P], F32R)
    w_lo = fixed("w_lo", [P, 2, KT, P], F32R)
    w_raw = fixed("w_raw", [P, 2, KT, P])
    hn_hi = fixed("hn_hi", [P, KT, N], F32R)
    hn_lo = fixed("hn_lo", [P, KT, N], F32R)
    ident = fixed("ident", [P, P])
    ones = fixed("ones", [P, P])
    cap = fixed("cap", [P, P])
    gmix_c = fixed("gmix_c", [P, KT])
    gffn_c = fixed("gffn_c", [P, KT])
    ghead_c = fixed("ghead_c", [P, H])
    pscale_c = fixed("pscale_c", [P, G])
    eps_c = fixed("eps_c", [P, 1])
    sel = fixed("sel", [P, 2 * H], F32R)
    bgate = fixed("bgate", [P, 1])
    inv_count = fixed("inv_count", [P, 16])
    m0 = fixed("m0", [H, S])
    gate_raw = fixed("gate_raw", [P, KT, 2 * H])
    cols = fixed("cols", [P, 2, CH, H])
    m_before = fixed("m_before", [H, CH])
    sample_exp = fixed("sample_exp", [H, S, 3])
    sample_f = fixed("sample_f", [H, S])
    m_s = fixed("m_s", [H, S])
    scol = fixed("scol", [R, 3])
    u_last = fixed("u_last", [P, G, BUF + S])
    buf_sum = fixed("buf_sum", [P, G, S])
    small8 = fixed("small8", [P, S])
    gend = fixed("gend", [P, 2, H])
    per_head = fixed("per_head", [P, 6, H])
    den = per_head[:, 0, :]
    rden = per_head[:, 1, :]
    ssq_h = per_head[:, 2, :]
    ms_h = per_head[:, 3, :]
    rs_h = per_head[:, 4, :]
    half_c = per_head[:, 5, :]
    s_small = fixed("s_small", [R, 8])
    qkv_s = fixed("qkv_s", [P, 3, R])
    N_TOK = T // P + 1
    by_tok = fixed("by_tok", [P, 3, N_TOK])
    X = at[0]

    def placed(name, shape, off, dt=F32):
        return nc.alloc_sbuf_tensor_at(name, shape, dt, offset=X + off)

    ROW = N * 4
    xT = placed("xT", [P, KT, N], 0)
    x_tok = placed("x_tok", [P, 4, D], 8 * ROW)
    nt0 = placed("nt0", [P, KT, BW], 14 * ROW)
    hid = placed("hid", [P, 4, 2, N], 8 * ROW, F32R)
    out_sq = placed("out_sq", [P, NB, BW], 12 * ROW)
    ssq = placed("ssq", [P, NB, BW], 12 * ROW + KT * BW * 4)
    guw = placed("guw", [P, 2, 2, 2, KT, P], 16 * ROW, F32R)
    at_nt1 = 16 * ROW + 32768
    nt1 = placed("nt1", [P, KT, BW], at_nt1)
    dw_raw = placed("dw_raw", [P, 2, D], at_nt1)
    rstd_x = placed("rstd_x", [P, N], at_nt1 + KT * BW * 4)
    sq_junk = placed("sq_junk", [P, D], at_nt1 + KT * BW * 4 + N * 4)
    rstd = placed("rstd", [P, NB, BW], at_nt1 + 2 * D * 4)
    hf = placed("hf", [P, 4, BW], at_nt1 + (KT + 2) * BW * 4)
    nts = (nt0, nt1)
    C_fin = placed("C_fin", [P, H, P], at_nt1 + (KT + 2) * BW * 4)
    n_fin = placed("n_fin", [H, P], at_nt1 + (KT + 2) * BW * 4 + H * P * 4)
    y_tok = placed("y_tok", [P, 4, D], 12 * ROW)
    gfin = placed("gfin", [P, D], at_nt1)
    gi = placed("gi", [H, N], 12 * ROW)
    gf = placed("gf", [H, N], 13 * ROW)
    ab = placed("ab", [H, N], 8 * ROW)
    sel_f = placed("sel_f", [P, 2 * H], 12 * ROW - 64)
    keep = placed("keep", [H, T], 17 * ROW)
    b_row = placed("b_row", [H, T], 18 * ROW)
    m_row = placed("m_row", [H, T], 19 * ROW)
    r_row = placed("r_row", [H, T], 20 * ROW)
    g_row = placed("g_row", [H, T], 21 * ROW)
    g_hi = placed("g_hi", [H, T], 13 * ROW, F32R)
    gi_lo = placed("gi_lo", [H, N], 20 * ROW)
    gf_lo = placed("gf_lo", [H, N], 21 * ROW)
    gates_w = placed("gates_w", [P, KT, 96 + H], 22 * ROW, F32R)
    buf_rows = placed("buf_rows", [S * BUF, W], 23 * ROW)
    qkvo = placed("qkvo", [P, 4 * H, N], 0)
    PADT = BUF + N
    u = placed("u", [P, G, PADT], 16 * ROW)
    at_m = 16 * ROW + G * PADT * 4
    at_m += (-at_m) % 32
    step = [at_m]

    def temp(name, shape, dt=F32):
        size = 4
        for n in shape[1:]:
            size *= n
        t = placed(name, shape, step[0], dt)
        step[0] += size + (-size) % 32
        return t

    wt = temp("wt", [P, 2, H, P])
    pt = temp("pt", [P, H, P])
    qg = temp("qg", [P, H, P])
    k_tok = temp("k_tok", [P, 2, H, P])
    v_tok = temp("v_tok", [P, 2, H, P + 1])
    wv = temp("wv", [P, H, P + 1])
    C_st = temp("C_st", [P, H, P + 1])
    h_tok = temp("h_tok", [P, H, P])
    junk = temp("junk", [P, H, P])
    C_s = placed("C_s", [P, R, P], 16 * ROW)
    bc_s = placed("bc_s", [P, R // 2, 2 * P + 1], 16 * ROW + R * P * 4)
    tmp_s = placed("tmp_s", [P, R // 2, P], 16 * ROW + R * P * 4 + (R // 2) * (2 * P + 1) * 4)
    step[0] = max(step[0], 16 * ROW + R * P * 4 + (R // 2) * (3 * P + 1) * 4)
    step[0] += (-step[0]) % 32
    win = placed("win", [P, 2, BW + 16], step[0])
    s_rows = temp("s_rows", [R, 3, P])
    s_pack = temp("s_pack", [R, 2 * P + 1])
    n_s = temp("n_s", [R, P])
    n_new = temp("n_new", [R, P])
    u_rows = temp("u_rows", [BUF + S, W])
    h_s = temp("h_s", [R, P])
    inter = temp("inter", [P, R])
    tmp_rows = temp("tmp_rows", [R, P])
    rr = placed("rr", [P, T], step[0], F32R)
    assert X + step[0] + T * 4 <= nc.sbuf_top and at_nt1 + (KT + 6) * BW * 4 + X <= nc.sbuf_top
    assert KT * BW * 4 + N * 4 + D * 4 <= (KT + 6) * BW * 4

    x_spill = nc.dram_tensor("x_spill", [P, KT, N], F32)
    gates_d = nc.dram_tensor("gates_d", [R, 3], F32)
    pack_d = nc.dram_tensor("pack_d", [R, 2 * P + 1], F32)

    with ExitStack() as ctx:
        def sem(name):
            return ctx.enter_context(nc.semaphore(name))

        ps = ctx.enter_context(nc.psum_tensor("ps", [P, 8, 512], F32))
        PA = (ps[:, 0, :], ps[:, 1, :])

        x_loaded = [sem(f"x_loaded{i}") for i in range(4)]
        vecs_loaded = sem("vecs_loaded")
        gate_w_loaded = sem("gate_w_loaded")
        consts = sem("consts")
        x_turned = sem("x_turned")
        xt_act = sem("xt_act")
        xt_dve = sem("xt_dve")
        x_spilled = [sem(f"x_spilled{i}") for i in range(NB)]
        x_back = sem("x_back")
        x_squared = sem("x_squared")
        x_std = sem("x_std")
        x_rstd = sem("x_rstd")
        rstd_spread = sem("rstd_spread")
        rstd_copied = sem("rstd_copied")
        norm_total = sem("norm_total")
        norm_std = sem("norm_std")
        norm_rstd = sem("norm_rstd")
        normed = sem("normed")
        hn_hi_done = sem("hn_hi_done")
        hn_lo_pool = sem("hn_lo_pool")
        hn_lo_dve = sem("hn_lo_dve")
        raw_loaded = [sem(f"raw_loaded{i}") for i in range(2)]
        w_zeroed = sem("w_zeroed")
        w_hi_done = sem("w_hi_done")
        w_ready = sem("w_ready")
        unit_done = sem("unit_done")
        unit_evac = sem("unit_evac")
        gates_sum = sem("gates_sum")
        row_act = sem("row_act")
        row_dve = sem("row_dve")
        row_pool = sem("row_pool")
        cols_turned = sem("cols_turned")
        cols_done = sem("cols_done")
        buf_loaded = sem("buf_loaded")
        buf_turned = sem("buf_turned")
        buf_summed = sem("buf_summed")
        sg_dve = sem("sg_dve")
        sg_act = sem("sg_act")
        gates_sent = sem("gates_sent")
        scol_loaded = sem("scol_loaded")
        n_loaded = sem("n_loaded")
        s_gathered = sem("s_gathered")
        s_turned = sem("s_turned")
        s_rows_done = sem("s_rows_done")
        s_packed = sem("s_packed")
        pack_sent = sem("pack_sent")
        C_loaded = [sem(f"C_loaded{i}") for i in range(2)]
        bc_loaded = [sem(f"bc_loaded{i}") for i in range(2)]
        s_state = sem("s_state")
        s_scaled = sem("s_scaled")
        C_stored = sem("C_stored")
        inter_turned = sem("inter_turned")
        s_den = sem("s_den")
        s_head = sem("s_head")
        s_pow = sem("s_pow")
        hs_turned = sem("hs_turned")
        s_mixed = sem("s_mixed")
        o_scaled = sem("o_scaled")
        m_init = sem("m_init")
        rg_done = sem("rg_done")
        scores = sem("scores")
        d_done = sem("d_done")
        w_exp = sem("w_exp")
        gend_done = sem("gend_done")
        qg_done = sem("qg_done")
        p_done = sem("p_done")
        kv_turned = sem("kv_turned")
        kv_tok = sem("kv_tok")
        wv_done = sem("wv_done")
        num_done = sem("num_done")
        den_step = sem("den_step")
        h_done = sem("h_done")
        h_squared = sem("h_squared")
        rs_step = sem("rs_step")
        hs_done = sem("hs_done")
        h_turned = sem("h_turned")
        mixed = sem("mixed")
        kv_done = sem("kv_done")
        c_done = sem("c_done")
        C_turned = sem("C_turned")
        C_out = sem("C_out")
        win_step = sem("win_step")
        win_done = sem("win_done")
        u_saved = sem("u_saved")
        p_step = sem("p_step")
        pooled = sem("pooled")
        p_hi = sem("p_hi")
        p_lo_pool = sem("p_lo_pool")
        p_lo_dve = sem("p_lo_dve")
        pmix_hi = sem("pmix_hi")
        pmix_lo = sem("pmix_lo")
        u_rows_turned = sem("u_rows_turned")
        u_rows_done = sem("u_rows_done")
        hmix_hi = sem("hmix_hi")
        hmix_lo = sem("hmix_lo")
        hmix_lo_last = sem("hmix_lo_last")
        resid = sem("resid")
        resid_sq = sem("resid_sq")
        resid_sum = sem("resid_sum")
        rows_stored = sem("rows_stored")
        C_fin_stored = sem("C_fin_stored")
        gu_loaded = sem("gu_loaded")
        gu_hi = sem("gu_hi")
        gu_ready = sem("gu_ready")
        gu_done = sem("gu_done")
        sig_done = sem("sig_done")
        gate_scaled = sem("gate_scaled")
        act_gate = sem("act_gate")
        act_up = sem("act_up")
        hid_f = sem("hid_f")
        hid_hi = sem("hid_hi")
        hid_lo = sem("hid_lo")
        dw_loaded = sem("dw_loaded")
        dw_hi = sem("dw_hi")
        dw_ready = sem("dw_ready")
        down_done = sem("down_done")
        x_acc = sem("x_acc")
        gfin_loaded = sem("gfin_loaded")
        y_turned = sem("y_turned")
        y_ss = sem("y_ss")
        y_std = sem("y_std")
        y_rstd = sem("y_rstd")
        y_done = sem("y_done")
        y_stored = [sem(f"y_stored{i}") for i in range(4)]
        stored = sem("stored")

        J_Q, J_U = 1, 1 + 4 * H
        J_POOL = J_U + G
        J_OUT = J_POOL + 1
        UNITS_U = NB * J_U
        UNITS_POOL = NB * J_POOL
        UNITS_OUT = UNITS_POOL + NB * G
        assert J_U % 2 == 1 and J_OUT % 2 == 0 and UNITS_POOL == 63
        GROUP_OF = tuple(reversed(range(G)))
        POOL_BANK = (1, 0, 1, 0, 1, 0, 1, 0, 4, 1, 0, 4)
        POOL_AT = {(1, 0): [(0, 2)], (1, 1): [(0, 1)], (2, 0): [(0, 0)],
                   (3, 0): [(1, 2)], (3, 1): [(1, 1)], (4, 0): [(1, 0)],
                   (4, 1): [(2, 2)], (5, 2): [(2, 1)], (5, 0): [(2, 0)]}
        TILES_OF = (3, 6, 9)
        NSTORES = [0]

        def rows_of(tt):
            return P if tt < T // P else S

        block = ctx.enter_context(nc.Block())

        dw_last = guw[:, 0].rearrange("p g s k c -> p (g s k c)").rearrange("p (s a n) -> p s a n", s=2, a=2)

        DOWN_AFTER = ((0, 0), (0, 5), (5, 10), (10, 15), (15, 20), (20, 24))
        DOWN_AFTER_LAST = ((0, 0), (0, 4), (4, 8), (8, 12), (12, 16), (16, 24))

        LAST_PARTS = ((0, 4 * P), (4 * P, 6 * P), (6 * P, N))
        Y_BANKS = (0, 2, 0, 2, 0, 2, 4, 6, 0)
        FINAL_TURN = {10: 0, 12: 1, 14: 2, 16: 3, 18: 4, 21: 5}
        FINAL_AFTER = {11: 0, 13: 1, 15: 2, 17: 3, 20: 4, 23: 5}

        def gate_bank(e):
            return (e + 1) % 2

        @block.sync
        def _(sp):
            win_src = w_in[0].rearrange("(k p) n -> p k n", p=P)
            wout_src = w_out[0].rearrange("(k p) n -> p k n", p=P)

            def load_x(tt):
                if tt >= 4:
                    sp.wait_ge(x_turned, 2 * (tt - 3))
                    sp.wait_ge(x_squared, tt - 3)
                src = x_prompt[0, chk(tt), :] if tt < T // P else x_sample[:, 0, :]
                sp.dma_start(x_tok[0:rows_of(tt), tt % 4, :], src).then_inc(x_loaded[tt % 4], 16)

            def vec(dst, src):
                sp.dma_start(dst, src).then_inc(vecs_loaded, 16)

            def out(dst, src):
                NSTORES[0] += 1
                sp.dma_start(dst, src).then_inc(stored, 16)

            load_x(0)
            load_x(1)
            load_x(2)
            with nc.allow_non_contiguous_dma(reason="small vectors"):
                vec(gmix_c[:], g_mix[0].rearrange("(k p) -> p k", p=P))
                vec(gffn_c[:], g_ffn[0].rearrange("(k p) -> p k", p=P))
                vec(ghead_c[:], g_head[0].rearrange("(k p) -> p k", p=P))
                vec(pscale_c[:], pool_scale[0].rearrange("(k p) -> p k", p=P))
                vec(bgate[0:H, :], b_gate[0, 0:H].rearrange("(h a) -> h a", a=1))
                vec(bgate[32:32 + H, :], b_gate[0, H:2 * H].rearrange("(h a) -> h a", a=1))
                vec(m0[:], state_m[0].rearrange("b h -> h b"))
            load_x(3)
            sp.dma_start(gate_raw[:], win_src[:, :, 4 * W:4 * W + 2 * H]).then_inc(gate_w_loaded, 16)
            sp.dma_start(w_raw[:, 1], win_src[:, :, 0:P]).then_inc(raw_loaded[1], 16)
            load_x(4)
            sp.dma_start(w_raw[:, 0], win_src[:, :, P:2 * P]).then_inc(raw_loaded[0], 16)
            for tt in range(5, N_TOK):
                load_x(tt)
            sp.dma_start(buf_rows[:], state_buf[0].rearrange("b j w -> (b j) w")).then_inc(buf_loaded, 16)
            for c in range(NB):
                sp.wait_ge(xt_act, TILES_OF[c])
                sp.wait_ge(xt_dve, TILES_OF[c])
                sp.dma_start(x_spill[:, :, blk(c)], xT[:, :, blk(c)]).then_inc(x_spilled[c], 16)

            def load_tiles(first, last):
                with sp.Fori(first, last) as i:
                    sp.wait_ge(w_ready, i * 2 + 2)
                    sp.dma_start(w_raw[:, 1], win_src[:, :, bass.ds(i * (2 * P) + 2 * P, P)])\
                      .then_inc(raw_loaded[1], 16)
                    sp.wait_ge(w_ready, i * 2 + 3)
                    sp.dma_start(w_raw[:, 0], win_src[:, :, bass.ds(i * (2 * P) + 3 * P, P)])\
                      .then_inc(raw_loaded[0], 16)

            load_tiles(0, 4)
            sp.wait_ge(sg_act, 1)
            sp.dma_start(gates_d[:].rearrange("(h b) q -> h (b q)", h=H), sample_exp[:].rearrange("h b q -> h (b q)"))\
              .then_inc(gates_sent, 16)
            sp.wait_ge(gates_sent, 16)
            sp.dma_start(scol[:], gates_d[:]).then_inc(scol_loaded, 16)
            sp.wait_ge(cols_done, 1)
            sp.wait_ge(row_act, 8)
            sp.wait_ge(buf_summed, G)
            for h in range(H):
                sp.dma_start(n_s[h * S:(h + 1) * S, :], state_n[0, :, h, :]).then_inc(n_loaded, 16)
            for part in range(2):
                for h in range(2 * part, 2 * part + 2):
                    sp.dma_start(C_s[:, h * S:(h + 1) * S, :], state_C[0, :, h].rearrange("b v k -> v b k"))\
                      .then_inc(C_loaded[part], 16)
            load_tiles(4, 6)
            sp.wait_ge(s_packed, 4)
            sp.dma_start(pack_d[:], s_pack[:]).then_inc(pack_sent, 16)
            sp.wait_ge(pack_sent, 16)
            sp.dma_start(bc_s[:], pack_d[0:R // 2, :].partition_broadcast(P)).then_inc(bc_loaded[0], 16)
            load_tiles(6, 7)
            sp.wait_ge(s_state, 3)
            sp.wait_ge(s_scaled, 1)
            sp.dma_start(bc_s[:], pack_d[R // 2:R, :].partition_broadcast(P)).then_inc(bc_loaded[1], 16)

            def load_u(j):
                sp.wait_ge(w_ready, j - 1)
                col = 4 * W + 2 * H + GROUP_OF[j - J_U] * P
                sp.dma_start(w_raw[:, j % 2], win_src[:, :, col:col + P]).then_inc(raw_loaded[j % 2], 16)

            load_u(J_U)
            for half_ in range(2):
                sp.wait_ge(s_state, 4 * (half_ + 1))
                for h in range(2 * half_, 2 * half_ + 2):
                    sp.dma_start(C_sample[0, :, h].rearrange("b v k -> v b k"), C_s[:, h * S:(h + 1) * S, :])\
                      .then_inc(C_stored, 16)
            load_u(J_U + 1)
            with nc.allow_non_contiguous_dma(reason="a few words"):
                out(m_sample[0].rearrange("b h -> h b"), m_s[:])
                out(m_prompt[0, 0].rearrange("(h a) -> h a", a=1), m_before[:, 0:1])
            for h in range(H):
                sp.dma_start(n_sample[0, :, h, :], n_new[h * S:(h + 1) * S, :]).then_inc(rows_stored, 16)
            out(buf_sample[0, :, 0:BUF - 1, :], state_buf[0, :, 1:BUF, :])
            load_u(J_U + 2)
            load_u(J_U + 3)
            sp.wait_ge(w_ready, J_POOL - 1)
            sp.dma_start(w_raw[:, 1, 0:G, :], w_pool[0].rearrange("g c d -> c g d")).then_inc(raw_loaded[1], 16)
            sp.wait_ge(w_ready, J_POOL)
            sp.dma_start(w_raw[:, 0], wout_src[:, :, 0:P]).then_inc(raw_loaded[0], 16)
            sp.wait_ge(w_ready, J_POOL + 1)
            sp.dma_start(w_raw[:, 1], wout_src[:, :, P:2 * P]).then_inc(raw_loaded[1], 16)
            sp.wait_ge(scores, CH)
            sp.wait_ge(kv_turned, 2 * CH)
            sp.wait_ge(qg_done, CH)
            for c in range(NB):
                sp.dma_start(xT[:, :, blk(c)], x_spill[:, :, blk(c)]).then_inc(x_back, 16)
            sp.wait_ge(u_rows_done, 1)
            sp.dma_start(buf_prompt[0, 0], u_rows[0:BUF, :]).then_inc(rows_stored, 16)
            sp.dma_start(buf_sample[0, :, BUF - 1, :], u_rows[BUF:BUF + S, :]).then_inc(rows_stored, 16)

            with sp.Fori(0, KT // 2 - 1) as i:
                sp.wait_ge(w_ready, i * 2 + J_OUT + 1)
                sp.dma_start(w_raw[:, 0], wout_src[:, :, bass.ds(i * (2 * P) + 2 * P, P)]).then_inc(raw_loaded[0], 16)
                sp.wait_ge(w_ready, i * 2 + J_OUT + 2)
                sp.dma_start(w_raw[:, 1], wout_src[:, :, bass.ds(i * (2 * P) + 3 * P, P)]).then_inc(raw_loaded[1], 16)
            sp.wait_ge(C_out, 2)
            sp.dma_start(C_prompt[0, 0].rearrange("h v k -> v h k"), C_fin[:]).then_inc(C_fin_stored, 16)
            sp.dma_start(n_prompt[0, 0], n_fin[:]).then_inc(C_fin_stored, 16)

            gate_src = w_gate[0].rearrange("(k p) n -> p k n", p=P)
            up_src = w_up[0].rearrange("(k p) n -> p k n", p=P)
            down_src = w_down[0].rearrange("(i a p) n -> i p a n", p=P, a=2)

            def load_gu(col, ready):
                sp.wait_ge(gu_ready, ready)
                sp.dma_start(w_raw[:, 0], gate_src[:, :, col]).then_inc(gu_loaded, 16)
                sp.dma_start(w_raw[:, 1], up_src[:, :, col]).then_inc(gu_loaded, 16)

            sp.wait_ge(w_ready, J_OUT + KT)
            sp.dma_start(w_raw[:, 0], gate_src[:, :, 0:P]).then_inc(gu_loaded, 16)
            sp.dma_start(w_raw[:, 1], up_src[:, :, 0:P]).then_inc(gu_loaded, 16)
            load_gu(slice(P, 2 * P), 1)
            sp.dma_start(dw_raw[:], down_src[0]).then_inc(dw_loaded, 16)
            with sp.Fori(0, FT // 2 - 1) as i:
                load_gu(bass.ds(i * (2 * P) + 2 * P, P), i * 2 + 2)
                load_gu(bass.ds(i * (2 * P) + 3 * P, P), i * 2 + 3)
                sp.wait_ge(dw_ready, i + 1)
                sp.dma_start(dw_raw[:], down_src[bass.ds(i + 1, 1)].rearrange("i p a n -> (i p) a n"))\
                  .then_inc(dw_loaded, 16)

            sp.wait_ge(dw_ready, FT // 2)
            sp.dma_start(gfin[:], g_final.partition_broadcast(P)).then_inc(gfin_loaded, 16)
            for tt in range(N_TOK):
                sp.wait_ge(y_done, tt + 1)
                dst = y_prompt[0, chk(tt), :] if tt < T // P else y_sample[:, 0, :]
                sp.dma_start(dst, y_tok[0:rows_of(tt), tt % 4, :]).then_inc(y_stored[tt % 4], 16)
            for q in range(4):
                sp.wait_ge(y_stored[q], 16 * len(range(q, N_TOK, 4)))
            sp.wait_ge(C_stored, 16 * H)
            for c in range(NB):
                sp.wait_ge(x_spilled[c], 16)
            sp.wait_ge(rows_stored, 16 * (H + 2))
            sp.wait_ge(C_fin_stored, 32)
            sp.wait_ge(stored, 16 * NSTORES[0])

        @block.gpsimd
        def _(pool):
            pool.memset(ident[:], 0.0).then_inc(consts, 1)
            pool.memset(ones[:], 1.0).then_inc(consts, 1)
            pool.memset(eps_c[:], EPS).then_inc(consts, 1)
            pool.memset(gates_w[:].bitcast(F32), 0.0).then_inc(w_zeroed, 1)
            pool.wait_ge(consts, 1)
            pool.affine_select(out=ident[:], in_=ident[:], compare_op=ALU.not_equal, fill=1.0, base=0,
                               pattern=[[-1, P]], channel_multiplier=1).then_inc(consts, 1)
            pool.memset(cap[:], 0.0).then_inc(row_pool, 1)
            pool.memset(sel_f[:], 0.0).then_inc(row_pool, 1)
            pool.memset(half_c[:], -0.5).then_inc(row_pool, 1)
            pool.memset(keep[:], 1.0).then_inc(row_pool, 1)
            pool.memset(m_before[:], 0.0).then_inc(row_pool, 1)
            pool.iota(inv_count[:], pattern=[[1, 16]], base=1, channel_multiplier=0,
                      allow_small_or_imprecise_dtypes=True).then_inc(row_pool, 1)
            pool.wait_ge(row_pool, 4)
            pool.affine_select(out=cap[:], in_=cap[:], compare_op=ALU.is_ge, fill=NEG, base=0,
                               pattern=[[1, P]], channel_multiplier=-1).then_inc(row_pool, 1)
            pool.memset(keep[:].rearrange("h (c t) -> h c t", t=P)[:, :, 0:1], 0.0).then_inc(row_pool, 1)
            for q in range(4):
                part = sel_f[:, H * (q // 2):H * (q // 2) + H]
                pool.wait_ge(row_pool, 8 + q)
                pool.affine_select(out=part, in_=part, compare_op=ALU.not_equal, fill=1.0, base=-32 * q,
                                   pattern=[[-1, H]], channel_multiplier=1).then_inc(row_pool, 1)
            pool.wait_ge(row_pool, 12)
            pool.tensor_copy(sel[:], sel_f[:]).then_inc(row_pool, 1)

            def lo_gates():
                pool.wait_ge(w_hi_done, 1)
                pool.tensor_tensor(gates_w[:, :, 64:64 + H], gate_raw[:, :, 0:H], gates_w[:, :, 0:H].bitcast(F32),
                                   ALU.subtract).then_inc(row_pool, 1)
                pool.wait_ge(row_pool, 14)
                pool.tensor_tensor(gates_w[:, :, 96:96 + H], gate_raw[:, :, H:2 * H],
                                   gates_w[:, :, 32:32 + H].bitcast(F32), ALU.subtract).then_inc(w_ready, 1)

            def lo(slot, need, n=KT):
                pool.wait_ge(w_hi_done, need)
                pool.tensor_tensor(w_lo[:, slot, 0:n], w_raw[:, slot, 0:n], w_hi[:, slot, 0:n].bitcast(F32),
                                   ALU.subtract).then_inc(w_ready, 1)

            def norm_lo(k):
                c = k % NB
                for n in range(0, KT, 2):
                    pool.wait_ge(hn_hi_done, KT * k + n + 1)
                    pool.tensor_tensor(hn_lo[:, n, blk(c)], nts[k % 2][:, n, :], hn_hi[:, n, blk(c)].bitcast(F32),
                                       ALU.subtract).then_inc(hn_lo_pool, 1)

            pool.wait_ge(w_zeroed, 1)
            lo_gates()
            lo(1, 2)
            norm_lo(0)
            lo(0, 3)
            norm_lo(1)
            norm_lo(2)
            pool.wait_ge(x_squared, N_TOK)
            pool.wait_ge(normed, NB * KT)
            pool.memset(rr[:].bitcast(F32), 0.0).then_inc(row_pool, 1)
            with pool.Fori(0, 2 * H - 2) as i:
                lo(1, i * 2 + 4)
                lo(0, i * 2 + 5)
            lo(1, 4 * H)

            def decay_state(half_):
                rs = slice(half_ * (R // 2), (half_ + 1) * (R // 2))
                pool.wait_ge(bc_loaded[half_], 16)
                pool.wait_ge(s_state, 4 * half_ + 1)
                pool.tensor_tensor(C_s[:, rs, :], C_s[:, rs, :],
                                   bc_s[:, :, 2 * P:2 * P + 1].to_broadcast([P, R // 2, P]), ALU.mult)\
                    .then_inc(s_scaled, 1)

            decay_state(0)
            lo(0, 4 * H + 1)
            decay_state(1)
            lo(1, 4 * H + 2)

            pool.wait_ge(s_state, 8)
            pool.wait_ge(C_stored, 16 * H)
            pool.memset(C_st[:], 0.0).then_inc(m_init, 1)
            pool.memset(v_tok[:, :, :, P:P + 1], 1.0).then_inc(m_init, 1)
            pool.memset(u[:, :, 0:BUF], 0.0).then_inc(m_init, 1)
            pool.wait_ge(s_head, 8)
            pool.tensor_scalar(s_small[:, 5:6], s_small[:, 4:5], 1.0 / P, EPS, ALU.mult, ALU.add).then_inc(s_pow, 1)
            pool.wait_ge(s_pow, 1)
            pool.tensor_tensor(s_small[:, 6:7], s_small[:, 5:6], half_c[0:R, 0:1], ALU.pow).then_inc(s_pow, 1)

            def weigh_v(c):
                pool.wait_ge(kv_tok, 2 * c + 2)
                pool.wait_ge(w_exp, c + 1)
                if c:
                    pool.wait_ge(kv_done, c)
                else:
                    pool.wait_ge(m_init, 3)
                wend = wt[:, c % 2, :, P - 1:P].to_broadcast([P, H, P + 1])
                pool.tensor_tensor(wv[:], v_tok[:, c % 2], wend, ALU.mult).then_inc(wv_done, 1)

            def head_rms(c):
                pool.wait_ge(h_squared, c + 1)
                if c:
                    pool.wait_ge(hs_done, c)
                pool.tensor_scalar(ms_h[:], ssq_h[:], 1.0 / P, EPS, ALU.mult, ALU.add).then_inc(rs_step, 1)
                pool.wait_ge(rs_step, 2 * c + 1)
                pool.tensor_tensor(rs_h[:], ms_h[:], half_c[:], ALU.pow).then_inc(rs_step, 1)

            wsteps = [0]

            def windows(n, c):
                g, q = GROUP_OF[n], NB * n + (NB - 1 - c)
                pool.wait_ge(unit_evac, UNITS_U + NB * n + NB)
                if q:
                    pool.wait_ge(pooled, q)
                t0, t1 = c * BW, min((c + 1) * BW, T)
                src, at_t0 = u[:, g, :], BUF + t0
                for d in range(g + 1):
                    k = 1 << d
                    need = WINDOWS[g] - 2 * k
                    n_col = t1 - t0 + need
                    a = at_t0 - need
                    if d:
                        pool.wait_ge(win_step, wsteps[0])
                    ins = pool.tensor_tensor(win[:, d % 2, 0:n_col], src[:, a:a + n_col], src[:, a - k:a - k + n_col],
                                             ALU.add)
                    if d < g:
                        ins.then_inc(win_step, 1)
                        wsteps[0] += 1
                    else:
                        ins.then_inc(win_done, 1)
                    src, at_t0 = win[:, d % 2, :], need

            def p_split_lo(n):
                k = H + GROUP_OF[n]
                pool.wait_ge(p_hi, n + 1)
                pool.tensor_tensor(hn_lo[:, k, :], u[:, GROUP_OF[n], BUF:BUF + N], hn_hi[:, k, :].bitcast(F32),
                                   ALU.subtract).then_inc(p_lo_pool, 1)

            def hmix_low(c):
                pool.wait_ge(hmix_hi, c + 1)
                pool.tensor_tensor(hn_lo[:, 0:H, blk(c)], qkvo[:, 3 * H:4 * H, blk(c)], hn_hi[:, 0:H, blk(c)].bitcast(F32),
                                   ALU.subtract).then_inc(hmix_lo, 1)

            def windows_at(c, place):
                for n, b in POOL_AT.get((c, place), ()):
                    windows(n, b)

            pool.wait_ge(s_head, 9)
            LO_AT = {0: J_U + 1, 1: J_U + 2, 3: J_U + 3, 4: J_POOL}
            for c in range(CH):
                def lo_at():
                    lo(LO_AT[c] % 2, LO_AT[c] + 1, G if LO_AT[c] == J_POOL else KT)

                if c in (0, 3):
                    lo_at()
                if c == CH - 1:
                    lo(0, J_OUT + 1)
                weigh_v(c)
                windows_at(c - 1, 1)
                if c == CH - 2:
                    p_split_lo(1)
                if c == CH - 1:
                    p_split_lo(2)
                head_rms(c)
                if c in (1, 4):
                    lo_at()
                windows_at(c, 2)
                windows_at(c, 0)
                if c == CH - 3:
                    p_split_lo(0)
            hmix_low(0)
            hmix_low(1)
            lo(1, J_OUT + 2)
            with pool.Fori(0, KT // 2 - 1) as i:
                lo(0, i * 2 + J_OUT + 3)
                lo(1, i * 2 + J_OUT + 4)

            def gu_lo(a, need):
                pool.wait_ge(gu_hi, need)
                pool.tensor_tensor(guw[:, a, :, 1], w_raw[:], guw[:, a, :, 0].bitcast(F32), ALU.subtract)\
                    .then_inc(gu_ready, 1)

            def down_lo(need):
                pool.wait_ge(dw_hi, need)
                pool.tensor_tensor(w_lo[:].rearrange("p a k c -> p a (k c)"), dw_raw[:],
                                   w_hi[:].rearrange("p a k c -> p a (k c)").bitcast(F32), ALU.subtract)\
                    .then_inc(dw_ready, 1)

            gu_lo(0, 1)
            gu_lo(1, 2)
            gu_lo(0, 3)
            with pool.Fori(1, FT // 2 - 1) as i:
                down_lo(i)
                gu_lo(1, i * 2 + 2)
                gu_lo(0, i * 2 + 3)
            down_lo(FT // 2 - 1)
            gu_lo(1, FT)
            pool.wait_ge(dw_hi, FT // 2)
            pool.tensor_tensor(dw_last[:, 1], dw_raw[:], dw_last[:, 0].bitcast(F32), ALU.subtract).then_inc(dw_ready, 1)

        @block.scalar
        def _(act):
            def turn_half(tt):
                r = rows_of(tt)
                act.wait_ge(x_turned, 2 * tt + 1)
                b = 2 + 2 * (tt % 2)
                act.activation(xT[:, 0:4, tt * P:tt * P + r],
                               ps[:, b, :].rearrange("p (k t) -> p k t", t=P)[:, :, 0:r], ACT.Copy).then_inc(xt_act, 1)

            def square(tt):
                r = rows_of(tt)
                act.wait_ge(x_loaded[tt % 4], 16 * (tt // 4 + 1))
                if tt:
                    act.wait_ge(x_squared, tt)
                act.activation(sq_junk[0:r, :], x_tok[0:r, tt % 4, :], ACT.Square, accum_out=by_tok[0:r, 0, tt:tt + 1])\
                   .then_inc(x_squared, 1)
                act.wait_ge(x_squared, tt + 1)
                if tt == 0:
                    act.wait_ge(consts, 4)
                act.activation(by_tok[0:r, 1, tt:tt + 1], by_tok[0:r, 0, tt:tt + 1], ACT.Sqrt, bias=eps_c[0:r, :],
                               scale=1.0 / D).then_inc(x_std, 1)

            def norm_root(c):
                act.wait_ge(norm_total, c + 1)
                act.activation(rstd[:, c, :], ps[:, 5 + c, 0:BW], ACT.Sqrt, bias=eps_c[:], scale=1.0 / D).then_inc(norm_std, 1)

            def scaled_hi(c):
                act.wait_ge(unit_done, UNITS_OUT + NB * (KT - 1) + c + 1)
                for n in range(KT):
                    act.wait_ge(resid, n * NB + c + 1)
                    act.activation(hn_hi[:, n, blk(c)], xT[:, n, blk(c)], ACT.Copy, scale=gffn_c[:, n:n + 1])\
                       .then_inc(hn_hi_done, 1)

            def norm_hi(k, first=0, last=KT):
                for n in range(first, last):
                    act.wait_ge(normed, KT * k + n + 1)
                    act.activation(hn_hi[:, n, blk(k % NB)], nts[k % 2][:, n, :], ACT.Copy).then_inc(hn_hi_done, 1)

            def hi(slot, loaded, free, n=KT):
                act.wait_ge(raw_loaded[slot], loaded)
                if free is not None:
                    act.wait_ge(unit_done, free)
                act.activation(w_hi[:, slot, 0:n], w_raw[:, slot, 0:n], ACT.Copy).then_inc(w_hi_done, 1)

            def evac(dst, n_units, func=ACT.Copy, scale=1.0):
                act.wait_ge(unit_done, n_units)
                act.activation(dst, ps[:, n_units_bank[0] % 2, 0:BW], func, scale=scale).then_inc(unit_evac, 1)
                n_units_bank[0] += 1

            n_units_bank = [0]

            def evac_gates(c):
                act.wait_ge(unit_done, NB * c + 1)
                act.activation(gi[:, blk(c)], PA[c % 2][0:H, 0:BW], ACT.Identity, bias=bgate[0:H, :])
                act.activation(gf[:, blk(c)], PA[c % 2][32:32 + H, 0:BW], ACT.Identity, bias=bgate[32:32 + H, :])
                act.activation(gi_lo[:, blk(c)], PA[c % 2][64:64 + H, 0:BW], ACT.Copy)
                act.activation(gf_lo[:, blk(c)], PA[c % 2][96:96 + H, 0:BW], ACT.Copy).then_inc(unit_evac, 1)
                n_units_bank[0] += 1

            def evac_q(c, tile):
                act.wait_ge(x_spilled[c], 16)
                evac(qkvo[:, tile - 1, blk(c)], NB * c + tile + 1)

            turn_half(0)
            square(0)
            turn_half(1)
            square(1)
            turn_half(2)
            square(2)
            act.wait_ge(gate_w_loaded, 16)
            act.wait_ge(w_zeroed, 1)
            act.activation(gates_w[:, :, 0:H], gate_raw[:, :, 0:H], ACT.Copy)
            act.activation(gates_w[:, :, 32:32 + H], gate_raw[:, :, H:2 * H], ACT.Copy).then_inc(w_hi_done, 1)
            hi(1, 16, None)
            norm_hi(0, 0, 4)
            turn_half(3)
            square(3)
            norm_hi(0, 4, KT)
            hi(0, 16, None)
            turn_half(4)
            square(4)
            turn_half(5)
            square(5)
            square(6)
            square(7)
            act.wait_ge(vecs_loaded, 16 * 7)
            evac_gates(0)
            norm_hi(1, 0, 4)
            turn_half(6)
            norm_hi(1, 4, KT)
            square(8)
            evac_q(0, 1)
            turn_half(7)
            evac_q(0, 2)
            turn_half(8)
            norm_hi(2)
            for c in (1, 2):
                evac_gates(c)
                if c == 1:
                    evac_q(c, 1)
                    evac_q(c, 2)

            evac_q(2, 1)
            hi(1, 32, 3 * NB - 1)
            act.wait_ge(gates_sum, 2)
            act.activation(ab[:], gf[:], ACT.Abs).then_inc(row_act, 1)
            act.wait_ge(row_act, 1)
            act.activation(ab[:], ab[:], ACT.Exp, scale=-1.0).then_inc(row_act, 1)
            evac_q(2, 2)
            act.wait_ge(row_act, 2)
            act.activation(ab[:], ab[:], ACT.Ln, bias=ones[0:H, 0:1]).then_inc(row_act, 1)

            def pair(i, tile, func, scale, between=()):
                for d in range(2):
                    slot = d
                    hi(slot, i * 16 + (16 if slot == 0 else 32), i * 6 + (NB * d + NB))
                    for c in range(NB):
                        dst = qkvo[:, bass.ds(tile + d, 1), blk(c)].rearrange("p a t -> p (a t)")
                        evac(dst, i * 6 + NB + NB * d + c + 1, func, scale)
                        if NB * d + c < len(between):
                            between[NB * d + c]()

            def split_r():
                act.wait_ge(row_pool, 15)
                act.wait_ge(row_dve, 6)
                act.activation(rr[0:H, :], r_row[:], ACT.Copy).then_inc(row_act, 1)

            def exp_g():
                act.wait_ge(row_dve, 8)
                act.activation(g_row[:], g_row[:], ACT.Exp).then_inc(row_act, 1)

            def exp_m():
                act.activation(ab[:, 0:T], m_row[:], ACT.Exp, scale=-1.0).then_inc(row_act, 1)

            def split_g():
                act.wait_ge(row_act, 5)
                act.activation(g_hi[:], g_row[:], ACT.Copy).then_inc(row_act, 1)
                act.wait_ge(row_act, 7)
                act.activation(rr[64:64 + H, :], g_hi[:].bitcast(F32), ACT.Copy).then_inc(row_act, 1)

            def exp_sample():
                act.wait_ge(sg_dve, 5)
                act.activation(sample_exp[:].rearrange("h b q -> h (b q)"),
                               sample_exp[:].rearrange("h b q -> h (b q)"), ACT.Exp).then_inc(sg_act, 1)

            pair(1, 2, ACT.Copy, 1.0)
            pair(2, 4, ACT.Copy, KSCALE, between=(split_r, exp_g, exp_m, split_g, exp_sample))
            pair(3, 6, ACT.Copy, KSCALE)
            for part, func in ((2, ACT.Copy), (3, ACT.Sigmoid)):
                with act.Fori(2 * part, 2 * part + 2) as i:
                    pair(i, i * 2, func, 1.0)

            def unit_u(k):
                j, c = J_U + k // NB, k % NB
                if c == 0:
                    nxt = j + 1
                    nth = nxt // 2 if nxt % 2 == 0 else (nxt + 1) // 2
                    hi(nxt % 2, 16 * nth, NB * (nxt - 1), G if nxt == J_POOL else KT)
                dst = u[:, GROUP_OF[j - J_U], BUF + c * BW:BUF + (c + 1) * BW]
                evac(dst, UNITS_U + k + 1)

            def exp_w(c):
                act.wait_ge(d_done, c + 1)
                act.activation(wt[:, c % 2], wt[:, c % 2], ACT.Exp).then_inc(w_exp, 1)

            def kv_by_token(c):
                act.wait_ge(kv_turned, 2 * c + 1)
                if c >= 2:
                    act.wait_ge(kv_done, c - 1)
                elif c == 0:
                    act.wait_ge(m_init, 3)
                act.activation(k_tok[:, c % 2], ps[:, 2, :].rearrange("p (h t) -> p h t", h=H), ACT.Copy)\
                   .then_inc(kv_tok, 1)
                act.wait_ge(kv_turned, 2 * c + 2)
                act.activation(v_tok[:, c % 2, :, 0:P], ps[:, 3, :].rearrange("p (h t) -> p h t", h=H), ACT.Copy)\
                   .then_inc(kv_tok, 1)

            def square_h(c):
                act.wait_ge(h_done, c + 1)
                if c:
                    act.wait_ge(rs_step, 2 * c)
                for h in range(H):
                    ins = act.activation(junk[:, h, :], h_tok[:, h, :], ACT.Square, accum_out=ssq_h[:, h:h + 1])
                ins.then_inc(h_squared, 1)

            def p_split_hi(n):
                g = GROUP_OF[n]
                if n == 0:
                    act.wait_ge(unit_done, UNITS_POOL)
                act.wait_ge(pooled, NB * (n + 1))
                act.activation(hn_hi[:, H + g, :], u[:, g, BUF:BUF + N], ACT.Copy).then_inc(p_hi, 1)

            def pmix(q):
                g, c = GROUP_OF[q // NB], q % NB
                act.wait_ge(unit_done, UNITS_POOL + q + 1)
                act.activation(hn_hi[:, H + g, blk(c)], ps[:, POOL_BANK[q], 0:BW], ACT.Copy,
                               scale=pscale_c[:, g:g + 1]).then_inc(pmix_hi, 1)

            def hmix_high(c):
                act.wait_ge(mixed, min(CH, TILES_OF[c]))
                act.activation(hn_hi[:, 0:H, blk(c)], qkvo[:, 3 * H:4 * H, blk(c)], ACT.Copy).then_inc(hmix_hi, 1)

            exp_w(0)
            for c in range(CH - 2):
                kv_by_token(c)
                unit_u(2 * c)
                square_h(c)
                exp_w(c + 1)
                unit_u(2 * c + 1)
            hi(0, 16 * (J_OUT // 2), UNITS_POOL)
            kv_by_token(CH - 2)
            p_split_hi(0)
            p_split_hi(1)
            square_h(CH - 2)
            exp_w(CH - 1)
            pmix(0)
            pmix(1)
            kv_by_token(CH - 1)
            hmix_high(0)
            pmix(2)
            p_split_hi(2)
            square_h(CH - 1)
            pmix(3)
            pmix(4)
            p_split_hi(3)
            pmix(5)
            hmix_high(1)
            for q in (6, 7, 8):
                pmix(q)
            for q in (9, 10, 11):
                pmix(q)
            act.wait_ge(s_mixed, 1)
            hmix_high(2)
            hi(1, 16 * ((J_OUT + 2) // 2), UNITS_OUT)

            def out_square(m, c):
                act.wait_ge(resid, m * NB + c + 1)
                act.wait_ge(resid_sum, m * NB + c + 1)
                act.activation(out_sq[:, c, :], xT[:, bass.ds(m, 1), blk(c)].rearrange("p a t -> p (a t)"),
                               ACT.Square).then_inc(resid_sq, 1)

            def out_squares(m):
                for c in range(NB):
                    out_square(m, c)

            act.wait_ge(hmix_lo, NB - 1)
            act.wait_ge(hmix_lo_last, 1)
            with act.Fori(0, KT // 2 - 1) as i:
                out_squares(i * 2)
                hi(0, i * 16 + 16 * (J_OUT // 2 + 1), i * 6 + UNITS_OUT + NB)
                out_squares(i * 2 + 1)
                hi(1, i * 16 + 16 * (J_OUT // 2 + 2), i * 6 + UNITS_OUT + 2 * NB)
            out_squares(KT - 2)
            act.wait_ge(gu_loaded, 32)
            act.activation(guw[:, 0, :, 0], w_raw[:], ACT.Copy).then_inc(gu_hi, 1)
            for c in range(NB):
                scaled_hi(c)
                out_square(KT - 1, c)
            def gu_split(a, tile, used):
                act.wait_ge(gu_loaded, tile * 32 + 32)
                if used is not None:
                    act.wait_ge(gu_done, used)
                act.activation(guw[:, a, :, 0], w_raw[:], ACT.Copy).then_inc(gu_hi, 1)

            def down_split(i, used):
                act.wait_ge(dw_loaded, i * 16 + 16)
                act.wait_ge(*used)
                act.activation(w_hi[:].rearrange("p a k c -> p a (k c)"), dw_raw[:], ACT.Copy).then_inc(dw_hi, 1)

            def hidden(base, e, half):
                act.wait_ge(gate_scaled, base + (e + 1))
                act.activation(ps[:, gate_bank(e), 0:BW], hf[:, hslot(half, e), :], ACT.Sigmoid).then_inc(sig_done, 1)

            def hslot(half, e):
                return (6 * half + e) % 4

            def hidden_hi(base, e, half):
                act.wait_ge(hid_f, base + (e + 1))
                act.activation(hid[:, 2 * half + e // NB, 0, blk(e % NB)], hf[:, hslot(half, e), :], ACT.Copy)\
                   .then_inc(hid_hi, 1)

            def down_split_last(used):
                act.wait_ge(dw_loaded, 16 * (FT // 2))
                act.wait_ge(gu_done, used)
                act.activation(dw_last[:, 0], dw_raw[:], ACT.Copy).then_inc(dw_hi, 1)

            def ffn_tiles(base, it, half, first=False, last=False):
                if not first:
                    down_split(it + (-1), (gu_done, 1) if isinstance(it, int) and it == 1
                               else (down_done, it * 24 + (-24)))
                for e in range(6):
                    if e:
                        hidden_hi(base, e - 1, half)
                    hidden(base, e, half)
                    if e == 1 and not first:
                        gu_split(1, it * 2 + 1, it * 6)
                    if e == NB and last:
                        down_split_last(base + NB)
                    elif e == NB:
                        gu_split(0, it * 2 + 2, it * 6 + NB)
                hidden_hi(base, 5, half)

            norm_root(0)
            norm_root(1)
            norm_root(2)
            gu_split(1, 1, None)
            ffn_tiles(0, 0, 0, first=True)
            ffn_tiles(6, 1, 1)
            with act.Fori(0, FT // 4 - 2) as i:
                ffn_tiles(i * 12 + 12, i * 2 + 2, 0)
                ffn_tiles(i * 12 + 18, i * 2 + 3, 1)
            n = FT // 2 - 3
            ffn_tiles(6 * n, n, 0)
            ffn_tiles(6 * n + 6, n + 1, 1)
            ffn_tiles(6 * n + 12, n + 2, 0, last=True)

            for tt in range(N_TOK):
                r = rows_of(tt)
                b = Y_BANKS[tt]
                act.wait_ge(y_turned, tt + 1)
                if tt >= 4:
                    act.wait_ge(y_stored[tt % 4], 16 * (tt // 4))
                act.activation(y_tok[0:r, tt % 4, :].rearrange("p (a t) -> p a t", a=2), ps[0:r, b:b + 2, :], ACT.Square,
                               accum_out=by_tok[0:r, 0, tt:tt + 1]).then_inc(y_ss, 1)
                act.wait_ge(y_ss, tt + 1)
                act.activation(by_tok[0:r, 1, tt:tt + 1], by_tok[0:r, 0, tt:tt + 1], ACT.Sqrt,
                               bias=eps_c[0:r, :], scale=1.0 / D).then_inc(y_std, 1)

        @block.vector
        def _(dve):
            def turn_half(tt):
                r = rows_of(tt)
                dve.wait_ge(x_turned, 2 * tt + 2)
                b = 3 + 2 * (tt % 2)
                dve.tensor_copy(xT[:, 4:8, tt * P:tt * P + r],
                                ps[:, b, :].rearrange("p (k t) -> p k t", t=P)[:, :, 0:r]).then_inc(xt_dve, 1)

            def root_to_rstd(tt):
                r = rows_of(tt)
                dve.wait_ge(x_std, tt + 1)
                dve.reciprocal(by_tok[0:r, 2, tt:tt + 1], by_tok[0:r, 1, tt:tt + 1]).then_inc(x_rstd, 1)

            def take_rstd(tt):
                r = rows_of(tt)
                dve.wait_ge(rstd_spread, tt + 1)
                dve.tensor_copy(rstd_x[:, tt * P:tt * P + r], ps[:, 6 + tt % 2, 0:r])\
                   .then_inc(rstd_copied, 1)

            def norm(k, g, first=0, last=KT):
                c = k % NB
                dve.wait_ge(rstd_copied, TILES_OF[c])
                dve.wait_ge(xt_act, TILES_OF[c])
                dve.wait_ge(xt_dve, TILES_OF[c])
                if k >= 2:
                    dve.wait_ge(hn_lo_pool, 4 * (k - 1))
                    dve.wait_ge(hn_lo_dve, 4 * (k - 1))
                for n in range(first, last):
                    dve.scalar_tensor_tensor(out=nts[k % 2][:, n, :], in0=xT[:, n, blk(c)], scalar=g[:, n:n + 1],
                                             in1=rstd_x[:, blk(c)], op0=ALU.mult, op1=ALU.mult).then_inc(normed, 1)
                    if n >= 3 and n % 2:
                        lo_odd(k, n - 2)
                if last == KT:
                    lo_odd(k, KT - 1)

            def lo_odd(k, n):
                dve.wait_ge(hn_hi_done, KT * k + n + 1)
                dve.tensor_tensor(hn_lo[:, n, blk(k % NB)], nts[k % 2][:, n, :], hn_hi[:, n, blk(k % NB)].bitcast(F32),
                                  ALU.subtract).then_inc(hn_lo_dve, 1)

            turn_half(0)
            root_to_rstd(0)
            turn_half(1)
            root_to_rstd(1)
            take_rstd(0)
            turn_half(2)
            root_to_rstd(2)
            take_rstd(1)
            take_rstd(2)
            dve.wait_ge(vecs_loaded, 16 * 7)
            norm(0, gmix_c, 0, 4)
            turn_half(3)
            norm(0, gmix_c, 4, KT)
            root_to_rstd(3)
            take_rstd(3)
            turn_half(4)
            root_to_rstd(4)
            turn_half(5)
            root_to_rstd(5)
            take_rstd(4)
            take_rstd(5)
            root_to_rstd(6)
            norm(1, gmix_c, 0, 4)
            turn_half(6)
            norm(1, gmix_c, 4, KT)
            turn_half(7)
            take_rstd(6)
            root_to_rstd(7)
            root_to_rstd(8)
            turn_half(8)
            take_rstd(7)
            take_rstd(8)
            norm(2, gmix_c)

            dve.wait_ge(unit_evac, 2 * NB + 1)
            dve.tensor_tensor(gi[:], gi[:], gi_lo[:], ALU.add).then_inc(gates_sum, 1)
            dve.tensor_tensor(gf[:], gf[:], gf_lo[:], ALU.add).then_inc(gates_sum, 1)
            dve.wait_ge(gates_sum, 2)
            dve.wait_ge(row_act, 1)
            dve.tensor_scalar(gf[:], gf[:], 0.0, None, ALU.min).then_inc(row_dve, 1)
            dve.wait_ge(row_act, 3)
            dve.wait_ge(row_dve, 1)
            dve.tensor_tensor(gf[:], gf[:], ab[:], ALU.subtract).then_inc(row_dve, 1)
            dve.wait_ge(row_dve, 2)
            dve.wait_ge(row_pool, 15)
            dve.tensor_tensor_scan(b_row[:], keep[:], gf[:, 0:T], 0.0, ALU.mult, ALU.add).then_inc(row_dve, 1)
            dve.tensor_tensor_scan(m_row[:], gf[:, 0:T], gi[:, 0:T], 0.0, ALU.add, ALU.max).then_inc(row_dve, 1)
            dve.tensor_tensor(sample_f[:], gf[:, T:N], m0[:], ALU.add).then_inc(sg_dve, 1)
            dve.wait_ge(sg_dve, 1)
            dve.tensor_tensor(m_s[:], sample_f[:], gi[:, T:N], ALU.max).then_inc(sg_dve, 1)
            dve.wait_ge(sg_dve, 2)
            dve.tensor_tensor(sample_exp[:, :, 0], gi[:, T:N], m_s[:], ALU.subtract).then_inc(sg_dve, 1)
            dve.tensor_tensor(sample_exp[:, :, 1], sample_f[:], m_s[:], ALU.subtract).then_inc(sg_dve, 1)
            dve.tensor_scalar(sample_exp[:, :, 2], m_s[:], -1.0, None, ALU.mult).then_inc(sg_dve, 1)
            dve.wait_ge(row_dve, 4)
            dve.tensor_tensor(gi[:, 0:T], gi[:, 0:T], b_row[:], ALU.subtract).then_inc(row_dve, 1)
            dve.tensor_tensor(r_row[:], b_row[:], m_row[:], ALU.subtract).then_inc(row_dve, 1)
            dve.tensor_copy(m_before[:, 1:CH], m_row[:, P - 1:T - 1:P]).then_inc(row_dve, 1)
            dve.wait_ge(row_dve, 7)
            dve.tensor_tensor(g_row[:].rearrange("h (c t) -> h c t", t=P), r_row[:].rearrange("h (c t) -> h c t", t=P),
                              m_before[:].rearrange("h (c a) -> h c a", a=1).to_broadcast([H, CH, P]), ALU.add)\
               .then_inc(row_dve, 1)
            dve.wait_ge(row_act, 4)
            dve.tensor_tensor(rr[32:32 + H, :], r_row[:], rr[0:H, :].bitcast(F32), ALU.subtract).then_inc(row_dve, 1)
            dve.wait_ge(row_act, 7)
            dve.tensor_tensor(rr[96:96 + H, :], g_row[:], g_hi[:].bitcast(F32), ALU.subtract).then_inc(row_dve, 1)
            dve.wait_ge(row_dve, 8)
            dve.tensor_copy(m_before[:, 0:1], m_row[:, T - 1:T]).then_inc(row_dve, 1)
            dve.reciprocal(inv_count[:], inv_count[:]).then_inc(row_dve, 1)
            dve.wait_ge(cols_turned, 1)
            dve.tensor_copy(cols[:].rearrange("p a c h -> p (a c h)"), ps[:, 2, 0:2 * CH * H]).then_inc(cols_done, 1)
            dve.wait_ge(buf_turned, 1)
            for g in range(G):
                view = ps[:, 3, g * P:g * P + S * BUF].rearrange("p (b j) -> p b j", j=BUF)
                dve.tensor_reduce(buf_sum[:, g, :], view[:, :, BUF - (WINDOWS[g] - 1):BUF], AX.X, ALU.add)\
                   .then_inc(buf_summed, 1)

            dve.wait_ge(unit_evac, NB * (1 + 3 * H))
            dve.tensor_copy(qkv_s[:].rearrange("p a (h b) -> p (a h) b", h=H), qkvo[:, 0:3 * H, T:N]).then_inc(s_gathered, 1)
            dve.wait_ge(s_turned, 3)
            dve.tensor_copy(s_rows[:].rearrange("r a d -> r (a d)"), ps[0:R, 2, 0:3 * P]).then_inc(s_rows_done, 1)
            dve.wait_ge(s_rows_done, 1)
            dve.wait_ge(scol_loaded, 16)
            dve.tensor_scalar(s_pack[:, 0:P], s_rows[:, 0, :], scol[:, 1:2], None, ALU.mult).then_inc(s_packed, 1)
            dve.tensor_scalar(s_pack[:, P:2 * P], s_rows[:, 1, :], scol[:, 0:1], None, ALU.mult).then_inc(s_packed, 1)
            dve.tensor_copy(s_pack[:, 2 * P:2 * P + 1], scol[:, 1:2]).then_inc(s_packed, 1)
            dve.wait_ge(n_loaded, 16 * H)
            dve.wait_ge(s_packed, 3)
            dve.scalar_tensor_tensor(out=n_new[:], in0=n_s[:], scalar=scol[:, 1:2], in1=s_pack[:, P:2 * P],
                                     op0=ALU.mult, op1=ALU.add).then_inc(s_packed, 1)
            dve.tensor_tensor_reduce(tmp_rows[:], s_rows[:, 0, :], s_pack[:, P:2 * P], 1.0, 0.0, ALU.mult, ALU.add,
                                     s_small[:, 0:1]).then_inc(s_head, 1)
            dve.wait_ge(s_head, 1)
            dve.tensor_tensor_reduce(tmp_rows[:], n_s[:], s_pack[:, 0:P], 1.0, 0.0, ALU.mult, ALU.add,
                                     s_small[:, 1:2]).then_inc(s_head, 1)
            dve.wait_ge(s_head, 2)
            dve.tensor_tensor(s_small[:, 2:3], s_small[:, 0:1], s_small[:, 1:2], ALU.add).then_inc(s_head, 1)
            dve.wait_ge(s_head, 3)
            dve.scalar_tensor_tensor(out=s_small[:, 3:4], in0=s_small[:, 2:3], scalar=-1.0, in1=scol[:, 2:3],
                                     op0=ALU.mult, op1=ALU.max).then_inc(s_den, 1)
            dve.wait_ge(s_den, 1)
            dve.tensor_tensor(s_small[:, 3:4], s_small[:, 2:3], s_small[:, 3:4], ALU.max).then_inc(s_head, 1)
            dve.wait_ge(s_head, 4)
            dve.reciprocal(s_small[:, 7:8], s_small[:, 3:4]).then_inc(s_head, 1)
            for half_ in range(2):
                rs = slice(half_ * (R // 2), (half_ + 1) * (R // 2))
                dve.wait_ge(C_loaded[half_], 32)
                dve.wait_ge(bc_loaded[half_], 16)
                n0 = 4 * half_
                if half_:
                    dve.wait_ge(s_state, n0)
                dve.tensor_tensor(tmp_s[:], C_s[:, rs, :], bc_s[:, :, 0:P], ALU.mult).then_inc(s_state, 1)
                dve.wait_ge(s_state, n0 + 1)
                dve.tensor_reduce(inter[:, rs], tmp_s[:], AX.X, ALU.add).then_inc(s_state, 1)
                dve.wait_ge(s_state, n0 + 2)
                vcol = qkvo[:, 2 * H + 2 * half_:2 * H + 2 * half_ + 2, T:N].rearrange("p h (b a) -> p h b a", a=1)\
                    .to_broadcast([P, 2, S, P])
                dve.tensor_tensor(tmp_s[:].rearrange("p (h b) k -> p h b k", h=2),
                                  bc_s[:, :, P:2 * P].rearrange("p (h b) k -> p h b k", h=2), vcol, ALU.mult)\
                   .then_inc(s_state, 1)
                dve.wait_ge(s_scaled, half_ + 1)
                dve.wait_ge(s_state, n0 + 3)
                dve.tensor_tensor(C_s[:, rs, :], C_s[:, rs, :], tmp_s[:], ALU.add).then_inc(s_state, 1)

            def decode_heads():
                dve.wait_ge(inter_turned, 1)
                dve.wait_ge(s_head, 5)
                dve.scalar_tensor_tensor(out=h_s[:], in0=s_rows[:, 2, :], scalar=s_small[:, 0:1], in1=ps[0:R, 5, 0:P],
                                         op0=ALU.mult, op1=ALU.add).then_inc(s_head, 1)
                dve.wait_ge(s_head, 6)
                dve.tensor_scalar(h_s[:], h_s[:], s_small[:, 7:8], None, ALU.mult).then_inc(s_head, 1)
                dve.wait_ge(s_head, 7)
                dve.tensor_tensor_reduce(tmp_rows[:], h_s[:], h_s[:], 1.0, 0.0, ALU.mult, ALU.add,
                                         s_small[:, 4:5]).then_inc(s_head, 1)
                dve.wait_ge(s_pow, 2)
                dve.tensor_scalar(h_s[:], h_s[:], s_small[:, 6:7], None, ALU.mult).then_inc(s_head, 1)

            def scale_o():
                for h in range(H):
                    dve.wait_ge(unit_evac, NB * (1 + 3 * H + h + 1))
                    dve.tensor_scalar(qkvo[:, 3 * H + h, :], qkvo[:, 3 * H + h, :], ghead_c[:, h:h + 1], None, ALU.mult)\
                       .then_inc(o_scaled, 1)

            def exponents(c):
                dve.wait_ge(rg_done, c + 1)
                if c >= 2:
                    dve.wait_ge(p_done, c - 1)
                    dve.wait_ge(wv_done, c - 1)
                for h in range(H):
                    ins = dve.scalar_tensor_tensor(out=wt[:, c % 2, h, :], in0=ps[:, 2, h * P:(h + 1) * P],
                                                   scalar=cols[:, 0, c, h:h + 1], in1=cap[:], op0=ALU.add, op1=ALU.min)
                ins.then_inc(d_done, 1)

            def scaled_q(c):
                gv = ps[:, 3, :].rearrange("p (h t) -> p h t", h=H)
                if c >= 2:
                    dve.wait_ge(c_done, c - 1)
                dve.tensor_copy(gend[:, c % 2, :], gv[:, :, P - 1]).then_inc(gend_done, 1)
                if c:
                    dve.wait_ge(num_done, c)
                dve.tensor_tensor(qg[:], qkvo[:, 0:H, chk(c)], gv, ALU.mult).then_inc(qg_done, 1)

            def weights(c):
                dve.wait_ge(scores, c + 1)
                dve.wait_ge(w_exp, c + 1)
                if c:
                    dve.wait_ge(num_done, c)
                dve.tensor_tensor(pt[:], ps[:, 4, :].rearrange("p (h t) -> p h t", h=H), wt[:, c % 2], ALU.mult)\
                   .then_inc(p_done, 1)

            nv = ps[:, 6:8, 0:2 * (P + 1)].rearrange("p a (h v) -> p a h v", v=P + 1)

            def head(c):
                dve.wait_ge(num_done, c + 1)
                den2 = den[:].rearrange("p (a h) -> p a h", a=2)
                dve.scalar_tensor_tensor(out=den2, in0=nv[:, :, :, P], scalar=-1.0,
                                         in1=cols[:, 1, c, :].rearrange("p (a h) -> p a h", a=2), op0=ALU.mult,
                                         op1=ALU.max).then_inc(den_step, 1)
                dve.wait_ge(den_step, 3 * c + 1)
                dve.tensor_tensor(den2, nv[:, :, :, P], den2, ALU.max).then_inc(den_step, 1)
                dve.wait_ge(den_step, 3 * c + 2)
                if c:
                    dve.wait_ge(h_turned, c)
                dve.reciprocal(rden[:], den[:]).then_inc(den_step, 1)
                dve.wait_ge(den_step, 3 * c + 3)
                dve.tensor_tensor(h_tok[:].rearrange("p (a h) v -> p a h v", a=2), nv[:, :, :, 0:P],
                                  rden[:].rearrange("p (a h b) -> p a h b", a=2, b=1).to_broadcast([P, 2, 2, P]),
                                  ALU.mult).then_inc(h_done, 1)

            def scaled_h(c):
                dve.wait_ge(rs_step, 2 * c + 2)
                dve.tensor_tensor(h_tok[:], h_tok[:], rs_h[:].rearrange("p (h a) -> p h a", a=1).to_broadcast([P, H, P]),
                                  ALU.mult).then_inc(hs_done, 1)

            def mix(c):
                dve.wait_ge(h_turned, c + 1)
                if c == 0:
                    dve.wait_ge(o_scaled, H)
                dve.tensor_tensor(qkvo[:, 3 * H:4 * H, chk(c)], ps[:, 5, :].rearrange("p (h t) -> p h t", h=H),
                                  qkvo[:, 3 * H:4 * H, chk(c)], ALU.mult).then_inc(mixed, 1)

            def state(c):
                dve.wait_ge(kv_done, c + 1)
                dve.wait_ge(gend_done, c + 1)
                if c:
                    dve.wait_ge(c_done, c)
                for h in range(H):
                    ins = dve.scalar_tensor_tensor(out=C_st[:, h, :], in0=C_st[:, h, :], scalar=gend[:, c % 2, h:h + 1],
                                                   in1=nv[:, h // 2, h % 2, :], op0=ALU.mult, op1=ALU.add)
                ins.then_inc(c_done, 1)

            psteps = [0]

            def p_wait():
                if psteps[0]:
                    dve.wait_ge(p_step, psteps[0])

            def p_inc(ins):
                psteps[0] += 1
                ins.then_inc(p_step, 1)

            def pool_block(n, c):
                g, q = GROUP_OF[n], NB * n + (NB - 1 - c)
                k = WINDOWS[g]
                if c == NB - 1:
                    dve.wait_ge(unit_evac, UNITS_U + NB * n + NB)
                    dve.tensor_copy(u_last[:, g, :], u[:, g, BUF + T - BUF:BUF + N]).then_inc(u_saved, 1)
                    dve.wait_ge(u_saved, n + 1)
                    us = u[:, g, BUF + T:BUF + N]
                    dve.wait_ge(buf_summed, G)
                    p_wait()
                    p_inc(dve.tensor_tensor(small8[:], buf_sum[:, g, :], us, ALU.add))
                    p_wait()
                    p_inc(dve.scalar_tensor_tensor(out=us, in0=small8[:], scalar=1.0 / k, in1=us, op0=ALU.mult,
                                                   op1=ALU.subtract))
                t0, t1 = c * BW, min((c + 1) * BW, T)
                s = win[:, g % 2, 0:t1 - t0]
                if n == G - 1:
                    dve.wait_ge(pooled, q)
                    p_wait()
                    a = BUF + t0
                    p_inc(dve.tensor_tensor(s, u[:, g, a:BUF + t1], u[:, g, a - 1:BUF + t1 - 1], ALU.add))
                    p_wait()
                else:
                    dve.wait_ge(win_done, q + 1)
                head_n = k - 1 if c == 0 else 0
                if head_n:
                    uh = u[:, g, BUF:BUF + head_n]
                    p_inc(dve.tensor_tensor(s[:, 0:head_n], s[:, 0:head_n], inv_count[:, 0:head_n], ALU.mult))
                    p_wait()
                    p_inc(dve.tensor_tensor(uh, s[:, 0:head_n], uh, ALU.subtract))
                uu = u[:, g, BUF + t0 + head_n:BUF + t1]
                dve.scalar_tensor_tensor(out=uu, in0=s[:, head_n:], scalar=1.0 / k, in1=uu, op0=ALU.mult,
                                         op1=ALU.subtract).then_inc(pooled, 1)

            def pool_at(c, place):
                for n, b in POOL_AT.get((c, place), ()):
                    pool_block(n, b)

            def p_split_lo(n):
                g = GROUP_OF[n]
                dve.wait_ge(p_hi, n + 1)
                p_wait()
                dve.tensor_tensor(hn_lo[:, H + g, :], u[:, g, BUF:BUF + N], hn_hi[:, H + g, :].bitcast(F32), ALU.subtract)\
                   .then_inc(p_lo_dve, 1)

            def pmix(q):
                g, c = GROUP_OF[q // NB], q % NB
                dve.wait_ge(pmix_hi, q + 1)
                dve.scalar_tensor_tensor(out=hn_lo[:, H + g, blk(c)], in0=ps[:, POOL_BANK[q], 0:BW],
                                         scalar=pscale_c[:, g:g + 1], in1=hn_hi[:, H + g, blk(c)].bitcast(F32),
                                         op0=ALU.mult, op1=ALU.subtract).then_inc(pmix_lo, 1)

            dve.wait_ge(m_init, 3)
            exponents(0)
            scaled_q(0)
            weights(0)
            decode_heads()
            scale_o()
            for c in range(CH - 1):
                if c:
                    mix(c - 1)
                pool_at(c - 1, 0)
                head(c)
                exponents(c + 1)
                scaled_q(c + 1)
                pool_at(c - 1, 1)
                state(c)
                weights(c + 1)
                pool_at(c, 2)
                if c == CH - 2:
                    pmix(0)
                    pmix(1)
                scaled_h(c)
                if c == 3:
                    dve.wait_ge(hs_turned, 1)
                    dve.tensor_tensor(qkvo[:, 3 * H:4 * H, T:N], ps[:, 5, 0:R].rearrange("p (h b) -> p h b", h=H),
                                      qkvo[:, 3 * H:4 * H, T:N], ALU.mult).then_inc(s_mixed, 1)
            pmix(2)
            pool_block(G - 1, 2)
            mix(CH - 2)
            head(CH - 1)
            pool_block(G - 1, 1)
            state(CH - 1)
            pmix(3)
            pool_block(G - 1, 0)
            scaled_h(CH - 1)
            pmix(4)
            pmix(5)
            mix(CH - 1)
            p_split_lo(3)
            for q in range(6, NB * G):
                pmix(q)

            dve.wait_ge(hmix_hi, NB)
            dve.tensor_tensor(hn_lo[:, 0:H, blk(NB - 1)], qkvo[:, 3 * H:4 * H, blk(NB - 1)],
                              hn_hi[:, 0:H, blk(NB - 1)].bitcast(F32), ALU.subtract).then_inc(hmix_lo_last, 1)
            dve.wait_ge(u_rows_turned, 1)
            dve.tensor_copy(u_rows[:], ps[0:BUF + S, 3, :]).then_inc(u_rows_done, 1)
            dve.wait_ge(C_turned, 1)
            dve.wait_ge(rows_stored, 16 * (H + 2))
            dve.tensor_copy(C_fin[:].rearrange("p h k -> p (h k)"), ps[:, 2, :]).then_inc(C_out, 1)
            dve.tensor_copy(n_fin[:], ps[0:H, 6, 0:P]).then_inc(C_out, 1)

            dve.wait_ge(hmix_lo, NB - 1)
            dve.wait_ge(hmix_lo_last, 1)
            for c in range(NB):
                dve.memset(ssq[:, c, :], 0.0).then_inc(resid_sum, 1)
            dve.wait_ge(x_back, 16 * NB)

            def residual(m, start, c):
                dve.wait_ge(unit_done, m * NB + UNITS_OUT + c + 1)
                xs = xT[:, bass.ds(m, 1), blk(c)].rearrange("p a t -> p (a t)")
                dve.tensor_tensor(xs, ps[:, (start + c) % 2, 0:BW], xs, ALU.add).then_inc(resid, 1)

            def square_sum(m, c):
                dve.wait_ge(resid_sq, m * NB + c + 1)
                dve.wait_ge(resid_sum, m * NB + c + 1)
                dve.tensor_tensor(ssq[:, c, :], ssq[:, c, :], out_sq[:, c, :], ALU.add).then_inc(resid_sum, 1)

            def out_tile(m, start):
                for c in range(NB):
                    residual(m, start, c)
                for c in range(NB):
                    square_sum(m, c)

            def scaled_lo(c):
                for n in range(KT):
                    dve.wait_ge(hn_hi_done, KT * (NB + c) + n + 1)
                    dve.scalar_tensor_tensor(out=hn_lo[:, n, blk(c)], in0=xT[:, n, blk(c)], scalar=gffn_c[:, n:n + 1],
                                             in1=hn_hi[:, n, blk(c)].bitcast(F32), op0=ALU.mult, op1=ALU.subtract)\
                       .then_inc(hn_lo_dve, 1)

            def norm_inverse(c):
                dve.wait_ge(norm_std, c + 1)
                dve.reciprocal(rstd[:, c, :], rstd[:, c, :]).then_inc(norm_rstd, 1)

            with dve.Fori(0, KT // 2 - 1) as i:
                out_tile(i * 2, UNITS_OUT)
                out_tile(i * 2 + 1, UNITS_OUT + NB)
            out_tile(KT - 2, UNITS_OUT)
            residual(KT - 1, UNITS_OUT + NB, 0)
            scaled_lo(0)
            residual(KT - 1, UNITS_OUT + NB, 1)
            scaled_lo(1)
            residual(KT - 1, UNITS_OUT + NB, 2)
            square_sum(KT - 1, 0)
            scaled_lo(2)
            square_sum(KT - 1, 1)
            square_sum(KT - 1, 2)
            def ffn_tiles(base, half, down_base=None, after=DOWN_AFTER):
                for e in range(6):
                    s, r = hf[:, (6 * half + e) % 4, :], rstd[:, e % NB, :]
                    dve.wait_ge(gu_done, base + (e + 1))
                    if isinstance(base, int) and base + e < NB:
                        norm_inverse(e)
                        dve.wait_ge(norm_rstd, e + 1)
                    dve.tensor_tensor(s, ps[:, gate_bank(e), 0:BW], r, ALU.mult).then_inc(gate_scaled, 1)
                    if e:
                        hidden_lo(base, e - 1, half)
                    dve.wait_ge(sig_done, base + (e + 1))
                    dve.tensor_tensor(s, ps[:, gate_bank(e), 0:BW], s, ALU.mult).then_inc(act_gate, 1)
                    dve.wait_ge(act_gate, base + (e + 1))
                    dve.tensor_tensor(s, ps[:, 2 + gate_bank(e), 0:BW], s, ALU.mult).then_inc(act_up, 1)
                    units = range(*after[e]) if down_base is not None else ()
                    for q in units[0:1]:
                        down_add(down_base, q)
                    dve.wait_ge(act_up, base + (e + 1))
                    dve.tensor_tensor(s, s, r, ALU.mult).then_inc(hid_f, 1)
                    for n, q in enumerate(units[1:]):
                        if e == 5 and n == 1:
                            hidden_lo(base, 5, half)
                        down_add(down_base, q)
                if down_base is None:
                    hidden_lo(base, 5, half)

            def down_add(base, q):
                dve.wait_ge(down_done, base + (q + 1))
                xs = xT[:, q % KT, blk(q // KT)]
                dve.tensor_tensor(xs, ps[:, 4 + q % 4, 0:BW], xs, ALU.add).then_inc(x_acc, 1)

            def hidden_lo(base, e, half):
                dve.wait_ge(hid_hi, base + (e + 1))
                t, c = 2 * half + e // NB, e % NB
                dve.tensor_tensor(hid[:, t, 1, blk(c)], hf[:, (6 * half + e) % 4, :], hid[:, t, 0, blk(c)].bitcast(F32),
                                  ALU.subtract).then_inc(hid_lo, 1)

            dve.wait_ge(C_fin_stored, 32)
            ffn_tiles(0, 0)
            with dve.Fori(0, FT // 4 - 1) as i:
                ffn_tiles(i * 12 + 6, 1, i * 48)
                ffn_tiles(i * 12 + 12, 0, i * 48 + 24)
            n = FT // 2 - 2
            ffn_tiles(6 * n, 1, 24 * (n - 1))
            ffn_tiles(6 * n + 6, 0, 24 * n, DOWN_AFTER_LAST)
            last = 24 * (FT // 2 - 1)

            def final(tt):
                r = rows_of(tt)
                b = Y_BANKS[tt]
                dve.wait_ge(y_std, tt + 1)
                dve.reciprocal(by_tok[0:r, 2, tt:tt + 1], by_tok[0:r, 1, tt:tt + 1]).then_inc(y_rstd, 1)
                dve.wait_ge(y_rstd, tt + 1)
                dve.wait_ge(gfin_loaded, 16)
                dve.scalar_tensor_tensor(out=y_tok[0:r, tt % 4, :].rearrange("p (a t) -> p a t", a=2),
                                         in0=ps[0:r, b:b + 2, :], scalar=by_tok[0:r, 2, tt:tt + 1],
                                         in1=gfin[0:r, :].rearrange("p (a t) -> p a t", a=2), op0=ALU.mult, op1=ALU.mult)\
                   .then_inc(y_done, 1)

            for c, (t0, t1) in enumerate(LAST_PARTS):
                for n in range(KT):
                    q = c * KT + n
                    dve.wait_ge(down_done, last + q + 1)
                    dve.tensor_tensor(xT[:, n, t0:t1], ps[:, 4 + q % 4, 0:t1 - t0], xT[:, n, t0:t1], ALU.add)\
                       .then_inc(x_acc, 1)
                    if q in FINAL_AFTER:
                        final(FINAL_AFTER[q])
            for tt in range(len(FINAL_AFTER), N_TOK):
                final(tt)

        @block.tensor
        def _(pe):
            def turn(tt):
                r = rows_of(tt)
                pe.wait_ge(x_loaded[tt % 4], 16 * (tt // 4 + 1))
                for half, freed in ((0, xt_act), (1, xt_dve)):
                    if tt >= 2:
                        pe.wait_ge(freed, tt - 1)
                    for n in range(4):
                        k = 4 * half + n
                        ins = pe.transpose(ps[:, 2 + 2 * (tt % 2) + half, n * P:n * P + r],
                                           x_tok[0:r, tt % 4, k * P:(k + 1) * P], ident[0:r, 0:r])
                    ins.then_inc(x_turned, 1)

            def spread_rstd(tt):
                r = rows_of(tt)
                pe.wait_ge(x_rstd, tt + 1)
                if tt >= 2:
                    pe.wait_ge(rstd_copied, tt - 1)
                pe.matmul(ps[:, 6 + tt % 2, 0:r], by_tok[0:r, 2, tt:tt + 1].to_broadcast([r, P]),
                          ident[0:r, 0:r], start=True, stop=True).then_inc(rstd_spread, 1)

            def norm_sum(c):
                pe.wait_ge(resid_sum, NB * KT + c + 1)
                pe.matmul(ps[:, 5 + c, 0:BW], ones[:], ssq[:, c, :], start=True, stop=True).then_inc(norm_total, 1)

            def product(out, lhs_hi, lhs_lo, rhs_hi, rhs_lo, ks, begin=True, end=True):
                for i, k in enumerate(ks):
                    pe.matmul(out, lhs_hi(k), rhs_hi(k), start=(begin and i == 0), stop=False)
                    pe.matmul(out, lhs_hi(k), rhs_lo(k), start=False, stop=False)
                    ins = pe.matmul(out, lhs_lo(k), rhs_hi(k), start=False, stop=(end and i == len(ks) - 1))
                return ins

            def gates_unit(bank, c):
                for k in range(KT):
                    for wide in (True, False) if k == 0 else (False, True):
                        cols, hn = (96 + H, hn_hi) if wide else (32 + H, hn_lo)
                        ins = pe.matmul(ps[0:cols, bank, 0:BW], gates_w[:, k, 0:cols], hn[:, k, blk(c)],
                                        start=(k == 0 and wide), stop=(k == KT - 1 and wide))
                return ins

            def unit(slot, bank, c, ks=range(KT), **parts):
                return product(ps[:, bank, 0:BW], lambda k: w_hi[:, slot, k, :], lambda k: w_lo[:, slot, k, :],
                               lambda k: hn_hi[:, k, blk(c)], lambda k: hn_lo[:, k, blk(c)], ks, **parts)

            def first_units(c, tile):
                pe.wait_ge(w_ready, tile + 1)
                pe.wait_ge(hn_lo_pool, 4 * (c + 1))
                pe.wait_ge(hn_lo_dve, 4 * (c + 1))
                n = NB * c + tile
                if n >= 2:
                    pe.wait_ge(unit_evac, n - 1)
                (unit(tile % 2, n % 2, c) if tile else gates_unit(n % 2, c)).then_inc(unit_done, 1)

            pe.wait_ge(consts, 4)
            turn(0)
            turn(1)
            spread_rstd(0)
            turn(2)
            spread_rstd(1)
            spread_rstd(2)
            turn(3)
            turn(4)
            turn(5)
            spread_rstd(3)
            first_units(0, 0)
            spread_rstd(4)
            spread_rstd(5)
            first_units(0, 1)
            turn(6)
            turn(7)
            spread_rstd(6)
            first_units(0, 2)
            turn(8)
            spread_rstd(7)
            spread_rstd(8)
            first_units(1, 0)
            first_units(1, 1)
            first_units(1, 2)
            for tile in range(3):
                first_units(2, tile)

            def pair(i):
                for d in range(2):
                    pe.wait_ge(w_ready, i * 2 + 2 + d)
                    for c in range(NB):
                        n = NB + NB * d + c
                        pe.wait_ge(unit_evac, i * 6 + (n - 1))
                        unit((1 + d) % 2, n % 2, c).then_inc(unit_done, 1)

            with pe.Fori(1, 4) as i:
                pair(i)
            pe.wait_ge(row_dve, 5)
            pe.wait_ge(row_act, 6)
            for n, row in enumerate((gi, ab)):
                for c in range(CH):
                    ins = pe.transpose(ps[:, 2, (n * CH + c) * H:(n * CH + c + 1) * H], row[:, chk(c)], ident[0:H, 0:H])
            ins.then_inc(cols_turned, 1)
            pe.wait_ge(buf_loaded, 16)
            for g in range(G):
                ins = pe.transpose(ps[:, 3, g * P:g * P + S * BUF], buf_rows[:, chk(g)], ident[0:S * BUF, 0:S * BUF])
            ins.then_inc(buf_turned, 1)
            with pe.Fori(4, 6) as i:
                pair(i)
            pe.wait_ge(s_gathered, 1)
            pe.wait_ge(cols_done, 1)
            for n in range(3):
                ins = pe.transpose(ps[0:R, 2, n * P:(n + 1) * P], qkv_s[:, n, :], ident[:])\
                    .then_inc(s_turned, 1)
            with pe.Fori(6, 8) as i:
                pair(i)

            def rows_everywhere(c):
                if c:
                    pe.wait_ge(kv_tok, 2 * c)
                for q, bank in ((0, 2), (1, 3)):
                    for h in range(H):
                        n = H * q + h
                        ins = pe.matmul(ps[:, bank, chk(h)], sel[:, n:n + 1].to_broadcast([P, P]), rr[:, chk(c)],
                                        start=True, stop=True)
                ins.then_inc(rg_done, 1)

            def score(c):
                if c:
                    pe.wait_ge(p_done, c)
                for h in range(H):
                    ins = pe.matmul(ps[:, 4, chk(h)], qkvo[:, H + h, chk(c)], qkvo[:, h, chk(c)], start=True, stop=True)
                ins.then_inc(scores, 1)

            def kv_turn(c):
                for n, bank, freed in ((1, 2, d_done), (2, 3, qg_done)):
                    pe.wait_ge(freed, c + 1)
                    for h in range(H):
                        ins = pe.transpose(ps[:, bank, chk(h)], qkvo[:, n * H + h, chk(c)], ident[:])
                    ins.then_inc(kv_turned, 1)

            nv = ps[:, 6:8, 0:2 * (P + 1)].rearrange("p a (h v) -> p a h v", v=P + 1)

            def numerator(c):
                pe.wait_ge(p_done, c + 1)
                pe.wait_ge(qg_done, c + 1)
                pe.wait_ge(kv_tok, 2 * c + 2)
                if c:
                    pe.wait_ge(c_done, c)
                for h in range(H):
                    pe.matmul(nv[:, h // 2, h % 2, :], pt[:, h, :], v_tok[:, c % 2, h, :], start=True, stop=False)
                    ins = pe.matmul(nv[:, h // 2, h % 2, :], qg[:, h, :], C_st[:, h, :], start=False, stop=True)
                ins.then_inc(num_done, 1)

            def outer(c):
                pe.wait_ge(h_done, c + 1)
                pe.wait_ge(wv_done, c + 1)
                for h in range(H):
                    ins = pe.matmul(nv[:, h // 2, h % 2, :], k_tok[:, c % 2, h, :], wv[:, h, :], start=True, stop=True)
                ins.then_inc(kv_done, 1)

            def h_turn(c):
                pe.wait_ge(hs_done, c + 1)
                if c:
                    pe.wait_ge(mixed, c)
                else:
                    pe.wait_ge(s_head, 6)
                if c == 3:
                    pe.wait_ge(s_mixed, 1)
                for h in range(H):
                    ins = pe.transpose(ps[:, 5, chk(h)], h_tok[:, h, :], ident[:])
                ins.then_inc(h_turned, 1)

            def unit_u(k):
                j, c = J_U + k // NB, k % NB
                pe.wait_ge(w_ready, j + 1)
                pe.wait_ge(unit_evac, UNITS_U + k - 1)
                unit(j % 2, (UNITS_U + k) % 2, c).then_inc(unit_done, 1)

            def unit_pool(q):
                g, c = GROUP_OF[q // NB], q % NB
                pe.wait_ge(w_ready, J_POOL + 1)
                before = [n for n in range(q) if POOL_BANK[n] == POOL_BANK[q]]
                if before:
                    pe.wait_ge(pmix_lo, before[-1] + 1)
                elif q < 2:
                    pe.wait_ge(unit_evac, UNITS_POOL - 1 + q)
                else:
                    pe.wait_ge(p_done, CH)
                if q // NB < G - 1:
                    pe.wait_ge(p_lo_pool, q // NB + 1)
                else:
                    pe.wait_ge(p_lo_dve, 1)
                bank, k = ps[:, POOL_BANK[q], 0:BW], H + g
                pe.matmul(bank, w_hi[:, 1, g, :], hn_hi[:, k, blk(c)], start=True, stop=False)
                pe.matmul(bank, w_hi[:, 1, g, :], hn_lo[:, k, blk(c)], start=False, stop=False)
                pe.matmul(bank, w_lo[:, 1, g, :], hn_hi[:, k, blk(c)], start=False, stop=True).then_inc(unit_done, 1)

            pe.wait_ge(row_dve, 10)
            pe.wait_ge(row_act, 8)
            pe.wait_ge(s_rows_done, 1)
            pe.wait_ge(buf_summed, G)
            rows_everywhere(0)
            score(0)
            pe.wait_ge(s_state, 6)
            pe.transpose(ps[0:R, 5, 0:P], inter[:], ident[:]).then_inc(inter_turned, 1)
            unit_u(0)
            unit_u(1)
            for c in range(CH - 2):
                kv_turn(c)
                if c:
                    unit_u(2 * c)
                    h_turn(c - 1)
                numerator(c)
                rows_everywhere(c + 1)
                score(c + 1)
                if c:
                    unit_u(2 * c + 1)
                outer(c)
                if c == 3:
                    pe.wait_ge(mixed, c)
                    pe.wait_ge(s_head, 9)
                    pe.transpose(ps[:, 5, 0:R], h_s[:], ident[0:R, 0:R]).then_inc(hs_turned, 1)
            c = CH - 2
            kv_turn(c)
            numerator(c)
            rows_everywhere(c + 1)
            score(c + 1)
            h_turn(c - 1)
            unit_pool(0)
            unit_pool(1)
            outer(c)
            c = CH - 1
            kv_turn(c)
            unit_pool(2)
            h_turn(c - 1)
            numerator(c)
            unit_pool(3)
            outer(c)
            unit_pool(4)
            unit_pool(5)
            pe.wait_ge(kv_tok, 2 * CH)
            pe.wait_ge(u_saved, G)
            for g in range(G):
                ins = pe.transpose(ps[0:BUF + S, 3, chk(g)], u_last[:, g, :], ident[:])
            ins.then_inc(u_rows_turned, 1)
            h_turn(c)
            for q in range(6, NB * G):
                unit_pool(q)
            pe.wait_ge(c_done, CH)
            pe.wait_ge(kv_tok, 2 * CH)
            for h in range(H):
                pe.transpose(ps[:, 2, chk(h)], C_st[:, h, 0:P], ident[:])
            pe.transpose(ps[0:H, 6, 0:P], C_st[:, :, P], ident[:]).then_inc(C_turned, 1)

            def out_tile(m, slot, start, first):
                pe.wait_ge(w_ready, m + J_OUT + 1)
                for c in range(NB):
                    if first and c < 2:
                        pe.wait_ge(pmix_lo, NB * G)
                    else:
                        pe.wait_ge(resid, m * NB + (c - 1))
                    if first:
                        unit(slot, (start + c) % 2, c, range(H, KT), end=False)
                        pe.wait_ge(*((hmix_lo, c + 1) if c < NB - 1 else (hmix_lo_last, 1)))
                        unit(slot, (start + c) % 2, c, range(H), begin=False).then_inc(unit_done, 1)
                    else:
                        unit(slot, (start + c) % 2, c).then_inc(unit_done, 1)

            out_tile(0, 0, UNITS_OUT, True)
            out_tile(1, 1, UNITS_OUT + NB, False)
            with pe.Fori(1, KT // 2) as i:
                out_tile(i * 2, 0, UNITS_OUT, False)
                out_tile(i * 2 + 1, 1, UNITS_OUT + NB, False)

            def gate_up(base, tile, e, first=False):
                a, c = e // NB, e % NB
                if c == 0:
                    pe.wait_ge(gu_ready, tile * 2 + (a + 1))
                if first and a == 0:
                    pe.wait_ge(hn_lo_dve, 4 * NB + KT * (c + 1))
                if first and e < 2:
                    pe.wait_ge(resid, NB * (KT - 1) + 2 + e)
                else:
                    pe.wait_ge(act_up, base + (e - 1))
                for g in range(2):
                    if first and 2 * e + g in (1, 2):
                        for b in ((), (0,), (1, 2))[2 * e + g]:
                            norm_sum(b)
                    ins = product(ps[:, 2 * g + gate_bank(e), 0:BW], lambda k: guw[:, a, g, 0, k, :],
                                  lambda k: guw[:, a, g, 1, k, :], lambda k: hn_hi[:, k, blk(c)],
                                  lambda k: hn_lo[:, k, blk(c)], range(KT))
                ins.then_inc(gu_done, 1)

            dw = [w[:].rearrange("p a k c -> p a (k c)") for w in (w_hi, w_lo)]

            def down(it, base, units, half, q, first=False):
                c, n = q // KT, q % KT
                if q == 0:
                    pe.wait_ge(dw_ready, it + 1)
                if n == 0:
                    pe.wait_ge(hid_lo, units + (NB + c + 1))
                if not (first and q < 4):
                    pe.wait_ge(x_acc, base + (q - 3))
                product(ps[:, 4 + q % 4, 0:BW], lambda k: dw[0][:, k, chk(n)], lambda k: dw[1][:, k, chk(n)],
                        lambda k: hid[:, 2 * half + k, 0, blk(c)], lambda k: hid[:, 2 * half + k, 1, blk(c)],
                        range(2)).then_inc(down_done, 1)

            def ffn_tiles(it, units, half, base=None, first=False, after=DOWN_AFTER):
                for e in range(6):
                    gate_up(units, it, e, first=base is None)
                    for q in range(*after[e]) if base is not None else ():
                        down(it + (-1), base, units + (-6), 1 - half, q, first)

            def down_last(it):
                base = 24 * it
                pe.wait_ge(dw_ready, it + 1)
                for c, (t0, t1) in enumerate(LAST_PARTS):
                    pe.wait_ge(hid_lo, 6 * it + NB + (t1 + BW - 1) // BW)
                    for n in range(KT):
                        q = c * KT + n
                        pe.wait_ge(x_acc, base + (q - 3))
                        product(ps[:, 4 + q % 4, 0:t1 - t0], lambda k: dw_last[:, 0, k, chk(n)],
                                lambda k: dw_last[:, 1, k, chk(n)], lambda k: hid[:, k, 0, t0:t1],
                                lambda k: hid[:, k, 1, t0:t1], range(2)).then_inc(down_done, 1)
                        if q in FINAL_TURN:
                            y_turn(FINAL_TURN[q], base)

            def y_turn(tt, base):
                r = rows_of(tt)
                need = next(c for c, part in enumerate(LAST_PARTS) if tt * P < part[1])
                pe.wait_ge(x_acc, base + KT * (need + 1))
                before = [n for n in range(tt) if Y_BANKS[n] == Y_BANKS[tt]]
                if before:
                    pe.wait_ge(y_done, before[-1] + 1)
                for k in range(KT):
                    ins = pe.transpose(ps[0:r, Y_BANKS[tt] + k // 4, (k % 4) * P:(k % 4 + 1) * P],
                                       xT[:, k, tt * P:tt * P + r], ident[:])
                ins.then_inc(y_turned, 1)

            ffn_tiles(0, 0, 0)
            ffn_tiles(1, 6, 1, 0, first=True)
            ffn_tiles(2, 12, 0, 24)
            with pe.Fori(1, FT // 4 - 1) as i:
                ffn_tiles(i * 2 + 1, i * 12 + 6, 1, i * 48)
                ffn_tiles(i * 2 + 2, i * 12 + 12, 0, i * 48 + 24)
            n = FT // 2 - 2
            ffn_tiles(n, 6 * n, 1, 24 * (n - 1))
            ffn_tiles(n + 1, 6 * n + 6, 0, 24 * n, after=DOWN_AFTER_LAST)
            last = FT // 2 - 1
            down_last(last)
            for tt in range(len(FINAL_TURN), N_TOK):
                y_turn(tt, 24 * last)


_INS = ['x_prompt', 'x_sample', 'state_mlstm_C', 'state_mlstm_n', 'state_mlstm_m', 'state_pool_buf', 'g_mix', 'w_in',
        'b_gate', 'g_head', 'w_pool', 'pool_scale', 'w_out', 'g_ffn', 'w_gate', 'w_up', 'w_down', 'g_final']
_OUTS = [(1, 1024, 1024), (8, 1, 1024), (1, 1, 4, 128, 128), (1, 1, 4, 128), (1, 1, 4), (1, 1, 15, 512),
         (1, 8, 4, 128, 128), (1, 8, 4, 128), (1, 8, 4), (1, 8, 15, 512)]


def kernel(**inputs):
    import numpy as _np
    import concourse.bacc as _bacc
    from concourse import mybir as _mybir
    from concourse.bass_utils import run_bass_kernel_spmd as _run

    nc = _bacc.Bacc("TRN2", target_bir_lowering=False, num_devices=1)
    arrays, args = {}, []
    for name in _INS:
        a = _np.ascontiguousarray(inputs[name])
        arrays[f"in_{name}"] = a
        args.append(nc.dram_tensor(f"in_{name}", a.shape, _mybir.dt.from_np(a.dtype), kind="ExternalInput").ap())
    for i, shape in enumerate(_OUTS):
        args.append(nc.dram_tensor(f"out_{i}", shape, _mybir.dt.float32, kind="ExternalOutput").ap())
    trunk_kernel(nc, *args)
    r = _run(nc, [arrays], core_ids=[0])
    return tuple(r.results[0][f"out_{i}"] for i in range(len(_OUTS)))
```
